# Optimizing a Trainium2 kernel written in Bass

```python
import math
import jax, jax.numpy as jnp
from jax import lax
import numpy as np

D_MODEL = 1024
BATCH = 1
SEQ = 512
DEPTH = 4
DEC_BATCH = 8
DEC_SEQ = 1
PAST_LEN = 256
PAGE_SIZE = 128

N_MIXERS = 3
POOL_WINDOWS = (2, 4, 8, 16)
N_POOL_GROUPS = len(POOL_WINDOWS)
POOL_GROUP = D_MODEL // N_POOL_GROUPS
POOL_HIST = max(POOL_WINDOWS) - 1
CONV_WIDTH = 31
CONV_HIST = CONV_WIDTH - 1
N_HEADS = 8
HEAD_DIM = D_MODEL // N_HEADS
QK_DIM = HEAD_DIM // 2
D_FF = -(-8 * D_MODEL // (3 * 256)) * 256
QBLOCK = 128
NORM_EPS = 1e-6
MASK_VALUE = -1e30
N_POOL_LAYERS = len(range(0, DEPTH, N_MIXERS))
N_CONV_LAYERS = len(range(1, DEPTH, N_MIXERS))
N_ATTN_LAYERS = len(range(2, DEPTH, N_MIXERS))

kernel_name = "pool_conv_diffattn_hybrid_step"

def rmsnorm(x, g):
    xf = x.astype(jnp.float32)
    y = xf * lax.rsqrt(jnp.mean(xf * xf, axis=-1, keepdims=True) + NORM_EPS)
    return (y * g.astype(jnp.float32)).astype(x.dtype)

def layernorm(x, g, b):
    xf = x.astype(jnp.float32)
    mu = jnp.mean(xf, axis=-1, keepdims=True)
    xc = xf - mu
    y = xc * lax.rsqrt(jnp.mean(xc * xc, axis=-1, keepdims=True) + NORM_EPS)
    return (y * g.astype(jnp.float32) + b.astype(jnp.float32)).astype(x.dtype)

def alibi_slopes():
    return jnp.exp2(-8.0 * jnp.arange(1, N_HEADS + 1, dtype=jnp.float32) / N_HEADS)

def pool_mix(u, n_hist, w, scale):
    B, L, D = u.shape
    T = L - n_hist
    uf = u.astype(jnp.float32)
    cs = jnp.concatenate([jnp.zeros((B, 1, D), jnp.float32), jnp.cumsum(uf, axis=1)], axis=1)
    hi = np.arange(n_hist + 1, L + 1)
    diffs = []
    for g, win in enumerate(POOL_WINDOWS):
        lo = np.maximum(hi - win, 0)
        cnt = (hi - lo).astype(np.float32)
        sl = slice(g * POOL_GROUP, (g + 1) * POOL_GROUP)
        mean = (cs[:, hi, sl] - cs[:, lo, sl]) / cnt[None, :, None]
        diffs.append(mean - uf[:, n_hist:, sl])
    d = jnp.stack(diffs, axis=2)
    y = jnp.einsum('btgc,gcd->btgd', d, w.astype(jnp.float32)).reshape(B, T, D)
    return (y * scale.astype(jnp.float32)).astype(u.dtype)

def conv_module(h, hist, w_in, b_in, dw, dw_b, ln_g, ln_b, w_out, b_out):
    a = h @ w_in + b_in
    glu = a[..., :D_MODEL] * jax.nn.sigmoid(a[..., D_MODEL:])
    full = jnp.concatenate([hist, glu], axis=1)
    c = lax.conv_general_dilated(full, dw[:, None, :], window_strides=(1,), padding='VALID',
                                 dimension_numbers=('NWC', 'WIO', 'NWC'),
                                 feature_group_count=D_MODEL) + dw_b
    c = jax.nn.silu(layernorm(c, ln_g, ln_b))
    y = c @ w_out + b_out
    return y, full[:, -CONV_HIST:]

def swiglu(h, w_gate, w_up, w_down):
    return (jax.nn.silu(h @ w_gate) * (h @ w_up)) @ w_down

def diff_project(h, w_qkv, q_norm, k_norm):
    B, T, _ = h.shape
    q, k, v = jnp.split(h @ w_qkv, 3, axis=-1)
    q = rmsnorm(q.reshape(B, T, N_HEADS, 2, QK_DIM), q_norm)
    k = rmsnorm(k.reshape(B, T, N_HEADS, 2, QK_DIM), k_norm)
    v = v.reshape(B, T, N_HEADS, HEAD_DIM)
    return q, k, v

def diff_core(q, k, v, q_pos, k_pos, lam):
    s = jnp.einsum('bqhcd,bkhcd->bhcqk', q, k).astype(jnp.float32) * (QK_DIM ** -0.5)
    dist = (q_pos[:, None] - k_pos[None, :]).astype(jnp.float32)
    s = s - alibi_slopes()[None, :, None, None, None] * dist
    s = jnp.where(dist >= 0, s, MASK_VALUE)
    p = jax.nn.softmax(s, axis=-1)
    a = p[:, :, 0] - lam * p[:, :, 1]
    return jnp.einsum('bhqk,bkhd->bqhd', a.astype(v.dtype), v)

def diff_output(o, subln, w_o, lambda_init):
    B, T = o.shape[:2]
    o = rmsnorm(o, subln) * (1.0 - lambda_init)
    return o.reshape(B, T, D_MODEL) @ w_o

def setup_inputs(seed: int = 0) -> dict:
    key = jax.random.key(seed)
    ks = iter(jax.random.split(key, 40))
    f32 = jnp.float32

    def nrm(shape, scale):
        return jax.random.normal(next(ks), shape, f32) * scale

    n_pages = PAST_LEN // PAGE_SIZE
    n_used = DEC_BATCH * n_pages
    n_phys = n_used + n_used // 4
    perm = jax.random.permutation(next(ks), n_phys)
    page_table = perm[:n_used].reshape(DEC_BATCH, n_pages).astype(jnp.int32)
    return {
        "x_prompt": nrm((BATCH, SEQ, D_MODEL), 1.0),
        "x_sample": nrm((DEC_BATCH, DEC_SEQ, D_MODEL), 1.0),
        "state_pool": nrm((N_POOL_LAYERS, DEC_BATCH, POOL_HIST, D_MODEL), 1.0),
        "state_conv": nrm((N_CONV_LAYERS, DEC_BATCH, CONV_HIST, D_MODEL), 0.5),
        "cache_k": nrm((N_ATTN_LAYERS, n_phys, PAGE_SIZE, N_HEADS, 2, QK_DIM), 1.0),
        "cache_v": nrm((N_ATTN_LAYERS, n_phys, PAGE_SIZE, N_HEADS, HEAD_DIM), 1.0),
        "page_table": page_table,
        "norm_mix": 1.0 + nrm((DEPTH, D_MODEL), 0.05),
        "norm_ffn": 1.0 + nrm((DEPTH, D_MODEL), 0.05),
        "pool_w": nrm((N_POOL_LAYERS, N_POOL_GROUPS, POOL_GROUP, POOL_GROUP), POOL_GROUP ** -0.5),
        "pool_scale": 1.0 + nrm((N_POOL_LAYERS, D_MODEL), 0.1),
        "conv_w_in": nrm((N_CONV_LAYERS, D_MODEL, 2 * D_MODEL), D_MODEL ** -0.5),
        "conv_b_in": nrm((N_CONV_LAYERS, 2 * D_MODEL), 0.01),
        "conv_dw": nrm((N_CONV_LAYERS, CONV_WIDTH, D_MODEL), CONV_WIDTH ** -0.5),
        "conv_dw_b": nrm((N_CONV_LAYERS, D_MODEL), 0.01),
        "conv_ln_g": 1.0 + nrm((N_CONV_LAYERS, D_MODEL), 0.05),
        "conv_ln_b": nrm((N_CONV_LAYERS, D_MODEL), 0.01),
        "conv_w_out": nrm((N_CONV_LAYERS, D_MODEL, D_MODEL), D_MODEL ** -0.5),
        "conv_b_out": nrm((N_CONV_LAYERS, D_MODEL), 0.01),
        "attn_w_qkv": nrm((N_ATTN_LAYERS, D_MODEL, 3 * D_MODEL), D_MODEL ** -0.5),
        "attn_q_norm": 1.0 + nrm((N_ATTN_LAYERS, QK_DIM), 0.05),
        "attn_k_norm": 1.0 + nrm((N_ATTN_LAYERS, QK_DIM), 0.05),
        "attn_lq1": nrm((N_ATTN_LAYERS, QK_DIM), 0.1),
        "attn_lk1": nrm((N_ATTN_LAYERS, QK_DIM), 0.1),
        "attn_lq2": nrm((N_ATTN_LAYERS, QK_DIM), 0.1),
        "attn_lk2": nrm((N_ATTN_LAYERS, QK_DIM), 0.1),
        "attn_subln": 1.0 + nrm((N_ATTN_LAYERS, HEAD_DIM), 0.05),
        "attn_w_o": nrm((N_ATTN_LAYERS, D_MODEL, D_MODEL), D_MODEL ** -0.5),
        "ffn_w_gate": nrm((DEPTH, D_MODEL, D_FF), D_MODEL ** -0.5),
        "ffn_w_up": nrm((DEPTH, D_MODEL, D_FF), D_MODEL ** -0.5),
        "ffn_w_down": nrm((DEPTH, D_FF, D_MODEL), D_FF ** -0.5),
    }

def reference(x_prompt, x_sample, state_pool, state_conv, cache_k, cache_v, page_table,
              norm_mix, norm_ffn, pool_w, pool_scale,
              conv_w_in, conv_b_in, conv_dw, conv_dw_b, conv_ln_g, conv_ln_b, conv_w_out, conv_b_out,
              attn_w_qkv, attn_q_norm, attn_k_norm, attn_lq1, attn_lk1, attn_lq2, attn_lk2,
              attn_subln, attn_w_o, ffn_w_gate, ffn_w_up, ffn_w_down):
    xp, xs = x_prompt, x_sample
    Bp, Tp, _ = xp.shape
    Bs, Ts, _ = xs.shape
    past = page_table.shape[1] * PAGE_SIZE
    pool_p, pool_s, conv_p, conv_s = [], [], [], []
    kp_rows, vp_rows, ks_rows, vs_rows = [], [], [], []
    ia = ib = ic = 0
    for i in range(DEPTH):
        kind = i % N_MIXERS
        hp = rmsnorm(xp, norm_mix[i])
        hs = rmsnorm(xs, norm_mix[i])
        if kind == 0:
            yp = pool_mix(hp, 0, pool_w[ia], pool_scale[ia])
            full_s = jnp.concatenate([state_pool[ia], hs], axis=1)
            ys = pool_mix(full_s, POOL_HIST, pool_w[ia], pool_scale[ia])
            pool_p.append(hp[:, -POOL_HIST:])
            pool_s.append(full_s[:, -POOL_HIST:])
            ia += 1
        elif kind == 1:
            cargs = (conv_w_in[ib], conv_b_in[ib], conv_dw[ib], conv_dw_b[ib],
                     conv_ln_g[ib], conv_ln_b[ib], conv_w_out[ib], conv_b_out[ib])
            yp, hist_p = conv_module(hp, jnp.zeros((Bp, CONV_HIST, D_MODEL), hp.dtype), *cargs)
            ys, hist_s = conv_module(hs, state_conv[ib], *cargs)
            conv_p.append(hist_p)
            conv_s.append(hist_s)
            ib += 1
        else:
            lambda_init = 0.8 - 0.6 * math.exp(-0.3 * i)
            lam = (jnp.exp(jnp.sum(attn_lq1[ic].astype(jnp.float32) * attn_lk1[ic].astype(jnp.float32)))
                   - jnp.exp(jnp.sum(attn_lq2[ic].astype(jnp.float32) * attn_lk2[ic].astype(jnp.float32)))
                   + lambda_init)
            q, k, v = diff_project(hp, attn_w_qkv[ic], attn_q_norm[ic], attn_k_norm[ic])
            nb = Tp // QBLOCK
            qb = q.reshape(Bp, nb, QBLOCK, N_HEADS, 2, QK_DIM).transpose(1, 0, 2, 3, 4, 5)
            posb = jnp.arange(Tp).reshape(nb, QBLOCK)
            kpos = jnp.arange(Tp)
            ob = lax.map(lambda a: diff_core(a[0], k, v, a[1], kpos, lam), (qb, posb))
            o = ob.transpose(1, 0, 2, 3, 4).reshape(Bp, Tp, N_HEADS, HEAD_DIM)
            yp = diff_output(o, attn_subln[ic], attn_w_o[ic], lambda_init)
            kp_rows.append(k)
            vp_rows.append(v)
            qn, kn, vn = diff_project(hs, attn_w_qkv[ic], attn_q_norm[ic], attn_k_norm[ic])
            k_past = cache_k[ic][page_table].reshape(Bs, past, N_HEADS, 2, QK_DIM)
            v_past = cache_v[ic][page_table].reshape(Bs, past, N_HEADS, HEAD_DIM)
            k_all = jnp.concatenate([k_past, kn.astype(k_past.dtype)], axis=1)
            v_all = jnp.concatenate([v_past, vn.astype(v_past.dtype)], axis=1)
            os_ = diff_core(qn, k_all, v_all, past + jnp.arange(Ts), jnp.arange(past + Ts), lam)
            ys = diff_output(os_, attn_subln[ic], attn_w_o[ic], lambda_init)
            ks_rows.append(kn)
            vs_rows.append(vn)
            ic += 1
        xp = xp + yp
        xs = xs + ys
        xp = xp + swiglu(rmsnorm(xp, norm_ffn[i]), ffn_w_gate[i], ffn_w_up[i], ffn_w_down[i])
        xs = xs + swiglu(rmsnorm(xs, norm_ffn[i]), ffn_w_gate[i], ffn_w_up[i], ffn_w_down[i])
    return (xp, xs, jnp.stack(pool_p), jnp.stack(pool_s), jnp.stack(conv_p), jnp.stack(conv_s),
            jnp.stack(kp_rows), jnp.stack(vp_rows), jnp.stack(ks_rows), jnp.stack(vs_rows))


_drawn_inputs = setup_inputs


def setup_inputs(seed=0):
    import zlib

    import numpy as np

    out = dict(_drawn_inputs(seed))
    spreads = {}
    factors = {'conv_b_in': 5.381,
     'conv_dw_b': 5.619,
     'conv_ln_b': 8.0,
     'conv_b_out': 6.76,
     'attn_q_norm': 3.366,
     'attn_lq1': 4.852,
     'attn_lk1': 200.0,
     'attn_lq2': 61.032,
     'attn_lk2': 64.0,
     'attn_subln': 3.813}
    for name, (base, spread) in spreads.items():
        noise = np.random.default_rng([zlib.crc32(name.encode()), seed]).standard_normal(out[name].shape)
        drawn = base * np.exp(spread * noise) if base else spread * noise
        out[name] = __import__('jax').numpy.asarray(drawn.astype(out[name].dtype))
    for name, factor in factors.items():
        out[name] = (out[name] * factor).astype(out[name].dtype)
    return out
```

```python
import math
from contextlib import ExitStack

import numpy as np

import concourse.bass as bass
from concourse import mybir

F32 = mybir.dt.float32
F32R = mybir.dt.float32r
I32 = mybir.dt.int32
ALU = mybir.AluOpType
ACT = mybir.ActivationFunctionType
AX = mybir.AxisListType

P = 128
D = 1024
KT = D // P
SEQ, DEC = 512, 8
T = SEQ + DEC
HALF = T // 2
FF = 2816
FT = FF // P
HEADS, QK = 8, 64
PAST, PAGE = 256, 128
WINDOWS = (2, 4, 8, 16)
HIST_P, HIST_C, TAPS = 15, 30, 31
EPS = 1e-6
LAMBDA_INIT = 0.8 - 0.6 * math.exp(-0.3 * 2)
SCALE = QK ** -0.5
TAIL_P = HIST_P + DEC
TAIL_C = HIST_C + DEC

ORDER = [("pool0", 2, 8), ("ffn0", 2 * FT + 24, 2 * FT + 8), ("conv_in", 16, 16), ("conv_out", 8, 8),
         ("ffn1", 2 * FT + 24, 2 * FT + 8), ("qkv", 24, 24), ("w_o", 8, 8),
         ("ffn2", 2 * FT + 24, 2 * FT + 8), ("pool1", 2, 8), ("ffn3", 2 * FT + 24, 2 * FT + 8)]
UNIT, TILE = {}, {}
_u = _m = 0
for _name, _units, _tiles in ORDER:
    UNIT[_name], TILE[_name] = _u, _m
    _u, _m = _u + _units, _m + _tiles
UNITS = _u

V_MIX, V_FFN, V_PSCALE, V_BIN, V_DWB, V_LNG, V_LNB, V_BOUT, V_DW, V_QN, V_KN, V_SUB = (
    0, 32, 64, 80, 96, 104, 112, 120, 128, 376, 377, 378)
C_ID, C_BLK, C_DIST, C_POS, C_CNT = 0, 128, 256, 768, 1024
N_CONST = C_CNT + 64


class At:

    def __init__(self, start, step=0, i=None):
        self.start, self.step, self.i = start, step, i

    def __add__(self, k):
        return At(self.start + k, self.step, self.i)

    @property
    def v(self):
        return self.start if self.i is None else self.i * self.step + self.start

    def slot(self, depth):
        assert self.step % depth == 0
        return self.start % depth

    def turn(self, depth):
        assert self.step % depth == 0
        return At(self.start // depth, self.step // depth, self.i)


def at(start, step, i):
    return At(start + step * i) if isinstance(i, int) else At(start, step, i)


def tile_of(t, m):
    if m.i is None:
        return t[:, m.start, :]
    return t[:, bass.ds(m.v, 1), :].rearrange("p o c -> p (o c)")


XIN = {1: 0, 2: 1, 3: 2, 4: 3, 5: 4, 7: 5}
PIECES = (((0, 0), (P, 1)), ((0, 2),), ((0, 3),))
MIX = {"pool0": 0, "conv": 4, "attn": 12, "pool1": 21}
N_CONST_LOADS = 1 + 10 + 5
STORED = {"pool0": 2, "conv": 4, "attn": 4 + 2 * HEADS, "pool1": 6 + 2 * HEADS, "end": 6 + 2 * HEADS + 2 * KT}


def constants():
    c = np.zeros((P, N_CONST), np.float32)
    c[:, C_ID:C_ID + P] = np.eye(P)
    c[0:QK, C_BLK:C_BLK + QK] = 1.0 / QK
    c[QK:P, C_BLK + QK:C_BLK + P] = 1.0 / QK
    dist = np.arange(SEQ)[None, :] - (SEQ - P) - np.arange(P)[:, None]
    c[:, C_DIST:C_DIST + SEQ] = np.where(dist <= 0, dist, -1e33)
    slope = 2.0 ** -(np.arange(HEADS * DEC) // DEC + 1.0)
    c[0:HEADS * DEC, C_POS:C_POS + PAST] = slope[:, None] * (np.arange(PAST) - PAST)[None, :] / SCALE
    for g, win in enumerate(WINDOWS):
        c[:, C_CNT + 16 * g:C_CNT + 16 * g + 16] = 1.0 / np.minimum(np.arange(16) + 1, win)
    return c


def trunk_step(nc, x_prompt, x_sample, state_pool, state_conv, cache_k, cache_v, page_table,
               norm_mix, norm_ffn, pool_w, pool_scale, conv_w_in, conv_b_in, conv_dw, conv_dw_b,
               conv_ln_g, conv_ln_b, conv_w_out, conv_b_out, attn_w_qkv, attn_q_norm, attn_k_norm,
               attn_lq1, attn_lk1, attn_lq2, attn_lk2, attn_subln, attn_w_o,
               ffn_w_gate, ffn_w_up, ffn_w_down, shape_constants,
               y_prompt, y_sample, pool_state_p, pool_state_s, conv_state_p, conv_state_s,
               k_rows_p, v_rows_p, k_rows_s, v_rows_s):
    ctx = ExitStack()
    with ctx:
        place = [16512]

        def fixed(name, shape, dt=F32):
            t = nc.alloc_sbuf_tensor_at(name, shape, dt, offset=place[0])
            place[0] += (4 * int(np.prod(shape[1:])) + 31) // 32 * 32
            return t

        def overlay(start):
            at = [start]

            def take(name, shape, dt=F32):
                t = nc.alloc_sbuf_tensor_at(name, shape, dt, offset=at[0])
                at[0] += (4 * int(np.prod(shape[1:])) + 31) // 32 * 32
                take.end = at[0]
                return t
            return take

        x = fixed("x", [P, KT, T])
        xin_at = place[0]
        xin_hi = fixed("xin_hi", [P, KT, T], F32R)
        xin_lo = fixed("xin_lo", [P, KT, T], F32R)
        rstd = fixed("rstd", [P, T])
        lnb = fixed("lnb", [P, T])
        sqacc = fixed("sqacc", [P, T])
        sq = fixed("sq", [P, 2, T])
        raw = fixed("raw", [P, 4, 1024])
        w_hi = [fixed(f"w_hi{s}", [P, 1024], F32R) for s in range(2)]
        w_lo = [fixed(f"w_lo{s}", [P, 1024], F32R) for s in range(2)]
        const = fixed("const", [P, N_CONST])
        vec = fixed("vec", [P, 379])
        avg = fixed("avg", [P, P])
        eps = fixed("eps", [P, 1])
        neg_lam = fixed("neg_lam", [P, 1])
        sub_gain = fixed("sub_gain", [P, 1])
        stage = fixed("stage", [TAIL_C, D])
        qs, ks, vs = (fixed(n, [P, HEADS, DEC]) for n in ("qs", "ks", "vs"))
        temps_at = place[0]
        take = overlay(temps_at)
        g_buf = take("g_buf", [P, 2, T])
        sg_buf = take("sg_buf", [P, 2, T])
        u_buf = take("u_buf", [P, T])
        h_buf = take("h_buf", [P, 2, T])
        arena_at = take.end
        take = overlay(arena_at)
        h_hi = take("h_hi", [P, FT, T], F32R)
        h_lo = take("h_lo", [P, FT, T], F32R)
        arena_end = take.end
        assert arena_end <= nc.sbuf_usable_end
        ident = const[:, C_ID:C_ID + P]
        blk = const[:, C_BLK:C_BLK + P]

        take = overlay(arena_at)
        x_rows = take("x_rows", [P, 4, D])
        xs_rows = take("xs_rows", [DEC, D])
        vec_rows = take("vec_rows", [P, 3, P])
        lam_rows = take("lam_rows", [P, 4, QK])
        lam_tmp = take("lam_tmp", [P, QK + 4])
        take = overlay(arena_at)
        mix_hi = take("mix_hi", [P, KT, T], F32R)
        mix_lo = take("mix_lo", [P, KT, T], F32R)
        mixer_at = take.end
        take = overlay(mixer_at)
        hn = take("hn", [P, KT, 16 + T])
        hist_rows = take("hist_rows", [DEC * HIST_P, D])
        hist_s = take("hist_s", [P, KT, DEC, 16])
        wsum = take("wsum", [P, 2, 2, 16 + SEQ])
        diff = take("diff", [P, 2, 2, T])
        edge = take("edge", [P, 2, 16])
        last_s = take("last_s", [P, 2, DEC])
        assert take.end <= arena_end
        take = overlay(mixer_at)
        glu = take("glu", [P, KT, HIST_C + T])
        conv = take("conv", [P, KT, T])
        hist_c = take("hist_c", [P, KT, DEC, TAPS])
        chist_rows = take("chist_rows", [4 * HIST_C, 2, D])
        assert take.end <= arena_end
        x_out = nc.alloc_sbuf_tensor_at("x_out", [P, 4, T], F32, offset=temps_at)
        prod_s = nc.alloc_sbuf_tensor_at("prod_s", [P, DEC, TAPS], F32, offset=temps_at + 5 * 4 * T)
        act_in = g_buf
        gate_s = sg_buf
        take = overlay(temps_at)
        q_raw, k_raw, v_raw, qn, kn, ln_q, ln_k = (
            take(n, [P, T]) for n in ("q_raw", "k_raw", "v_raw", "qn", "kn", "ln_q", "ln_k"))
        assert take.end <= arena_at
        take = overlay(mixer_at)
        o_tok = take("o_tok", [P, 4, HEADS, P])
        k_page0 = take("k_page0", [P, 2, D])
        v_page0 = take("v_page0", [P, 2, D])
        head_at = take.end
        s_buf = take("s_buf", [P, 2, SEQ])
        a_buf = take("a_buf", [P, SEQ])
        t_buf = take("t_buf", [P, SEQ])
        aT = take("aT", [P, SEQ])
        v_tok = take("v_tok", [P, 2, 4, P])
        k_tok = take("k_tok", [P, 2, 4, P])
        bias_h = take("bias_h", [P, 2, SEQ])
        o_sq = take("o_sq", [P, SEQ])
        small_at = take.end
        row_max = take("row_max", [P, 2, 2])
        row_sum = take("row_sum", [P, 2, 2])
        row_scl = take("row_scl", [P, 2, 2])
        row_inv = take("row_inv", [P, 2, 2])
        o_max = take("o_max", [P, 4, HEADS])
        o_inv = take("o_inv", [P, 4, HEADS])
        o_ss = take("o_ss", [P, 4, HEADS])
        o_tmp = take("o_tmp", [P, 3, 4 * HEADS])
        assert take.end <= arena_end, take.end - arena_end
        take = overlay(head_at)
        k_page1 = take("k_page1", [P, 2, D])
        v_page1 = take("v_page1", [P, 2, D])
        assert take.end <= small_at
        ks_rows_sb = take("ks_rows_sb", [HEADS * DEC, P])
        vs_rows_sb = take("vs_rows_sb", [HEADS * DEC, P])
        os_tok = take("os_tok", [HEADS * DEC, P])
        os_sq = take("os_sq", [HEADS * DEC, P])
        assert take.end <= small_at, take.end - small_at
        k_page, v_page = [k_page0, k_page1], [v_page0, v_page1]
        R = HEADS * DEC
        take = overlay(temps_at)
        kT = take("kT", [P, 2, D])
        q_diag = take("q_diag", [P, R, 2])
        s_cols = take("s_cols", [P, 2, R, 2])
        s_dec = take("s_dec", [R, 2, PAST + 1])
        assert take.end <= temps_at + 7 * 4 * T
        a_dec = nc.alloc_sbuf_tensor_at("a_dec", [R, PAST + 1], F32, offset=xin_at)
        t_dec = nc.alloc_sbuf_tensor_at("t_dec", [R, PAST + 1], F32, offset=xin_at + 1056)
        aT_dec = nc.alloc_sbuf_tensor_at("aT_dec", [P, 2, R], F32, offset=xin_at + 2112)
        os_col = nc.alloc_sbuf_tensor_at("os_col", [P, R], F32, offset=xin_at + 2624)
        m_dec = nc.alloc_sbuf_tensor_at("m_dec", [R, 16], F32, offset=xin_at + 2880)
        new_dec = nc.alloc_sbuf_tensor_at("new_dec", [P, R], F32, offset=xin_at + 2944)
        y_sb = nc.alloc_sbuf_tensor_at("y_sb", [P, KT, SEQ + P], F32, offset=xin_at)

        acc = nc.alloc_psum_tensor("acc", [P, 4, 512], F32)
        pair = nc.alloc_psum_tensor("pair", [P, 2, 512], F32)
        bank6 = nc.alloc_psum_tensor("bank6", [P, 512], F32)
        bank7 = nc.alloc_psum_tensor("bank7", [P, 512], F32)
        bank = [bank6, bank7]

        def sem(name):
            return ctx.enter_context(nc.semaphore(name))

        landed = [sem(f"landed{s}") for s in range(4)]
        split_hi, split_lo = sem("split_hi"), sem("split_lo")
        units_done = sem("units_done")
        tile_done = sem("tile_done")
        evacuated = sem("evacuated")
        sq_ready, sq_added = sem("sq_ready"), sem("sq_added")
        mean_ready, rstd_ready = sem("mean_ready"), sem("rstd_ready")
        xin_hi_ok, xin_lo_ok = sem("xin_hi_ok"), sem("xin_lo_ok")
        tp_full, tp_taken = sem("tp_full"), sem("tp_taken")
        sg_ready, h_ready, h_hi_ok, h_lo_ok = sem("sg_ready"), sem("h_ready"), sem("h_hi_ok"), sem("h_lo_ok")
        const_in, rows_in, lam_in, hist_in = sem("const_in"), sem("rows_in"), sem("lam_in"), sem("hist_in")
        ready0 = sem("ready0")
        stored, moved = sem("stored"), sem("moved")
        act_seq, dve_seq, pool_seq = sem("act_seq"), sem("dve_seq"), sem("pool_seq")
        hn_ready, diff_ready, mix_hi_ok, mix_lo_ok = sem("hn_ready"), sem("diff_ready"), sem("mix_hi_ok"), sem("mix_lo_ok")
        glu_ready, gate_ready, conv_ready = sem("glu_ready"), sem("gate_ready"), sem("conv_ready")
        cmean, cent, csq, cvar, crstd, cnorm, cact = (
            sem(n) for n in ("cmean", "cent", "csq", "cvar", "crstd", "cnorm", "cact"))
        nsq_ready, nrm_ready, nrm_ln, nrm_exp = sem("nsq_ready"), sem("nrm_ready"), sem("nrm_ln"), sem("nrm_exp")
        qkn_ready, t_ready, t_taken = sem("qkn_ready"), sem("t_ready"), sem("t_taken")
        qk_ready, s_taken, max_ready, exp_done, a_ready, at_ready, at_taken, pv_done = (
            sem(n) for n in ("qk_ready", "s_taken", "max_ready", "exp_done", "a_ready", "at_ready", "at_taken", "pv_done"))
        bias_ready, o_taken, osq_done, oss_done, saved_s = (
            sem(n) for n in ("bias_ready", "o_taken", "osq_done", "oss_done", "saved_s"))
        rows_stored = [sem(f"rows_stored{s}") for s in range(2)]
        kpage_in = [sem(f"kpage_in{s}") for s in range(2)]
        vpage_in = [sem(f"vpage_in{s}") for s in range(2)]
        qdiag_ready, kT_full, kT_a, kT_d, page_used, vpage_used = (
            sem(n) for n in ("qdiag_ready", "kT_full", "kT_a", "kT_d", "page_used", "vpage_used"))
        s_cols_ok, new_prod_ok, s_rows_full, dec_max_ok, dec_exp_ok, a_dec_ok, a_dec_full, aT_dec_ok = (
            sem(n) for n in ("s_cols_ok", "new_prod_ok", "s_rows_full", "dec_max_ok", "dec_exp_ok", "a_dec_ok",
                             "a_dec_full", "aT_dec_ok"))
        rows_s_full, rows_s_taken, os_col_ok, os_full, os_in_ok, os_sq_ok, os_scaled, os_back = (
            sem(n) for n in ("rows_s_full", "rows_s_taken", "os_col_ok", "os_full", "os_in_ok", "os_sq_ok",
                             "os_scaled", "os_back"))
        roots_in, roots_ok, o_scaled, o_back, lam_sums, lam_exps = (
            sem(n) for n in ("roots_in", "roots_ok", "o_scaled", "o_back", "lam_sums", "lam_exps"))

        block = ctx.enter_context(nc.Block())

        def accum(m):
            b = 2 * m.slot(2)
            return acc[:, b:b + 2, 0:HALF]

        def halves(t):
            return t.rearrange("p (h c) -> p h c", h=2)

        TP = {"start": 0, "pool0": 12, "conv": 16, "pool1": 22, "end": 26}

        @block.sync
        def _(sp):
            def load(n, src, cols=1024):
                if n.i is not None or n.start >= 4:
                    sp.wait_ge(split_lo, (n + -3).v)
                sp.dma_start(raw[:, n.slot(4), 0:cols].rearrange("p (k c) -> p k c", c=src.shape[-1]), src)\
                  .then_inc(landed[n.slot(4)], 16)

            def tiles(w, k0, k1, col):
                return w[k0 * P:k1 * P, col].rearrange("(k p) c -> p k c", p=P)

            def load_pool(q):
                for u in range(2):
                    load(At(UNIT[f"pool{q}"] + u), pool_w[q, 2 * u:2 * u + 2].rearrange("g (k p) c -> p (g k) c", p=P))

            def load_ffn(layer):
                base = UNIT[f"ffn{layer}"]

                def two_tiles(i):
                    for j in range(4):
                        w = (ffn_w_gate, ffn_w_up)[j % 2][layer]
                        load(at(base + j, 4, i), tiles(w, 0, KT, bass.ds(i * (2 * P) + (j // 2) * P, P)))
                two_tiles(0)
                with sp.Fori(1, FT // 2) as i:
                    two_tiles(i)
                with sp.Fori(0, 2) as i:
                    for c in range(4):
                        for j, (k0, k1) in enumerate(((0, 8), (8, 16), (16, FT))):
                            load(At(base + 2 * FT + 3 * c + j, 12, i),
                                 tiles(ffn_w_down[layer], k0, k1, bass.ds(i * (4 * P) + c * P, P)), (k1 - k0) * P)

            sp.dma_start(const[:], shape_constants).then_inc(const_in, 16)
            row = [0]

            def rows(src):
                n = src.shape[0]
                r = row[0]
                while n:
                    t, p0 = divmod(r, P)
                    k = min(n, P - p0)
                    sp.dma_start(vec_rows[p0:p0 + k, t, :], src[src.shape[0] - n:src.shape[0] - n + k, :]).then_inc(const_in, 16)
                    r, n = r + k, n - k
                row[0] = r
            sp.dma_start(x_rows[:], x_prompt[0].rearrange("(b p) d -> p b d", p=P)).then_inc(rows_in, 16)
            sp.dma_start(xs_rows[:], x_sample[:, 0, :]).then_inc(rows_in, 16)
            for src in (norm_mix, norm_ffn, pool_scale, conv_b_in, conv_dw_b, conv_ln_g, conv_ln_b, conv_b_out,
                        conv_dw[0]):
                rows(src.rearrange("l (k p) -> (l k) p", p=P))
            for j, src in enumerate((attn_q_norm, attn_k_norm)):
                for c in range(2):
                    sp.dma_start(vec_rows[120 + j:121 + j, 2, c * QK:(c + 1) * QK], src).then_inc(const_in, 16)
            sp.dma_start(vec_rows[122:123, 2, :], attn_subln).then_inc(const_in, 16)
            for j, src in enumerate((attn_lq1, attn_lk1, attn_lq2, attn_lk2)):
                sp.dma_start(lam_rows[:, j, :], src[0].partition_broadcast(P)).then_inc(lam_in, 16)
            for q in range(2):
                sp.dma_start(pool_state_s[q, :, 0:HIST_P - 1, :], state_pool[q, :, 1:HIST_P, :]).then_inc(moved, 16)
            sp.dma_start(conv_state_s[0, :, 0:HIST_C - 1, :], state_conv[0, :, 1:HIST_C, :]).then_inc(moved, 16)

            load_pool(0)
            sp.dma_start(hist_rows[:], state_pool[0].rearrange("b j d -> (b j) d")).then_inc(hist_in, 16)
            load_ffn(0)
            for i in range(KT):
                for half in range(2):
                    load(At(UNIT["conv_in"] + 2 * i + half), tiles(conv_w_in[0], 0, KT, slice(half * D + i * P, half * D + (i + 1) * P)))
                if i == 0:
                    sp.wait_ge(units_done, UNIT["conv_in"])
                    for t in range(2):
                        sp.dma_start(chist_rows[:, t, :], state_conv[0, 4 * t:4 * t + 4].rearrange("b j d -> (b j) d")).then_inc(hist_in, 16)
            for i in range(KT):
                load(At(UNIT["conv_out"] + i), tiles(conv_w_out[0], 0, KT, slice(i * P, (i + 1) * P)))
            load_ffn(1)
            for h in range(HEADS):
                for j in range(3):
                    load(At(UNIT["qkv"] + 3 * h + j), tiles(attn_w_qkv[0], 0, KT, slice(j * D + h * P, j * D + (h + 1) * P)))
            for i in range(4):
                load(At(UNIT["w_o"] + i), tiles(attn_w_o[0], 0, KT, slice(i * P, (i + 1) * P)))
            def page(dst, cache, b, s, landed_sem, free=None):
                for j in range(2):
                    at_b = page_table[b:b + 1, j:j + 1] if isinstance(b, int) else page_table[bass.ds(b, 1), j:j + 1]
                    r = sp.value_load(at_b, min_val=0, max_val=cache.shape[1] - 1)
                    if free is not None and j == 0:
                        sp.wait_ge(*free)
                    sp.dma_start(dst[s][:, j, :], cache[0, bass.ds(r, 1)].rearrange("o p h d -> p (o h d)")).then_inc(landed_sem[s], 16)
            ck = cache_k.rearrange("l n p h c d -> l n p h (c d)")
            sp.wait_ge(pv_done, 3 * HEADS)
            sp.wait_ge(oss_done, HEADS)
            for s in range(2):
                sp.wait_ge(rows_stored[s], 16 * HEADS)
            for b in range(2):
                page(k_page, ck, b, b, kpage_in)
            for b in range(2):
                page(v_page, cache_v, b, b, vpage_in)
            with sp.Fori(0, DEC // 2 - 1) as i:
                for s in range(2):
                    page(k_page, ck, i * 2 + (s + 2), s, kpage_in, (page_used, i * 2 + (s + 1)))
            with sp.Fori(0, DEC // 2 - 1) as i:
                for s in range(2):
                    page(v_page, cache_v, i * 2 + (s + 2), s, vpage_in, (vpage_used, i * 2 + (s + 1)))
            for i in range(4, KT):
                load(At(UNIT["w_o"] + i), tiles(attn_w_o[0], 0, KT, slice(i * P, (i + 1) * P)))
            load_ffn(2)
            load_pool(1)
            sp.wait_ge(units_done, UNIT["pool1"])
            sp.dma_start(hist_rows[:], state_pool[1].rearrange("b j d -> (b j) d")).then_inc(hist_in, 16)
            load_ffn(3)
            sp.wait_ge(moved, 48)
            sp.wait_ge(stored, 16 * STORED["end"])

        @block.tensor
        def _(pe):
            def tile_products(m, w_tile, s, k_hi, k_lo, start, stop):
                b = 2 * m.slot(2)
                for t, (w, v) in enumerate(((w_hi[s], k_hi), (w_hi[s], k_lo), (w_lo[s], k_hi))):
                    for h in range(2):
                        last = pe.matmul(acc[:, b + h, 0:HALF], w[:, w_tile * P:(w_tile + 1) * P],
                                         v[:, h * HALF:(h + 1) * HALF],
                                         start=start and t == 0, stop=stop and t == 2)
                return last

            def unit(n, m, hi, lo, k0=0, k1=KT, kn_=KT, before=None):
                pe.wait_ge(split_lo, (n + 1).v)
                if k0 == 0 and (m.i is not None or m.start >= 2):
                    pe.wait_ge(evacuated, (m + -1).v)
                for k in range(k0, k1):
                    if before is not None:
                        before(k)
                    last = tile_products(m, k - k0, n.slot(2), hi[:, k, :], lo[:, k, :], k == 0, k == kn_ - 1)
                last.then_inc(units_done, 1)

            def means(r):
                pe.wait_ge(sq_added, 8 * r + 8)
                if r:
                    pe.wait_ge(rstd_ready, r)
                for h in range(2):
                    last = pe.matmul(pair[:, h, 0:HALF], avg[:], sqacc[:, h * HALF:(h + 1) * HALF], start=True, stop=True)
                last.then_inc(mean_ready, 1)

            def first_unit(n, m, r, xi):
                def before(k):
                    pe.wait_ge(xin_lo_ok, 8 * xi + k + 1)
                    if k == 5:
                        means(r)
                unit(n, m, xin_hi, xin_lo, before=before)

            def batch(b, parts, dst=None):
                if b >= 2:
                    pe.wait_ge(tp_taken, b - 1)
                to = bank[b % 2]
                for cols, src in parts:
                    rows_n, cols_n = src.shape[0], src.shape[-1]
                    last = pe.transpose(to[0:cols_n, cols:cols + rows_n], src, ident[0:rows_n, 0:rows_n])
                last.then_inc(tp_full, 1)

            def pool(q):
                u, m0, tb = UNIT[f"pool{q}"], TILE[f"pool{q}"], TP[f"pool{q}"]
                means(6 * q)
                pe.wait_ge(hist_in, 16 if q == 0 else 64)
                for b in range(2):
                    batch(tb + b, [(120 * k, hist_rows[:, (4 * b + k) * P:(4 * b + k + 1) * P]) for k in range(4)])
                pe.wait_ge(hn_ready, 8 * q + 8)
                for b in range(2):
                    tails(tb + 2 + b, hn, 16 + SEQ - HIST_P, TAIL_P, b)
                for g in range(4):
                    n = At(u + g // 2)
                    pe.wait_ge(split_lo, (n + 1).v)
                    pe.wait_ge(mix_lo_ok, MIX[f"pool{q}"] + g + 1)
                    for mt in range(2):
                        m = At(m0 + 2 * g + mt)
                        if m.start >= 2:
                            pe.wait_ge(evacuated, m.start - 1)
                        for k in range(2):
                            last = tile_products(m, ((g % 2) * 2 + k) * 2 + mt, n.slot(2),
                                                 mix_hi[:, 2 * g + k, :], mix_lo[:, 2 * g + k, :], k == 0, k == 1)
                        last.then_inc(units_done if (g % 2, mt) == (1, 1) else tile_done, 1)

            def tails(b, src, col, n, part):
                if b >= 2:
                    pe.wait_ge(tp_taken, b - 1)
                for k in range(4):
                    last = pe.transpose(bank[b % 2][0:n, k * P:(k + 1) * P], src[:, 4 * part + k, col:col + n], ident)
                last.then_inc(tp_full, 1)

            def ffn(layer):
                u, m0, r = UNIT[f"ffn{layer}"], TILE[f"ffn{layer}"], 2 * layer + 1
                first_unit(At(u), At(m0), r, XIN[r])
                for j in range(1, 4):
                    unit(At(u + j), At(m0 + j), xin_hi, xin_lo)
                with pe.Fori(1, FT // 2) as i:
                    for j in range(4):
                        unit(At(u + j, 4, i), At(m0 + j, 4, i), xin_hi, xin_lo)
                with pe.Fori(0, 2) as i:
                    for c in range(4):
                        m = At(m0 + 2 * FT + c, 4, i)
                        for j, (k0, k1) in enumerate(((0, 8), (8, 16), (16, FT))):
                            def before(k):
                                pe.wait_ge(h_lo_ok, FT * layer + k + 1)
                            unit(At(u + 2 * FT + 3 * c + j, 12, i), m, h_hi, h_lo, k0, k1, FT,
                                 before if c == 0 else None)
                        if layer == 3:
                            if c:
                                y_tile(m0, i, c - 1)
                            if c == 3:
                                y_tile(m0, i, 3)

            def y_tile(m0, i, c):
                pe.wait_ge(evacuated, i * 4 + (m0 + 2 * FT + c + 1))
                tb = TP["end"] + 2 * c
                pe.wait_ge(tp_taken, i * 8 + (tb - 1))
                for b in range(4):
                    last = pe.transpose(bank6[:, b * P:(b + 1) * P], x_out[:, c, b * P:(b + 1) * P], ident)
                last.then_inc(tp_full, 1)
                pe.wait_ge(tp_taken, i * 8 + tb)
                pe.transpose(bank7[0:DEC, 0:P], x_out[:, c, SEQ:T], ident).then_inc(tp_full, 1)

            def conv_mixer():
                u, m0 = UNIT["conv_in"], TILE["conv_in"]
                for i in range(KT):
                    for half in range(2):
                        n = 2 * i + half
                        if n == 0:
                            first_unit(At(u), At(m0), 2, XIN[2])
                        else:
                            unit(At(u + n), At(m0 + n), xin_hi, xin_lo)
                    if i == 1:
                        pe.wait_ge(hist_in, 48)
                        for b in range(4):
                            batch(TP["conv"] + b, [(240 * k + 120 * t, chist_rows[:, t, (2 * b + k) * P:(2 * b + k + 1) * P])
                                                   for k in range(2) for t in range(2)])
                pe.wait_ge(glu_ready, KT)
                for b in range(2):
                    tails(TP["conv"] + 4 + b, glu, SEQ, TAIL_C, b)
                pe.wait_ge(rstd_ready, 3)
                for k in range(KT):
                    pe.wait_ge(conv_ready, k + 1)
                    for h in range(2):
                        last = pe.matmul(pair[:, h, 0:HALF], avg[:], conv[:, k, h * HALF:(h + 1) * HALF],
                                         start=k == 0, stop=k == KT - 1)
                last.then_inc(cmean, 1)
                pe.wait_ge(cent, KT)
                for k in range(KT):
                    pe.wait_ge(csq, k + 1)
                    for h in range(2):
                        last = pe.matmul(pair[:, h, 0:HALF], avg[:], glu[:, k, h * HALF:(h + 1) * HALF],
                                         start=k == 0, stop=k == KT - 1)
                last.then_inc(cvar, 1)
                u, m0 = UNIT["conv_out"], TILE["conv_out"]
                for i in range(KT):
                    def before(k):
                        pe.wait_ge(mix_lo_ok, MIX["conv"] + k + 1)
                    unit(At(u + i), At(m0 + i), mix_hi, mix_lo, before=before if i == 0 else None)

            def attention():
                u, m0 = UNIT["qkv"], TILE["qkv"]

                def stats(i):
                    pe.wait_ge(nsq_ready, i + 1)
                    h, j = divmod(i, 2)
                    if h:
                        pe.wait_ge(s_taken, 3 * (h - 1) + j + 1)
                    else:
                        pe.wait_ge(rstd_ready, 5)
                        if j:
                            pe.wait_ge(nrm_ln, 1)
                    for t in range(2):
                        last = pe.matmul(pair[:, t, 0:HALF], blk, sq[:, 0, t * HALF:(t + 1) * HALF], start=True, stop=True)
                    last.then_inc(nrm_ready, 1)

                def turn_head(g):
                    pe.wait_ge(qkn_ready, 2 * g + 2)
                    if g:
                        pe.wait_ge(s_taken, 3 * g)
                    else:
                        pe.wait_ge(nrm_ln, 2)
                    for j, src in enumerate((kn, v_raw)):
                        for b in range(4):
                            last = pe.transpose(pair[:, j, b * P:(b + 1) * P], src[:, b * P:(b + 1) * P], ident)
                    last.then_inc(t_ready, 1)

                def scores(g, piece):
                    if piece == 0:
                        pe.wait_ge(t_taken, 2 * g + 2)
                    elif g + 1 < HEADS:
                        pe.wait_ge(nrm_ln, 2 * (g + 1) + piece)
                    pe.wait_ge(s_taken, 3 * g + piece) if g or piece else None
                    for off, i in PIECES[piece]:
                        for c in range(2):
                            w = (i + 1) * P
                            last = pe.matmul(pair[:, c, off:off + w], qn[c * QK:(c + 1) * QK, i * P:(i + 1) * P],
                                             kn[c * QK:(c + 1) * QK, 0:w], start=True, stop=True)
                    last.then_inc(qk_ready, 1)

                def turn_weights(g, piece):
                    pe.wait_ge(a_ready, 3 * g + piece + 1)
                    if g or piece:
                        pe.wait_ge(at_taken, 3 * g + piece)
                    for off, i in PIECES[piece]:
                        for j in range(i + 1):
                            last = pe.transpose(bank6[:, off + j * P:off + (j + 1) * P], a_buf[:, off + j * P:off + (j + 1) * P], ident)
                    last.then_inc(at_ready, 1)

                def mix_values(g, piece):
                    pe.wait_ge(at_taken, 3 * g + piece + 1)
                    pe.wait_ge(t_taken, 2 * g + 2)
                    if piece == 0 and g:
                        pe.wait_ge(o_taken, g)
                    for off, i in PIECES[piece]:
                        for j in range(i + 1):
                            last = pe.matmul(bank7[:, i * P:(i + 1) * P], aT[:, off + j * P:off + (j + 1) * P],
                                             v_tok[:, g % 2, j, :], start=j == 0, stop=j == i)
                    last.then_inc(pv_done, 1)

                pe.wait_ge(tp_taken, TP["conv"] + 6)
                for h in range(HEADS + 2):
                    n = 3 * h
                    if h == 0:
                        first_unit(At(u), At(m0), 4, XIN[4])
                    elif h < HEADS:
                        unit(At(u + n), At(m0 + n), xin_hi, xin_lo)
                    if h >= 2:
                        turn_weights(h - 2, 2)
                    if 1 <= h <= HEADS:
                        turn_head(h - 1)
                    if h >= 2:
                        mix_values(h - 2, 2)
                    if 1 <= h <= HEADS:
                        scores(h - 1, 0)
                    for j in (1, 2):
                        if h < HEADS:
                            unit(At(u + n + j), At(m0 + n + j), xin_hi, xin_lo)
                        if 1 <= h <= HEADS:
                            turn_weights(h - 1, j - 1)
                        if h < HEADS:
                            stats(2 * h + j - 1)
                        if 1 <= h <= HEADS:
                            mix_values(h - 1, j - 1)
                            scores(h - 1, j)

                pe.wait_ge(qdiag_ready, 1)
                pe.wait_ge(s_taken, 3 * HEADS)
                pe.wait_ge(evacuated, TILE["w_o"])
                with pe.Fori(0, DEC // 2) as i:
                    for s in range(2):
                        pe.wait_ge(kpage_in[s], i * 32 + 32)
                        for j, to in enumerate((pair, acc)):
                            for h in range(HEADS):
                                last = pe.transpose(to[:, h // 4, (h % 4) * P:(h % 4 + 1) * P],
                                                    k_page[s][:, j, h * P:(h + 1) * P], ident)
                            last.then_inc(kT_full, 1)
                        for j in range(2):
                            pe.wait_ge(kT_a, i * 4 + (2 * s + j + 1))
                            pe.wait_ge(kT_d, i * 4 + (2 * s + j + 1))
                            for h in range(HEADS):
                                last = pe.matmul(bank6[:, bass.ds(i * 4 + (j * R + h * DEC + s) * 2, 2)],
                                                 kT[:, j, h * P:(h + 1) * P],
                                                 q_diag[:, bass.ds(i * 2 + (h * DEC + s), 1), :].rearrange("p o c -> p (o c)"),
                                                 start=True, stop=True)
                        last.then_inc(page_used, 1)
                pe.wait_ge(o_taken, HEADS)
                for j, src in enumerate((ks, vs)):
                    last = pe.transpose(bank7[0:R, j * P:(j + 1) * P], src[:].rearrange("p h b -> p (h b)"), ident)
                last.then_inc(rows_s_full, 1)
                pe.wait_ge(s_cols_ok, 1)
                for c in range(2):
                    for j in range(2):
                        pe.transpose(pair[0:R, 0, (c * 2 + j) * P:(c * 2 + j + 1) * P], s_cols[:, j, :, c], ident)
                pe.wait_ge(new_prod_ok, 1)
                pe.matmul(pair[0:R, 1, 0:2], new_dec[:], blk[:, 0:P:QK], start=True, stop=True).then_inc(s_rows_full, 1)
                pe.wait_ge(a_dec_ok, 1)
                pe.wait_ge(rows_s_taken, 2)
                for j in range(2):
                    pe.transpose(bank6[:, j * R:(j + 1) * R], a_dec[:, j * PAGE:(j + 1) * PAGE], ident[0:R, 0:R])
                pe.matmul(bank7[:, 0:R], a_dec[:, PAST:PAST + 1].to_broadcast([R, P]), ident[0:R, 0:R],
                          start=True, stop=True).then_inc(a_dec_full, 1)
                pe.wait_ge(aT_dec_ok, 1)
                with pe.Fori(0, DEC // 2) as i:
                    for s in range(2):
                        pe.wait_ge(vpage_in[s], i * 32 + 32)
                        for h in range(HEADS):
                            for j in range(2):
                                last = pe.matmul(pair[:, 0, bass.ds(i * 2 + (h * DEC + s), 1)],
                                                 v_page[s][:, j, h * P:(h + 1) * P],
                                                 aT_dec[:, j, bass.ds(i * 2 + (h * DEC + s), 1)],
                                                 start=j == 0, stop=j == 1)
                        last.then_inc(vpage_used, 1)
                pe.wait_ge(os_col_ok, 1)
                pe.transpose(pair[:R, 1, 0:P], os_col[:], ident).then_inc(os_full, 1)
                pe.wait_ge(os_scaled, 1)
                pe.transpose(bank7[:, 0:R], os_tok[:], ident[0:R, 0:R]).then_inc(os_back, 1)
                for h in range(HEADS):
                    pe.wait_ge(o_scaled, h + 1)
                    if h:
                        pe.wait_ge(mix_lo_ok, MIX["attn"] + 1 + h)
                    for b in range(4):
                        last = pe.transpose(bank6[:, b * P:(b + 1) * P], o_tok[:, b, h, :], ident)
                    last.then_inc(o_back, 1)
                pe.wait_ge(mix_lo_ok, MIX["attn"] + 1 + HEADS)
                for i in range(KT):
                    unit(At(UNIT["w_o"] + i), At(TILE["w_o"] + i), mix_hi, mix_lo)

            pe.wait_ge(ready0, 2)
            pe.wait_ge(const_in, 16 * N_CONST_LOADS)
            for t, n in enumerate((P, P, 123)):
                batch(t, [(0, vec_rows[0:n, t, :])])
            pe.wait_ge(rows_in, 32)
            batch(3, [(k * DEC, xs_rows[:, k * P:(k + 1) * P]) for k in range(KT)])
            for k in range(KT):
                batch(4 + k, [(b * P, x_rows[:, b, k * P:(k + 1) * P]) for b in range(4)])
            pool(0)
            ffn(0)
            conv_mixer()
            ffn(1)
            attention()
            ffn(2)
            pool(1)
            ffn(3)

        @block.scalar
        def _(act):
            seq = [0]

            def step(ins):
                seq[0] += 1
                ins.then_inc(act_seq, 1)
                act.wait_ge(act_seq, seq[0])

            def split(n, cols=1024):
                act.wait_ge(landed[n.slot(4)], (n.turn(4).v + 1) * 16)
                if n.start >= 2:
                    act.wait_ge(units_done, (n + -1).v)
                act.activation(w_hi[n.slot(2)][:, 0:cols], raw[:, n.slot(4), 0:cols], ACT.Copy).then_inc(split_hi, 1)

            def squares(r, m, c):
                if r or m.start >= 2:
                    act.wait_ge(sq_added, m.v + (8 * r - 1))
                act.activation(sq[:, c % 2, :], tile_of(x, m), ACT.Square).then_inc(sq_ready, 1)

            def updated(r, tile0, m, c, gain):
                act.wait_ge(evacuated, (m + (tile0 + 1)).v)
                squares(r, m, c)
                if gain is not None:
                    g = vec[:, gain + m.start:gain + m.start + 1] if m.i is None else vec[:, bass.ds((m + gain).v, 1)]
                    act.activation(tile_of(xin_hi, m), tile_of(x, m), ACT.Copy, scale=g).then_inc(xin_hi_ok, 1)

            def token_scale(r):
                act.wait_ge(mean_ready, r + 1)
                step(act.activation(halves(lnb[:]), pair[:, :, 0:HALF], ACT.Ln, bias=eps[:]))
                act.activation(rstd[:], lnb[:], ACT.Exp, scale=-0.5).then_inc(rstd_ready, 1)

            def take_batch(b, dst, src):
                act.wait_ge(tp_full, b + 1)
                act.activation(dst, src, ACT.Copy).then_inc(tp_taken, 1)

            def pool(q):
                u, tb, r = UNIT[f"pool{q}"], TP[f"pool{q}"], 6 * q + 1
                token_scale(6 * q)
                for b in range(2):
                    take_batch(tb + b, hist_s[:, 4 * b:4 * b + 4, :, 0:HIST_P],
                               bank[b % 2][:, 0:480].rearrange("p (k b j) -> p k b j", k=4, b=DEC))
                if q:
                    act.wait_ge(stored, 16 * STORED["attn"])
                for b in range(2):
                    take_batch(tb + 2 + b, stage[0:TAIL_P, 512 * b:512 * b + 512], bank[b % 2][0:TAIL_P, :])
                for g in range(5):
                    if g < 4:
                        act.wait_ge(diff_ready, 4 * q + g + 1)
                        act.activation(mix_hi[:, 2 * g:2 * g + 2, :], diff[:, g % 2], ACT.Copy).then_inc(mix_hi_ok, 1)
                    for m in (2 * g - 2, 2 * g - 1) if g else ():
                        if m % 4 == 3:
                            split(At(u + 2 + m // 4))
                        updated(r, TILE[f"pool{q}"], At(m), m, V_FFN + 8 * (3 * q))

            def ffn(layer):
                u, m0, r = UNIT[f"ffn{layer}"], TILE[f"ffn{layer}"], 2 * layer + 1
                token_scale(r)
                if layer == 2:
                    act.wait_ge(stored, 16 * STORED["attn"])
                with act.Fori(0, FT // 2) as i:
                    for c in range(2):
                        n, m, f = At(u + 2 * c, 4, i), At(m0 + 2 * c, 4, i), At(c, 2, i)
                        split(n + 2)
                        act.wait_ge(evacuated, (m + 1).v)
                        act.activation(sg_buf[:, c, :], g_buf[:, c, :], ACT.Silu).then_inc(sg_ready, 1)
                        split(n + 3)
                        act.wait_ge(h_ready, (f + (FT * layer + 1)).v)
                        act.activation(tile_of(h_hi, f), h_buf[:, c, :], ACT.Copy).then_inc(h_hi_ok, 1)
                gain = {0: V_MIX + 8, 1: V_MIX + 16, 2: None, 3: None}[layer]

                def down(i):
                    for c in range(4):
                        n, m = at(u + 2 * FT + 3 * c, 12, i), at(c, 4, i)
                        split(n + 2, 768)
                        for j in (3, 4):
                            if n.i is not None or n.start + j < UNITS:
                                split(n + j)
                        if layer < 3:
                            updated(r + 1, m0 + 2 * FT, m, c, gain)
                        else:
                            for t in (c - 1, c)[c == 0:1 + (c == 3)]:
                                col = m.start - c + t
                                tb = TP["end"] + 2 * col
                                take_batch(tb, y_sb[:, col, 0:SEQ], bank6[:, :])
                                take_batch(tb + 1, y_sb[0:DEC, col, SEQ:SEQ + P], bank7[0:DEC, 0:P])
                if layer < 3:
                    with act.Fori(0, 2) as i:
                        down(i)
                else:
                    for i in range(2):
                        down(i)

            def conv_mixer():
                u, m0 = UNIT["conv_in"], TILE["conv_in"]
                token_scale(2)
                for i in range(KT):
                    n = At(u + 2 * i)
                    split(n + 2)
                    split(n + 3)
                    act.wait_ge(evacuated, m0 + 2 * i + 2)
                    if i >= 2:
                        act.wait_ge(glu_ready, i - 1)
                    act.activation(gate_s[:, i % 2, :], act_in[:, 1, :], ACT.Sigmoid,
                                   bias=vec[:, V_BIN + KT + i:V_BIN + KT + i + 1]).then_inc(gate_ready, 1)
                    if i == 1:
                        for b in range(4):
                            take_batch(TP["conv"] + b, hist_c[:, 2 * b:2 * b + 2, :, 0:HIST_C],
                                       bank[b % 2][:, 0:480].rearrange("p (k b j) -> p k b j", k=2, b=DEC))
                act.wait_ge(stored, 16 * STORED["pool0"])
                for b in range(2):
                    take_batch(TP["conv"] + 4 + b, stage[0:TAIL_C, 512 * b:512 * b + 512], bank[b % 2][0:TAIL_C, :])
                for k in range(KT):
                    act.wait_ge(cent, k + 1)
                    act.activation(glu[:, k, 0:T], conv[:, k, :], ACT.Square).then_inc(csq, 1)
                act.wait_ge(cvar, 1)
                step(act.activation(halves(lnb[:]), pair[:, :, 0:HALF], ACT.Ln, bias=eps[:]))
                act.activation(sq[:, 0, :], lnb[:], ACT.Exp, scale=-0.5).then_inc(crstd, 1)
                for k in range(KT):
                    act.wait_ge(cnorm, k + 1)
                    act.activation(conv[:, k, :], glu[:, k, 0:T], ACT.Silu, scale=vec[:, V_LNG + k:V_LNG + k + 1],
                                   bias=vec[:, V_LNB + k:V_LNB + k + 1]).then_inc(cact, 1)
                    act.wait_ge(cact, k + 1)
                    act.activation(mix_hi[:, k, :], conv[:, k, :], ACT.Copy).then_inc(mix_hi_ok, 1)
                for i in range(KT):
                    split(At(UNIT["conv_out"] + i + 2))
                    updated(3, TILE["conv_out"], At(i), i, V_FFN + 8)

            def attention():
                u, m0 = UNIT["qkv"], TILE["qkv"]
                token_scale(4)

                def norm(i, dst):
                    act.wait_ge(nrm_ready, i + 1)
                    act.activation(halves(dst[:]), pair[:, :, 0:HALF], ACT.Ln, bias=eps[:]).then_inc(nrm_ln, 1)
                    act.wait_ge(nrm_ln, i + 1)
                    act.activation(dst[:], dst[:], ACT.Exp, scale=-0.5).then_inc(nrm_exp, 1)

                def square(i, src, m):
                    act.wait_ge(evacuated, m + 1)
                    if i:
                        act.wait_ge(nrm_ready, i)
                    act.activation(sq[:, 0, :], src[:], ACT.Square).then_inc(nsq_ready, 1)

                def exps(g, piece):
                    act.wait_ge(max_ready, 3 * g + piece + 1)
                    for off, i in PIECES[piece]:
                        for c in range(2):
                            w, j = (i + 1) * P, i % 2
                            ins = act.activation(s_buf[:, c, off:off + w], s_buf[:, c, off:off + w], ACT.Exp,
                                                 bias=row_max[:, c, j:j + 1], scale=SCALE, accum_out=row_sum[:, c, j:j + 1])
                    ins.then_inc(exp_done, 1)

                def take_weights(g, piece):
                    act.wait_ge(at_ready, 3 * g + piece + 1)
                    if g or piece:
                        act.wait_ge(pv_done, 3 * g + piece)
                    w = (384, 384, 512)[piece]
                    act.activation(aT[:, 0:w], bank6[:, 0:w], ACT.Copy).then_inc(at_taken, 1)

                for h in range(HEADS + 2):
                    n = At(u + 3 * h)
                    g = h - 1
                    if h < HEADS:
                        split(n + 2)
                    if h >= 2:
                        take_weights(h - 2, 2)
                    if 1 <= h <= HEADS:
                        act.wait_ge(t_ready, g + 1)
                        if g >= 2:
                            act.wait_ge(rows_stored[g % 2], 32 * (g // 2))
                        for j, to in enumerate((k_tok, v_tok)):
                            act.activation(to[:, g % 2], pair[:, j, :].rearrange("p (b c) -> p b c", b=4), ACT.Copy).then_inc(t_taken, 1)
                    if h < HEADS:
                        square(2 * h, q_raw, m0 + 3 * h)
                    if 1 <= h <= HEADS:
                        exps(g, 0)
                    if h < HEADS:
                        split(n + 3)
                    if 1 <= h <= HEADS:
                        take_weights(g, 0)
                    if h < HEADS:
                        norm(2 * h, ln_q)
                        square(2 * h + 1, k_raw, m0 + 3 * h + 1)
                    if h >= 2:
                        act.wait_ge(o_taken, h - 1)
                        if h > 2:
                            act.wait_ge(oss_done, h - 2)
                        act.activation(o_sq[:].rearrange("p (b c) -> p b c", b=4), o_tok[:, :, h - 2, :], ACT.Square).then_inc(osq_done, 1)
                    if 1 <= h <= HEADS:
                        exps(g, 1)
                    if h < HEADS:
                        split(n + 4)
                    if 1 <= h <= HEADS:
                        take_weights(g, 1)
                    if h < HEADS:
                        norm(2 * h + 1, ln_k)
                    if 1 <= h <= HEADS:
                        exps(g, 2)

                with act.Fori(0, DEC) as b:
                    for j, src in enumerate((pair, acc)):
                        act.wait_ge(kT_full, b * 2 + (j + 1))
                        act.activation(kT[:, j, 0:512], src[:, 0, :], ACT.Copy).then_inc(kT_a, 1)
                act.wait_ge(page_used, DEC)
                act.activation(s_cols[:].rearrange("p j r c -> p (j r c)"), bank6[:, 0:4 * R], ACT.Copy).then_inc(s_cols_ok, 1)
                act.wait_ge(rows_s_full, 1)
                act.activation(ks_rows_sb[:], bank7[0:R, 0:P], ACT.Copy).then_inc(rows_s_taken, 1)
                act.activation(vs_rows_sb[:], bank7[0:R, P:2 * P], ACT.Copy).then_inc(rows_s_taken, 1)
                act.wait_ge(dec_max_ok, 1)
                for c in range(2):
                    ins = act.activation(s_dec[:, c, :], s_dec[:, c, :], ACT.Exp, bias=m_dec[:, 2 + c:3 + c], scale=SCALE,
                                         accum_out=m_dec[:, 4 + c:5 + c])
                ins.then_inc(dec_exp_ok, 1)
                act.wait_ge(a_dec_full, 1)
                act.activation(aT_dec[:].rearrange("p j r -> p (j r)"), bank6[:, 0:2 * R], ACT.Copy).then_inc(aT_dec_ok, 1)
                act.wait_ge(os_in_ok, 1)
                act.activation(os_sq[:], os_tok[:], ACT.Square, accum_out=m_dec[:, 8:9]).then_inc(os_sq_ok, 1)
                act.wait_ge(roots_in, 2)
                act.activation(m_dec[:, 9:11], m_dec[:, 9:11], ACT.Sqrt)
                act.activation(o_tmp[:, 0:2, :], o_tmp[:, 0:2, :], ACT.Sqrt).then_inc(roots_ok, 1)
                act.wait_ge(os_back, 1)
                act.activation(mix_hi[:, :, SEQ:T], bank7[:, 0:R].rearrange("p (h b) -> p h b", h=HEADS), ACT.Copy,
                               scale=sub_gain[:]).then_inc(mix_hi_ok, 1)
                for h in range(HEADS):
                    act.wait_ge(o_back, h + 1)
                    act.activation(mix_hi[:, h, 0:SEQ], bank6[:, :], ACT.Copy, scale=sub_gain[:]).then_inc(mix_hi_ok, 1)
                for i in range(KT):
                    split(At(UNIT["w_o"] + i + 2))
                    updated(5, TILE["w_o"], At(i), i, V_FFN + 16)

            split(At(0))
            split(At(1))
            for t, n in enumerate((P, P, 123)):
                take_batch(t, vec[:, t * P:t * P + n], bank[t % 2][:, 0:n])
            take_batch(3, x[:, :, SEQ:T], bank7[:, 0:KT * DEC].rearrange("p (k b) -> p k b", k=KT))
            for k in range(KT):
                take_batch(4 + k, x[:, k, 0:SEQ], bank[k % 2][:, :])
                act.wait_ge(tp_taken, 5 + k)
                squares(0, At(k), k)
            act.wait_ge(lam_sums, 2)
            act.activation(lam_tmp[:, QK:QK + 2], lam_tmp[:, QK:QK + 2], ACT.Exp).then_inc(lam_exps, 1)
            pool(0)
            ffn(0)
            conv_mixer()
            ffn(1)
            attention()
            ffn(2)
            pool(1)
            ffn(3)

        @block.vector
        def _(dve):
            seq = [0]

            def step(ins):
                seq[0] += 1
                ins.then_inc(dve_seq, 1)
                dve.wait_ge(dve_seq, seq[0])

            def split(n, cols=1024):
                dve.wait_ge(split_hi, (n + 1).v)
                if n.start >= 2:
                    dve.wait_ge(units_done, (n + -1).v)
                dve.tensor_tensor(w_lo[n.slot(2)][:, 0:cols], raw[:, n.slot(4), 0:cols],
                                  w_hi[n.slot(2)][:, 0:cols].bitcast(F32), ALU.subtract).then_inc(split_lo, 1)

            def accumulator(m):
                b = 2 * m.slot(2)
                return acc[:, b:b + 2, 0:HALF]

            def next_low(xi, m, gain):
                dve.wait_ge(xin_hi_ok, m.v + (8 * xi + 1))
                g = vec[:, gain + m.start:gain + m.start + 1] if m.i is None else vec[:, bass.ds((m + gain).v, 1)]
                dve.scalar_tensor_tensor(tile_of(xin_lo, m), tile_of(x, m), g, tile_of(xin_hi, m).bitcast(F32),
                                         ALU.mult, ALU.subtract).then_inc(xin_lo_ok, 1)

            def pool(q):
                u, m0, l = UNIT[f"pool{q}"], TILE[f"pool{q}"], 3 * q
                gain = V_MIX + 8 * l
                dve.wait_ge(rstd_ready, 6 * q + 1)
                dve.memset(hn[:, :, 0:16], 0.0)
                step(dve.memset(wsum[:, :, :, 0:16], 0.0))
                for k in range(KT):
                    dve.scalar_tensor_tensor(hn[:, k, 16:16 + T], x[:, k, :], vec[:, gain + k:gain + k + 1], rstd[:],
                                             ALU.mult, ALU.mult).then_inc(hn_ready, 1)
                dve.wait_ge(hn_ready, 8 * q + KT)

                def difference(g):
                    win = WINDOWS[g]
                    here = slice(2 * g, 2 * g + 2)
                    cur = hn[:, here, :]
                    for lev in range(g + 1):
                        to = wsum[:, lev % 2]
                        step(dve.tensor_tensor(to[:, :, 16:16 + SEQ], cur[:, :, 16:16 + SEQ],
                                               cur[:, :, 16 - (1 << lev):16 + SEQ - (1 << lev)], ALU.add))
                        cur = to
                    out = diff[:, g % 2]
                    if g >= 2:
                        dve.wait_ge(mix_lo_ok, MIX[f"pool{q}"] + g - 1)
                    step(dve.scalar_tensor_tensor(out[:, :, 0:SEQ], cur[:, :, 16:16 + SEQ], 1.0 / win,
                                                  hn[:, here, 16:16 + SEQ], ALU.mult, ALU.subtract))
                    inv = const[:, C_CNT + 16 * g:C_CNT + 16 * g + 16].unsqueeze(1).to_broadcast([P, 2, 16])
                    step(dve.tensor_tensor(edge[:], cur[:, :, 16:32], inv, ALU.mult))
                    dve.tensor_tensor(out[:, :, 0:16], edge[:], hn[:, here, 16:32], ALU.subtract)
                    dve.wait_ge(tp_taken, TP[f"pool{q}"] + 2)
                    step(dve.tensor_copy(hist_s[:, here, :, HIST_P], hn[:, here, 16 + SEQ:16 + T]))
                    step(dve.tensor_reduce(last_s[:], hist_s[:, here, :, 16 - win:16], AX.X, ALU.add))
                    dve.scalar_tensor_tensor(out[:, :, SEQ:T], last_s[:], 1.0 / win, hn[:, here, 16 + SEQ:16 + T],
                                             ALU.mult, ALU.subtract).then_inc(diff_ready, 1)

                def low(g):
                    dve.wait_ge(mix_hi_ok, MIX[f"pool{q}"] + g + 1)
                    dve.wait_ge(diff_ready, 4 * q + g + 1)
                    dve.tensor_tensor(mix_lo[:, 2 * g:2 * g + 2, :], diff[:, g % 2], mix_hi[:, 2 * g:2 * g + 2, :].bitcast(F32),
                                      ALU.subtract).then_inc(mix_lo_ok, 1)

                def update(m):
                    if m % 4 == 3:
                        dve.wait_ge(units_done, u + m // 4 + 1)
                    else:
                        dve.wait_ge(tile_done, 6 * q + 3 * (m // 4) + m % 4 + 1)
                    s = V_PSCALE + 8 * q + m
                    dve.scalar_tensor_tensor(halves(x[:, m, :]), accumulator(At(m0 + m)), vec[:, s:s + 1], halves(x[:, m, :]),
                                             ALU.mult, ALU.add).then_inc(evacuated, 1)
                    if m % 4 == 3:
                        split(At(u + 2 + m // 4))
                    next_low(XIN[6 * q + 1], At(m), V_FFN + 8 * l)

                difference(0)
                low(0)
                for g in range(1, 4):
                    difference(g)
                    low(g)
                    update(2 * g - 2)
                    update(2 * g - 1)
                update(6)
                update(7)

            def ffn(layer):
                u, m0, r = UNIT[f"ffn{layer}"], TILE[f"ffn{layer}"], 2 * layer + 1
                dve.wait_ge(rstd_ready, r + 1)
                if layer == 2:
                    dve.wait_ge(stored, 16 * STORED["attn"])
                with dve.Fori(0, FT // 2) as i:
                    for c in range(2):
                        n, m, f = At(u + 2 * c, 4, i), At(m0 + 2 * c, 4, i), At(c, 2, i)
                        dve.wait_ge(units_done, (n + 1).v)
                        dve.tensor_tensor(halves(g_buf[:, c, :]), accumulator(m), halves(rstd[:]), ALU.mult).then_inc(evacuated, 1)
                        split(n + 2)
                        dve.wait_ge(units_done, (n + 2).v)
                        dve.tensor_tensor(halves(u_buf[:]), accumulator(m + 1), halves(rstd[:]), ALU.mult).then_inc(evacuated, 1)
                        dve.wait_ge(sg_ready, (f + (FT * layer + 1)).v)
                        dve.wait_ge(evacuated, (m + 2).v)
                        dve.tensor_tensor(h_buf[:, c, :], u_buf[:], sg_buf[:, c, :], ALU.mult).then_inc(h_ready, 1)
                        split(n + 3)
                        dve.wait_ge(h_hi_ok, (f + (FT * layer + 1)).v)
                        dve.tensor_tensor(tile_of(h_lo, f), h_buf[:, c, :], tile_of(h_hi, f).bitcast(F32), ALU.subtract)\
                           .then_inc(h_lo_ok, 1)
                gain = {0: V_MIX + 8, 1: V_MIX + 16, 2: None, 3: None}[layer]

                def down(i):
                    for c in range(4):
                        n, m = at(u + 2 * FT + 3 * c, 12, i), at(c, 4, i)
                        split(n + 2, 768)
                        if n.i is not None or n.start + 3 < UNITS:
                            split(n + 3)
                        dve.wait_ge(units_done, (n + 3).v)
                        out = tile_of(x, m) if layer < 3 else x_out[:, c, :]
                        dve.tensor_tensor(halves(out), accumulator(At(c)), halves(tile_of(x, m)), ALU.add)\
                           .then_inc(evacuated, 1)
                        if n.i is not None or n.start + 4 < UNITS:
                            split(n + 4)
                        if gain is not None:
                            next_low(XIN[r + 1], m, gain)
                if layer < 3:
                    with dve.Fori(0, 2) as i:
                        down(i)
                else:
                    for i in range(2):
                        down(i)

            def conv_mixer():
                u, m0 = UNIT["conv_in"], TILE["conv_in"]
                dve.wait_ge(rstd_ready, 3)
                step(dve.memset(glu[:, :, 0:HIST_C], 0.0))

                def taps(i):
                    def tap(w):
                        return vec[:, V_DW + w * KT + i:V_DW + w * KT + i + 1]
                    out = conv[:, i, 0:SEQ]
                    step(dve.tensor_scalar(out, glu[:, i, 0:SEQ], tap(0), vec[:, V_DWB + i:V_DWB + i + 1], ALU.mult, ALU.add))
                    for w in range(1, TAPS):
                        step(dve.scalar_tensor_tensor(out, glu[:, i, w:w + SEQ], tap(w), out, ALU.mult, ALU.add))

                def sample(i):
                    step(dve.tensor_copy(hist_c[:, i, :, HIST_C], glu[:, i, HIST_C + SEQ:HIST_C + T]))
                    w = vec[:, V_DW + i:V_DW + (TAPS - 1) * KT + i + 1:KT].unsqueeze(1).to_broadcast([P, DEC, TAPS])
                    step(dve.tensor_tensor(prod_s[:], hist_c[:, i], w, ALU.mult))
                    step(dve.tensor_reduce(conv[:, i, SEQ:T], prod_s[:], AX.X, ALU.add))
                    dve.tensor_scalar(conv[:, i, SEQ:T], conv[:, i, SEQ:T], vec[:, V_DWB + i:V_DWB + i + 1], None, ALU.add)\
                       .then_inc(conv_ready, 1)

                for i in range(KT):
                    n = At(u + 2 * i)
                    dve.wait_ge(units_done, (n + 1).v)
                    dve.tensor_tensor(halves(act_in[:, 0, :]), accumulator(At(0)), halves(rstd[:]), ALU.mult).then_inc(evacuated, 1)
                    split(n + 2)
                    dve.wait_ge(units_done, (n + 2).v)
                    dve.tensor_tensor(halves(act_in[:, 1, :]), accumulator(At(1)), halves(rstd[:]), ALU.mult).then_inc(evacuated, 1)
                    split(n + 3)
                    dve.wait_ge(gate_ready, i + 1)
                    dve.wait_ge(evacuated, m0 + 2 * i + 1)
                    dve.scalar_tensor_tensor(glu[:, i, HIST_C:HIST_C + T], act_in[:, 0, :], vec[:, V_BIN + i:V_BIN + i + 1],
                                             gate_s[:, i % 2, :], ALU.add, ALU.mult).then_inc(glu_ready, 1)
                    dve.wait_ge(glu_ready, i + 1)
                    taps(i)
                    if i >= 3:
                        dve.wait_ge(tp_taken, TP["conv"] + 4)
                        for k in range(0 if i == 3 else i, i + 1):
                            sample(k)
                dve.wait_ge(cmean, 1)
                for k in range(KT):
                    dve.wait_ge(conv_ready, k + 1)
                    dve.tensor_tensor(halves(conv[:, k, :]), halves(conv[:, k, :]), pair[:, :, 0:HALF], ALU.subtract).then_inc(cent, 1)
                dve.wait_ge(crstd, 1)
                for k in range(KT):
                    dve.tensor_tensor(glu[:, k, 0:T], conv[:, k, :], sq[:, 0, :], ALU.mult).then_inc(cnorm, 1)
                for k in range(KT):
                    dve.wait_ge(mix_hi_ok, MIX["conv"] + k + 1)
                    dve.tensor_tensor(mix_lo[:, k, :], conv[:, k, :], mix_hi[:, k, :].bitcast(F32), ALU.subtract).then_inc(mix_lo_ok, 1)
                u = UNIT["conv_out"]
                for i in range(KT):
                    dve.wait_ge(units_done, u + i + 1)
                    dve.scalar_tensor_tensor(halves(x[:, i, :]), accumulator(At(i)), vec[:, V_BOUT + i:V_BOUT + i + 1],
                                             halves(x[:, i, :]), ALU.add, ALU.add).then_inc(evacuated, 1)
                    split(At(u + i + 2))
                    next_low(XIN[3], At(i), V_FFN + 8)

            def attention():
                u, m0 = UNIT["qkv"], TILE["qkv"]
                dve.wait_ge(rstd_ready, 5)

                def project(h, j, dst):
                    n = At(u + 3 * h + j)
                    dve.wait_ge(units_done, (n + 1).v)
                    if h:
                        if j < 2:
                            dve.wait_ge(qkn_ready, 2 * h)
                        else:
                            dve.wait_ge(t_ready, h)
                            dve.wait_ge(saved_s, 3 * h)
                    dve.tensor_tensor(halves(dst[:]), accumulator(At(m0 + 3 * h + j)), halves(rstd[:]), ALU.mult).then_inc(evacuated, 1)
                    split(n + 2)

                def maxima(g, piece):
                    dve.wait_ge(qk_ready, 3 * g + piece + 1)
                    dve.wait_ge(bias_ready, g + 1)
                    if g or piece:
                        dve.wait_ge(a_ready, 3 * g + piece)
                    for off, i in PIECES[piece]:
                        for c in range(2):
                            w, j = (i + 1) * P, i % 2
                            last = dve.tensor_tensor_reduce(
                                out=s_buf[:, c, off:off + w], in0=pair[:, c, off:off + w], in1=bias_h[:, g % 2, SEQ - w:SEQ],
                                scale=1.0, scalar=-3e38, op0=ALU.add, op1=ALU.max, accum_out=row_scl[:, c, j:j + 1])
                    last.then_inc(s_taken, 1)
                    dve.wait_ge(s_taken, 3 * g + piece + 1)
                    dve.tensor_scalar(row_max[:], row_scl[:], -SCALE, None, ALU.mult).then_inc(max_ready, 1)

                def weights(g, piece):
                    dve.wait_ge(exp_done, 3 * g + piece + 1)
                    step(dve.reciprocal(row_inv[:], row_sum[:]))
                    step(dve.tensor_scalar(row_inv[:, 1, :], row_inv[:, 1, :], neg_lam[:], None, ALU.mult))
                    if g or piece:
                        dve.wait_ge(at_ready, 3 * g + piece)
                    for off, i in PIECES[piece]:
                        w, j = (i + 1) * P, i % 2
                        dve.tensor_scalar(t_buf[:, off:off + w], s_buf[:, 1, off:off + w], row_inv[:, 1, j:j + 1], None, ALU.mult)\
                           .then_inc(dve_seq, 1)
                        seq[0] += 1
                    for off, i in PIECES[piece]:
                        w, j = (i + 1) * P, i % 2
                        dve.wait_ge(dve_seq, seq[0])
                        last = dve.scalar_tensor_tensor(a_buf[:, off:off + w], s_buf[:, 0, off:off + w], row_inv[:, 0, j:j + 1],
                                                        t_buf[:, off:off + w], ALU.mult, ALU.add)
                    last.then_inc(a_ready, 1)

                def take_output(g):
                    dve.wait_ge(pv_done, 3 * g + 3)
                    rows = bank7[:, :].rearrange("p (b c) -> p b c", b=4)
                    step(dve.tensor_reduce(o_max[:, :, g], rows, AX.X, ALU.max, apply_absolute_value=True))
                    step(dve.tensor_scalar(o_max[:, :, g], o_max[:, :, g], 1e-15, 1e37, ALU.max, ALU.min))
                    step(dve.reciprocal(o_inv[:, :, g], o_max[:, :, g]))
                    dve.tensor_tensor(o_tok[:, :, g, :], rows, o_inv[:, :, g:g + 1].to_broadcast([P, 4, P]), ALU.mult)\
                       .then_inc(o_taken, 1)
                    dve.wait_ge(osq_done, g + 1)
                    dve.tensor_reduce(o_ss[:, :, g], o_sq[:].rearrange("p (b c) -> p b c", b=4), AX.X, ALU.add)\
                       .then_inc(oss_done, 1)

                for h in range(HEADS + 2):
                    if h < HEADS:
                        project(h, 0, q_raw)
                    if 1 <= h <= HEADS:
                        maxima(h - 1, 0)
                        weights(h - 1, 0)
                    if h < HEADS:
                        project(h, 1, k_raw)
                    if h >= 2:
                        take_output(h - 2)
                    if 1 <= h <= HEADS:
                        maxima(h - 1, 1)
                        weights(h - 1, 1)
                    if h < HEADS:
                        project(h, 2, v_raw)
                    if 1 <= h <= HEADS:
                        maxima(h - 1, 2)
                    if h < HEADS:
                        for j, (src, ln, gain, dst) in enumerate(((q_raw, ln_q, V_QN, qn), (k_raw, ln_k, V_KN, kn))):
                            dve.wait_ge(nrm_exp, 2 * h + j + 1)
                            if h:
                                dve.wait_ge(saved_s, 3 * h)
                            dve.scalar_tensor_tensor(dst[:], src[:], vec[:, gain:gain + 1], ln[:], ALU.mult, ALU.mult)\
                               .then_inc(qkn_ready, 1)
                    if 1 <= h <= HEADS:
                        weights(h - 1, 2)

                dve.wait_ge(saved_s, 3 * HEADS)
                step(dve.memset(q_diag[:], 0.0))
                for c in range(2):
                    rows = slice(c * QK, (c + 1) * QK)
                    last = dve.tensor_copy(q_diag[rows, :, c], qs[rows].rearrange("p h b -> p (h b)"))
                last.then_inc(qdiag_ready, 1)
                dve.tensor_tensor(new_dec[:], qs[:].rearrange("p h b -> p (h b)"), ks[:].rearrange("p h b -> p (h b)"), ALU.mult)\
                   .then_inc(new_prod_ok, 1)
                with dve.Fori(0, DEC) as b:
                    for j, src in enumerate((pair, acc)):
                        dve.wait_ge(kT_full, b * 2 + (j + 1))
                        dve.tensor_copy(kT[:, j, 512:1024], src[:, 1, :]).then_inc(kT_d, 1)
                dve.wait_ge(s_rows_full, 1)
                dve.tensor_tensor(s_dec[:, :, 0:PAST], pair[0:R, 0, :].rearrange("p (c k) -> p c k", c=2),
                                  const[0:R, C_POS:C_POS + PAST].unsqueeze(1).to_broadcast([R, 2, PAST]), ALU.add)
                step(dve.tensor_scalar(s_dec[:, :, PAST], pair[0:R, 1, 0:2], float(QK), None, ALU.mult))
                step(dve.tensor_reduce(m_dec[:, 0:2], s_dec[:], AX.X, ALU.max))
                dve.tensor_scalar(m_dec[:, 2:4], m_dec[:, 0:2], -SCALE, None, ALU.mult).then_inc(dec_max_ok, 1)
                dve.wait_ge(dec_exp_ok, 1)
                step(dve.reciprocal(m_dec[:, 6:8], m_dec[:, 4:6]))
                step(dve.tensor_scalar(m_dec[:, 7:8], m_dec[:, 7:8], neg_lam[0:R, :], None, ALU.mult))
                step(dve.tensor_scalar(t_dec[:], s_dec[:, 1, :], m_dec[:, 7:8], None, ALU.mult))
                dve.scalar_tensor_tensor(a_dec[:], s_dec[:, 0, :], m_dec[:, 6:7], t_dec[:], ALU.mult, ALU.add).then_inc(a_dec_ok, 1)
                dve.wait_ge(a_dec_full, 1)
                step(dve.tensor_tensor(new_dec[:], bank7[:, 0:R], vs[:].rearrange("p h b -> p (h b)"), ALU.mult))
                dve.wait_ge(vpage_used, DEC)
                dve.tensor_tensor(os_col[:], pair[:, 0, 0:R], new_dec[:], ALU.add).then_inc(os_col_ok, 1)
                dve.wait_ge(os_full, 1)
                step(dve.tensor_reduce(m_dec[:, 11:12], pair[0:R, 1, 0:P], AX.X, ALU.max, apply_absolute_value=True))
                step(dve.tensor_scalar(m_dec[:, 11:12], m_dec[:, 11:12], 1e-15, 1e37, ALU.max, ALU.min))
                step(dve.reciprocal(m_dec[:, 12:13], m_dec[:, 11:12]))
                dve.tensor_scalar(os_tok[:], pair[0:R, 1, 0:P], m_dec[:, 12:13], None, ALU.mult).then_inc(os_in_ok, 1)

                def radicands(mean_out, sum_out, ss, inv):
                    step(dve.tensor_tensor(mean_out, inv, inv, ALU.mult))
                    step(dve.tensor_scalar(mean_out, mean_out, EPS, None, ALU.mult))
                    step(dve.scalar_tensor_tensor(mean_out, ss, 1.0 / P, mean_out, ALU.mult, ALU.add))
                    step(dve.tensor_copy(sum_out, ss))

                def factors(out, mean_root, sum_root, largest):
                    step(dve.scalar_tensor_tensor(sum_root, largest, 2.0 ** -64, sum_root, ALU.mult, ALU.mult))
                    step(dve.tensor_scalar(sum_root, sum_root, 1.0, None, ALU.is_lt))
                    step(dve.reciprocal(out, mean_root))
                    step(dve.tensor_tensor(out, out, sum_root, ALU.mult))

                flat = "p b h -> p (b h)"
                dve.wait_ge(oss_done, HEADS)
                radicands(o_tmp[:, 0, :], o_tmp[:, 1, :], o_ss[:].rearrange(flat), o_inv[:].rearrange(flat))
                dve.memset(row_inv[:, 0, 0:1], 0.0).then_inc(roots_in, 1)
                dve.wait_ge(os_sq_ok, 1)
                radicands(m_dec[:, 9:10], m_dec[:, 10:11], m_dec[:, 8:9], m_dec[:, 12:13])
                dve.memset(row_inv[:, 0, 0:1], 0.0).then_inc(roots_in, 1)
                dve.wait_ge(roots_ok, 1)
                factors(m_dec[:, 13:14], m_dec[:, 9:10], m_dec[:, 10:11], m_dec[:, 11:12])
                dve.tensor_scalar(os_tok[:], os_tok[:], m_dec[:, 13:14], None, ALU.mult).then_inc(os_scaled, 1)
                factors(o_tmp[:, 2, :], o_tmp[:, 0, :], o_tmp[:, 1, :], o_max[:].rearrange(flat))
                scale = o_tmp[:, 2, :].rearrange("p (b h) -> p b h", b=4)

                def scale_head(h):
                    dve.tensor_tensor(o_tok[:, :, h, :], o_tok[:, :, h, :], scale[:, :, h:h + 1].to_broadcast([P, 4, P]), ALU.mult)\
                       .then_inc(o_scaled, 1)
                scale_head(0)
                dve.wait_ge(mix_hi_ok, MIX["attn"] + 1)
                dve.scalar_tensor_tensor(mix_lo[:, :, SEQ:T], bank7[:, 0:R].rearrange("p (h b) -> p h b", h=HEADS), sub_gain[:],
                                         mix_hi[:, :, SEQ:T].bitcast(F32), ALU.mult, ALU.subtract).then_inc(mix_lo_ok, 1)
                for h in range(HEADS):
                    if h + 1 < HEADS:
                        scale_head(h + 1)
                    dve.wait_ge(mix_hi_ok, MIX["attn"] + 2 + h)
                    dve.scalar_tensor_tensor(mix_lo[:, h, 0:SEQ], bank6[:, :], sub_gain[:], mix_hi[:, h, 0:SEQ].bitcast(F32),
                                             ALU.mult, ALU.subtract).then_inc(mix_lo_ok, 1)
                u = UNIT["w_o"]
                for i in range(KT):
                    dve.wait_ge(units_done, u + i + 1)
                    dve.tensor_tensor(halves(x[:, i, :]), accumulator(At(i)), halves(x[:, i, :]), ALU.add).then_inc(evacuated, 1)
                    split(At(u + i + 2))
                    next_low(XIN[5], At(i), V_FFN + 16)

            split(At(0))
            split(At(1))
            dve.wait_ge(lam_in, 64)
            for j in range(2):
                dve.tensor_tensor_reduce(out=lam_tmp[:, 0:QK], in0=lam_rows[:, 2 * j, :], in1=lam_rows[:, 2 * j + 1, :],
                                         scale=1.0, scalar=0.0, op0=ALU.mult, op1=ALU.add,
                                         accum_out=lam_tmp[:, QK + j:QK + j + 1]).then_inc(lam_sums, 1)
                dve.wait_ge(lam_sums, j + 1)
            dve.wait_ge(lam_exps, 1)
            step(dve.tensor_tensor(neg_lam[:], lam_tmp[:, QK + 1:QK + 2], lam_tmp[:, QK:QK + 1], ALU.subtract))
            step(dve.tensor_scalar(neg_lam[:], neg_lam[:], -LAMBDA_INIT, None, ALU.add))
            dve.wait_ge(tp_taken, 3)
            step(dve.tensor_scalar(sub_gain[:], vec[:, V_SUB:V_SUB + 1], 1.0 - LAMBDA_INIT, None, ALU.mult))
            pool(0)
            ffn(0)
            conv_mixer()
            ffn(1)
            attention()
            ffn(2)
            pool(1)
            ffn(3)

        @block.gpsimd
        def _(pool_e):
            def add_squares(r):
                for m in range(KT):
                    pool_e.wait_ge(sq_ready, 8 * r + m + 1)
                    if m == 0:
                        if r:
                            pool_e.wait_ge(mean_ready, r)
                        pool_e.tensor_copy(sqacc[:], sq[:, 0, :]).then_inc(sq_added, 1)
                    else:
                        pool_e.wait_ge(sq_added, 8 * r + m)
                        pool_e.tensor_tensor(sqacc[:], sqacc[:], sq[:, m % 2, :], ALU.add).then_inc(sq_added, 1)

            def store_stage(b, hist, states_p, states_s):
                pool_e.wait_ge(tp_taken, b)
                pool_e.dma_start(states_p, stage[0:hist, :]).then_inc(stored, 16)
                pool_e.dma_start(states_s, stage[hist:hist + DEC, :]).then_inc(stored, 16)

            pool_e.memset(avg[:], 1.0 / D).then_inc(ready0, 1)
            pool_e.memset(eps[:], EPS).then_inc(ready0, 1)
            add_squares(0)
            for q in range(2):
                store_stage(TP[f"pool{q}"] + 4, HIST_P, pool_state_p[q, 0], pool_state_s[q, :, HIST_P - 1, :])
                add_squares(6 * q + 1)
                if q:
                    break
                add_squares(2)
                store_stage(TP["conv"] + 6, HIST_C, conv_state_p[0, 0], conv_state_s[0, :, HIST_C - 1, :])
                add_squares(3)
                add_squares(4)
                k_out = k_rows_p[0, 0].rearrange("(b p) h c d -> p b h (c d)", p=P)
                v_out = v_rows_p[0, 0].rearrange("(b p) h d -> p b h d", p=P)
                pool_e.wait_ge(units_done, UNIT["qkv"])
                for h in range(HEADS + 1):
                    if h < HEADS:
                        if h >= 2:
                            pool_e.wait_ge(s_taken, 3 * (h - 1))
                        pool_e.tensor_scalar(bias_h[:, h % 2, :], const[:, C_DIST:C_DIST + SEQ], 2.0 ** -(h + 1) / SCALE, 0.0,
                                             ALU.mult, ALU.add).then_inc(bias_ready, 1)
                        pool_e.wait_ge(evacuated, TILE["qkv"] + 3 * h + 3)
                        pool_e.tensor_copy(vs[:, h, :], v_raw[:, SEQ:T]).then_inc(saved_s, 1)
                        pool_e.wait_ge(qkn_ready, 2 * h + 2)
                        pool_e.tensor_copy(qs[:, h, :], qn[:, SEQ:T]).then_inc(saved_s, 1)
                        pool_e.tensor_copy(ks[:, h, :], kn[:, SEQ:T]).then_inc(saved_s, 1)
                    if h:
                        g = h - 1
                        pool_e.wait_ge(t_taken, 2 * g + 2)
                        pool_e.dma_start(k_out[:, :, g, :], k_tok[:, g % 2]).then_inc(rows_stored[g % 2], 16)
                        pool_e.dma_start(v_out[:, :, g, :], v_tok[:, g % 2]).then_inc(rows_stored[g % 2], 16)
                pool_e.wait_ge(rows_s_taken, 2)
                for h in range(HEADS):
                    pool_e.dma_start(k_rows_s[0, :, 0, h].rearrange("b c d -> b (c d)"), ks_rows_sb[h * DEC:(h + 1) * DEC, :])\
                          .then_inc(stored, 16)
                    pool_e.dma_start(v_rows_s[0, :, 0, h, :], vs_rows_sb[h * DEC:(h + 1) * DEC, :]).then_inc(stored, 16)
                add_squares(5)
                add_squares(6)
            for m in range(KT):
                tb = TP["end"] + 2 * m
                pool_e.wait_ge(tp_taken, tb + 1)
                pool_e.dma_start(y_prompt[0].rearrange("(b p) c -> p b c", p=P)[:, :, m * P:(m + 1) * P],
                                 y_sb[:, m, 0:SEQ].rearrange("p (b c) -> p b c", b=4)).then_inc(stored, 16)
                pool_e.wait_ge(tp_taken, tb + 2)
                pool_e.dma_start(y_sample[:, 0, m * P:(m + 1) * P], y_sb[0:DEC, m, SEQ:SEQ + P]).then_inc(stored, 16)


OUTPUTS = (("y_prompt", (1, SEQ, D)), ("y_sample", (DEC, 1, D)),
           ("pool_state_p", (2, 1, HIST_P, D)), ("pool_state_s", (2, DEC, HIST_P, D)),
           ("conv_state_p", (1, 1, HIST_C, D)), ("conv_state_s", (1, DEC, HIST_C, D)),
           ("k_rows_p", (1, 1, SEQ, HEADS, 2, QK)), ("v_rows_p", (1, 1, SEQ, HEADS, P)),
           ("k_rows_s", (1, DEC, 1, HEADS, 2, QK)), ("v_rows_s", (1, DEC, 1, HEADS, P)))
INPUTS = ("x_prompt", "x_sample", "state_pool", "state_conv", "cache_k", "cache_v", "page_table",
          "norm_mix", "norm_ffn", "pool_w", "pool_scale", "conv_w_in", "conv_b_in", "conv_dw", "conv_dw_b",
          "conv_ln_g", "conv_ln_b", "conv_w_out", "conv_b_out", "attn_w_qkv", "attn_q_norm", "attn_k_norm",
          "attn_lq1", "attn_lk1", "attn_lq2", "attn_lk2", "attn_subln", "attn_w_o",
          "ffn_w_gate", "ffn_w_up", "ffn_w_down")


def kernel(**inputs):
    from concourse import bacc
    from concourse.bass_utils import run_bass_kernel_spmd

    nc = bacc.Bacc("TRN2", target_bir_lowering=False, num_devices=1)
    arrays, args = {}, []
    for name in INPUTS:
        a = np.ascontiguousarray(inputs[name])
        arrays[f"in_{name}"] = a
        args.append(nc.dram_tensor(f"in_{name}", a.shape, mybir.dt.from_np(a.dtype), kind="ExternalInput").ap())
    arrays["in_shape_constants"] = constants()
    args.append(nc.dram_tensor("in_shape_constants", (P, N_CONST), F32, kind="ExternalInput").ap())
    for name, shape in OUTPUTS:
        args.append(nc.dram_tensor(f"out_{name}", shape, F32, kind="ExternalOutput").ap())
    trunk_step(nc, *args)
    r = run_bass_kernel_spmd(nc, [arrays], core_ids=[0])
    return tuple(r.results[0][f"out_{name}"] for name, _ in OUTPUTS)
```

```python
import math
from contextlib import ExitStack

import numpy as np

import concourse.bass as bass
from concourse import mybir

F32 = mybir.dt.float32
F32R = mybir.dt.float32r
I32 = mybir.dt.int32
ALU = mybir.AluOpType
ACT = mybir.ActivationFunctionType
AX = mybir.AxisListType

P = 128
D = 1024
KT = D // P
SEQ, DEC = 512, 8
T = SEQ + DEC
HALF = T // 2
FF = 2816
FT = FF // P
HEADS, QK = 8, 64
PAST, PAGE = 256, 128
WINDOWS = (2, 4, 8, 16)
HIST_P, HIST_C, TAPS = 15, 30, 31
EPS = 1e-6
LAMBDA_INIT = 0.8 - 0.6 * math.exp(-0.3 * 2)
SCALE = QK ** -0.5
TAIL_P = HIST_P + DEC
TAIL_C = HIST_C + DEC

ORDER = [("pool0", 2, 8), ("ffn0", 2 * FT + 24, 2 * FT + 8), ("conv_in", 16, 16), ("conv_out", 8, 8),
         ("ffn1", 2 * FT + 24, 2 * FT + 8), ("qkv", 24, 24), ("w_o", 8, 8),
         ("ffn2", 2 * FT + 24, 2 * FT + 8), ("pool1", 2, 8), ("ffn3", 2 * FT + 24, 2 * FT + 8)]
UNIT, TILE = {}, {}
_u = _m = 0
for _name, _units, _tiles in ORDER:
    UNIT[_name], TILE[_name] = _u, _m
    _u, _m = _u + _units, _m + _tiles
UNITS = _u

V_MIX, V_FFN, V_PSCALE, V_BIN, V_DWB, V_LNG, V_LNB, V_BOUT, V_DW, V_QN, V_KN, V_SUB = (
    0, 32, 64, 80, 96, 104, 112, 120, 128, 376, 377, 378)
C_ID, C_BLK, C_DIST, C_POS, C_CNT = 0, 128, 256, 768, 1024
N_CONST = C_CNT + 64


class At:

    def __init__(self, start, step=0, i=None):
        self.start, self.step, self.i = start, step, i

    def __add__(self, k):
        return At(self.start + k, self.step, self.i)

    @property
    def v(self):
        return self.start if self.i is None else self.i * self.step + self.start

    def slot(self, depth):
        assert self.step % depth == 0
        return self.start % depth

    def turn(self, depth):
        assert self.step % depth == 0
        return At(self.start // depth, self.step // depth, self.i)


def at(start, step, i):
    return At(start + step * i) if isinstance(i, int) else At(start, step, i)


def tile_of(t, m):
    if m.i is None:
        return t[:, m.start, :]
    return t[:, bass.ds(m.v, 1), :].rearrange("p o c -> p (o c)")


XIN = {1: 0, 2: 1, 3: 2, 4: 3, 5: 4, 7: 5}
PIECES = (((0, 0), (P, 1)), ((0, 2),), ((0, 3),))
MIX = {"pool0": 0, "conv": 4, "attn": 12, "pool1": 21}
N_CONST_LOADS = 1 + 10 + 5
DVE_TILES, POOL_TILES, PE_TILE = (1, 3, 5, 7), (0, 2, 4), 6
STORED = {"pool0": 2, "conv": 4, "attn": 4 + 2 * HEADS, "pool1": 6 + 2 * HEADS, "end": 6 + 2 * HEADS + 2 * KT}


def constants():
    c = np.zeros((P, N_CONST), np.float32)
    c[:, C_ID:C_ID + P] = np.eye(P)
    c[0:QK, C_BLK:C_BLK + QK] = 1.0 / QK
    c[QK:P, C_BLK + QK:C_BLK + P] = 1.0 / QK
    dist = np.arange(SEQ)[None, :] - (SEQ - P) - np.arange(P)[:, None]
    c[:, C_DIST:C_DIST + SEQ] = np.where(dist <= 0, dist, -1e33)
    slope = 2.0 ** -(np.arange(HEADS * DEC) // DEC + 1.0)
    c[0:HEADS * DEC, C_POS:C_POS + PAST] = slope[:, None] * (np.arange(PAST) - PAST)[None, :] / SCALE
    for g, win in enumerate(WINDOWS):
        c[:, C_CNT + 16 * g:C_CNT + 16 * g + 16] = 1.0 / np.minimum(np.arange(16) + 1, win)
    return c


def trunk_step(nc, x_prompt, x_sample, state_pool, state_conv, cache_k, cache_v, page_table,
               norm_mix, norm_ffn, pool_w, pool_scale, conv_w_in, conv_b_in, conv_dw, conv_dw_b,
               conv_ln_g, conv_ln_b, conv_w_out, conv_b_out, attn_w_qkv, attn_q_norm, attn_k_norm,
               attn_lq1, attn_lk1, attn_lq2, attn_lk2, attn_subln, attn_w_o,
               ffn_w_gate, ffn_w_up, ffn_w_down, shape_constants,
               y_prompt, y_sample, pool_state_p, pool_state_s, conv_state_p, conv_state_s,
               k_rows_p, v_rows_p, k_rows_s, v_rows_s):
    ctx = ExitStack()
    with ctx:
        place = [16512]

        def fixed(name, shape, dt=F32):
            t = nc.alloc_sbuf_tensor_at(name, shape, dt, offset=place[0])
            place[0] += (4 * int(np.prod(shape[1:])) + 31) // 32 * 32
            return t

        def overlay(start):
            at = [start]

            def take(name, shape, dt=F32):
                t = nc.alloc_sbuf_tensor_at(name, shape, dt, offset=at[0])
                at[0] += (4 * int(np.prod(shape[1:])) + 31) // 32 * 32
                take.end = at[0]
                return t
            return take

        x = fixed("x", [P, KT, T])
        xin_at = place[0]
        xin_hi = fixed("xin_hi", [P, KT, T], F32R)
        xin_lo = fixed("xin_lo", [P, KT, T], F32R)
        rstd_at = place[0]
        rstd = fixed("rstd", [P, T])
        lnb = fixed("lnb", [P, T])
        sqacc = fixed("sqacc", [P, T])
        sq = fixed("sq", [P, 2, T])
        raw = fixed("raw", [P, 4, 1024])
        w_hi = [fixed(f"w_hi{s}", [P, 1024], F32R) for s in range(2)]
        w_lo = [fixed(f"w_lo{s}", [P, 1024], F32R) for s in range(2)]
        const = fixed("const", [P, N_CONST])
        vec = fixed("vec", [P, 379])
        avg = fixed("avg", [P, P])
        eps = fixed("eps", [P, 1])
        one_row = fixed("one_row", [P, 2 * DEC - 1])
        neg_lam = fixed("neg_lam", [P, 1])
        sub_gain = fixed("sub_gain", [P, 1])
        stage = fixed("stage", [TAIL_C, D])
        qs, ks, vs = (fixed(n, [P, HEADS, DEC]) for n in ("qs", "ks", "vs"))
        temps_at = place[0]
        take = overlay(temps_at)
        g_buf = take("g_buf", [P, 2, T])
        sg_buf = take("sg_buf", [P, 2, T])
        u_buf = take("u_buf", [P, T])
        h_buf = take("h_buf", [P, 2, T])
        arena_at = take.end
        take = overlay(arena_at)
        h_hi = take("h_hi", [P, FT, T], F32R)
        h_lo = take("h_lo", [P, FT, T], F32R)
        arena_end = take.end
        assert arena_end <= nc.sbuf_usable_end
        ident = const[:, C_ID:C_ID + P]
        blk = const[:, C_BLK:C_BLK + P]

        take = overlay(arena_at)
        x_rows = take("x_rows", [P, 4, D])
        xs_rows = take("xs_rows", [DEC, D])
        vec_rows = take("vec_rows", [P, 3, P])
        lam_rows = take("lam_rows", [P, 4, QK])
        lam_tmp = take("lam_tmp", [P, QK + 4])
        take = overlay(arena_at)
        mix_hi = take("mix_hi", [P, KT, T], F32R)
        mix_lo = take("mix_lo", [P, KT, T], F32R)
        mixer_at = take.end
        take = overlay(mixer_at)
        hn = take("hn", [P, KT, 16 + T])
        hist_rows = take("hist_rows", [DEC * HIST_P, D])
        hist_s = take("hist_s", [P, KT, DEC, 16])
        wsum = take("wsum", [P, 2, 2, 16 + SEQ])
        diff = take("diff", [P, 2, 2, T])
        edge = take("edge", [P, 2, 16])
        last_s = take("last_s", [P, 2, DEC])
        assert take.end <= arena_end
        take = overlay(mixer_at)
        glu = take("glu", [P, KT, HIST_C + T])
        conv = take("conv", [P, KT, T])
        hist_c = take("hist_c", [P, KT, DEC, TAPS])
        chist_rows = take("chist_rows", [4 * HIST_C, 2, D])
        prod_p = take("prod_p", [P, 3, SEQ])
        assert take.end <= arena_end
        x_out = nc.alloc_sbuf_tensor_at("x_out", [P, 4, T], F32, offset=temps_at)
        prod_s = nc.alloc_sbuf_tensor_at("prod_s", [P, KT // 2, DEC, TAPS], F32, offset=temps_at + 5 * 4 * T)
        assert KT // 2 * DEC * TAPS <= 2 * T
        diag = nc.alloc_sbuf_tensor_at("diag", [P, 4, P], F32, offset=temps_at + 4 * 4 * T)
        act_in = g_buf
        gate_s = sg_buf
        take = overlay(temps_at)
        q_raw, k_raw, v_raw, qn, kn, ln_q, ln_k = (
            take(n, [P, T]) for n in ("q_raw", "k_raw", "v_raw", "qn", "kn", "ln_q", "ln_k"))
        assert take.end <= arena_at
        take = overlay(mixer_at)
        o_tok = take("o_tok", [P, 4, HEADS, P])
        v_page = [take(f"v_page{n}", [P, 2, D]) for n in range(2)]
        head_at = take.end
        s_buf = take("s_buf", [P, 2, SEQ])
        a_buf = take("a_buf", [P, SEQ])
        t_buf = take("t_buf", [P, SEQ])
        aT = take("aT", [P, SEQ])
        v_tok = take("v_tok", [P, 2, 4, P])
        k_tok = take("k_tok", [P, 2, 4, P])
        bias_h = take("bias_h", [P, 2, SEQ])
        o_sq = take("o_sq", [P, SEQ])
        small_at = take.end
        row_max = take("row_max", [P, 2, 2])
        row_sum = take("row_sum", [P, 2, 2])
        row_scl = take("row_scl", [P, 2, 2])
        row_inv = take("row_inv", [P, 2, 2])
        o_max = take("o_max", [P, 4, HEADS])
        o_inv = take("o_inv", [P, 4, HEADS])
        o_ss = take("o_ss", [P, 4, HEADS])
        o_tmp = take("o_tmp", [P, 3, 4 * HEADS])
        assert take.end <= arena_end, take.end - arena_end
        take = overlay(head_at)
        v_page += [take(f"v_page{n}", [P, 2, D]) for n in range(2, 4)]
        ks_rows_sb = take("ks_rows_sb", [HEADS * DEC, P])
        vs_rows_sb = take("vs_rows_sb", [HEADS * DEC, P])
        os_tok = take("os_tok", [HEADS * DEC, P])
        os_sq = take("os_sq", [HEADS * DEC, P])
        assert take.end <= small_at, take.end - small_at
        R = HEADS * DEC
        take = overlay(temps_at)
        k_prod = take("k_prod", [P, 2, 2, D // 2])
        s_cols = take("s_cols", [P, 2, R, 2])
        s_dec = take("s_dec", [R, 2, PAST + 1])
        assert take.end <= temps_at + 7 * 4 * T
        a_dec = nc.alloc_sbuf_tensor_at("a_dec", [R, PAST + 1], F32, offset=xin_at)
        t_dec = nc.alloc_sbuf_tensor_at("t_dec", [R, PAST + 1], F32, offset=xin_at + 1056)
        aT_dec = nc.alloc_sbuf_tensor_at("aT_dec", [P, 2, R], F32, offset=xin_at + 2112)
        os_col = nc.alloc_sbuf_tensor_at("os_col", [P, R], F32, offset=xin_at + 2624)
        m_dec = nc.alloc_sbuf_tensor_at("m_dec", [R, 16], F32, offset=xin_at + 2880)
        new_dec = nc.alloc_sbuf_tensor_at("new_dec", [P, R], F32, offset=xin_at + 2944)
        os_rows = nc.alloc_sbuf_tensor_at("os_rows", [DEC, D], F32, offset=temps_at)
        take = overlay(xin_at + 3520)
        k_page = [take(f"k_page{n}", [P, 2, D]) for n in range(3)]
        assert take.end <= rstd_at
        y_sb = nc.alloc_sbuf_tensor_at("y_sb", [P, KT, SEQ + P], F32, offset=xin_at)

        acc = nc.alloc_psum_tensor("acc", [P, 4, 512], F32)
        pair = nc.alloc_psum_tensor("pair", [P, 2, 512], F32)
        bank6 = nc.alloc_psum_tensor("bank6", [P, 512], F32)
        bank7 = nc.alloc_psum_tensor("bank7", [P, 512], F32)
        bank = [bank6, bank7]

        def sem(name):
            return ctx.enter_context(nc.semaphore(name))

        landed = [sem(f"landed{s}") for s in range(4)]
        split_hi, split_lo = sem("split_hi"), sem("split_lo")
        units_done = sem("units_done")
        tile_done = sem("tile_done")
        evacuated = sem("evacuated")
        sq_ready, sq_added = sem("sq_ready"), sem("sq_added")
        mean_ready, rstd_ready = sem("mean_ready"), sem("rstd_ready")
        xin_hi_ok, xin_lo_ok = sem("xin_hi_ok"), sem("xin_lo_ok")
        tp_full, tp_taken = sem("tp_full"), sem("tp_taken")
        sg_ready, h_ready, h_hi_ok, h_lo_ok = sem("sg_ready"), sem("h_ready"), sem("h_hi_ok"), sem("h_lo_ok")
        const_in, rows_in, lam_in, hist_in = sem("const_in"), sem("rows_in"), sem("lam_in"), sem("hist_in")
        ready0 = sem("ready0")
        stored, moved = sem("stored"), sem("moved")
        act_seq, dve_seq, pool_seq = sem("act_seq"), sem("dve_seq"), sem("pool_seq")
        hn_ready, diff_ready, mix_hi_ok, mix_lo_ok = sem("hn_ready"), sem("diff_ready"), sem("mix_hi_ok"), sem("mix_lo_ok")
        glu_ready, gate_ready = sem("glu_ready"), sem("gate_ready")
        conv_dve_ready, conv_pe_ready, conv_s_ready = sem("conv_dve_ready"), sem("conv_pe_ready"), sem("conv_s_ready")
        prod_ready, prod_added = sem("prod_ready"), sem("prod_added")
        diag_ready, diag_used = sem("diag_ready"), sem("diag_used")
        cmean, cent, csq, cvar, crstd, cnorm, cact = (
            sem(n) for n in ("cmean", "cent", "csq", "cvar", "crstd", "cnorm", "cact"))
        nsq_ready, nrm_ready, nrm_ln, nrm_exp = sem("nsq_ready"), sem("nrm_ready"), sem("nrm_ln"), sem("nrm_exp")
        qkn_ready, t_ready, t_taken = sem("qkn_ready"), sem("t_ready"), sem("t_taken")
        qk_ready, s_taken, max_ready, exp_done, a_ready, at_ready, at_taken, pv_done = (
            sem(n) for n in ("qk_ready", "s_taken", "max_ready", "exp_done", "a_ready", "at_ready", "at_taken", "pv_done"))
        bias_ready, o_taken, osq_done, oss_done, saved_s = (
            sem(n) for n in ("bias_ready", "o_taken", "osq_done", "oss_done", "saved_s"))
        rows_stored = [sem(f"rows_stored{s}") for s in range(2)]
        kpage_in = [sem(f"kpage_in{s}") for s in range(3)]
        vpage_in = [sem(f"vpage_in{s}") for s in range(4)]
        q_all_ready, kpage_used, vpage_used, factors_ok, v_weighted, os_rows_ok, os_turned = (
            sem(n) for n in ("q_all_ready", "kpage_used", "vpage_used", "factors_ok", "v_weighted", "os_rows_ok", "os_turned"))
        s_cols_ok, new_prod_ok, s_rows_full, dec_max_ok, dec_exp_ok, a_dec_ok, a_dec_full, aT_dec_ok = (
            sem(n) for n in ("s_cols_ok", "new_prod_ok", "s_rows_full", "dec_max_ok", "dec_exp_ok", "a_dec_ok",
                             "a_dec_full", "aT_dec_ok"))
        rows_s_full, rows_s_taken, os_col_ok, os_full, os_in_ok, os_sq_ok, os_scaled, os_back = (
            sem(n) for n in ("rows_s_full", "rows_s_taken", "os_col_ok", "os_full", "os_in_ok", "os_sq_ok",
                             "os_scaled", "os_back"))
        roots_in, roots_ok, o_scaled, o_back, lam_sums, lam_exps = (
            sem(n) for n in ("roots_in", "roots_ok", "o_scaled", "o_back", "lam_sums", "lam_exps"))

        block = ctx.enter_context(nc.Block())

        def accum(m):
            b = 2 * m.slot(2)
            return acc[:, b:b + 2, 0:HALF]

        def halves(t):
            return t.rearrange("p (h c) -> p h c", h=2)

        TP = {"start": 0, "pool0": 12, "conv": 16, "pool1": 22, "end": 26}

        @block.sync
        def _(sp):
            def load(n, src, cols=1024):
                if n.i is not None or n.start >= 4:
                    sp.wait_ge(split_lo, (n + -3).v)
                sp.dma_start(raw[:, n.slot(4), 0:cols].rearrange("p (k c) -> p k c", c=src.shape[-1]), src)\
                  .then_inc(landed[n.slot(4)], 16)

            def tiles(w, k0, k1, col):
                return w[k0 * P:k1 * P, col].rearrange("(k p) c -> p k c", p=P)

            def load_pool(q):
                for u in range(2):
                    load(At(UNIT[f"pool{q}"] + u), pool_w[q, 2 * u:2 * u + 2].rearrange("g (k p) c -> p (g k) c", p=P))

            def load_ffn(layer):
                base = UNIT[f"ffn{layer}"]

                def two_tiles(i):
                    for j in range(4):
                        w = (ffn_w_gate, ffn_w_up)[j % 2][layer]
                        load(at(base + j, 4, i), tiles(w, 0, KT, bass.ds(i * (2 * P) + (j // 2) * P, P)))
                two_tiles(0)
                with sp.Fori(1, FT // 2) as i:
                    two_tiles(i)
                with sp.Fori(0, 2) as i:
                    for c in range(4):
                        for j, (k0, k1) in enumerate(((0, 8), (8, 16), (16, FT))):
                            load(At(base + 2 * FT + 3 * c + j, 12, i),
                                 tiles(ffn_w_down[layer], k0, k1, bass.ds(i * (4 * P) + c * P, P)), (k1 - k0) * P)

            sp.dma_start(const[:], shape_constants).then_inc(const_in, 16)
            row = [0]

            def rows(src):
                n = src.shape[0]
                r = row[0]
                while n:
                    t, p0 = divmod(r, P)
                    k = min(n, P - p0)
                    sp.dma_start(vec_rows[p0:p0 + k, t, :], src[src.shape[0] - n:src.shape[0] - n + k, :]).then_inc(const_in, 16)
                    r, n = r + k, n - k
                row[0] = r
            sp.dma_start(x_rows[:], x_prompt[0].rearrange("(b p) d -> p b d", p=P)).then_inc(rows_in, 16)
            sp.dma_start(xs_rows[:], x_sample[:, 0, :]).then_inc(rows_in, 16)
            for src in (norm_mix, norm_ffn, pool_scale, conv_b_in, conv_dw_b, conv_ln_g, conv_ln_b, conv_b_out,
                        conv_dw[0]):
                rows(src.rearrange("l (k p) -> (l k) p", p=P))
            for j, src in enumerate((attn_q_norm, attn_k_norm)):
                for c in range(2):
                    sp.dma_start(vec_rows[120 + j:121 + j, 2, c * QK:(c + 1) * QK], src).then_inc(const_in, 16)
            sp.dma_start(vec_rows[122:123, 2, :], attn_subln).then_inc(const_in, 16)
            for j, src in enumerate((attn_lq1, attn_lk1, attn_lq2, attn_lk2)):
                sp.dma_start(lam_rows[:, j, :], src[0].partition_broadcast(P)).then_inc(lam_in, 16)
            for q in range(2):
                sp.dma_start(pool_state_s[q, :, 0:HIST_P - 1, :], state_pool[q, :, 1:HIST_P, :]).then_inc(moved, 16)
            sp.dma_start(conv_state_s[0, :, 0:HIST_C - 1, :], state_conv[0, :, 1:HIST_C, :]).then_inc(moved, 16)

            load_pool(0)
            sp.dma_start(hist_rows[:], state_pool[0].rearrange("b j d -> (b j) d")).then_inc(hist_in, 16)
            load_ffn(0)
            for i in range(KT):
                for half in range(2):
                    load(At(UNIT["conv_in"] + 2 * i + half), tiles(conv_w_in[0], 0, KT, slice(half * D + i * P, half * D + (i + 1) * P)))
                if i == 0:
                    sp.wait_ge(units_done, UNIT["conv_in"])
                    for t in range(2):
                        sp.dma_start(chist_rows[:, t, :], state_conv[0, 4 * t:4 * t + 4].rearrange("b j d -> (b j) d")).then_inc(hist_in, 16)
            for i in range(KT):
                load(At(UNIT["conv_out"] + i), tiles(conv_w_out[0], 0, KT, slice(i * P, (i + 1) * P)))
            load_ffn(1)
            def page(dst, cache, b, landed_sem):
                for j in range(2):
                    r = sp.value_load(page_table[b:b + 1, j:j + 1], min_val=0, max_val=cache.shape[1] - 1)
                    sp.dma_start(dst[:, j, :], cache[0, bass.ds(r, 1)].rearrange("o p h d -> p (o h d)")).then_inc(landed_sem, 16)
            for h in range(HEADS):
                for j in range(3):
                    load(At(UNIT["qkv"] + 3 * h + j), tiles(attn_w_qkv[0], 0, KT, slice(j * D + h * P, j * D + (h + 1) * P)))
                if h == 0:
                    sp.wait_ge(units_done, UNIT["qkv"])
                    for b in range(2):
                        page(v_page[b], cache_v, b, vpage_in[b])
            for i in range(4):
                load(At(UNIT["w_o"] + i), tiles(attn_w_o[0], 0, KT, slice(i * P, (i + 1) * P)))
            ck = cache_k.rearrange("l n p h c d -> l n p h (c d)")
            sp.wait_ge(units_done, UNIT["w_o"])
            for b in range(3):
                page(k_page[b], ck, b, kpage_in[b])
            sp.wait_ge(pv_done, 3 * HEADS)
            sp.wait_ge(oss_done, HEADS)
            for s in range(2):
                sp.wait_ge(rows_stored[s], 16 * HEADS)
            for b in range(2, 4):
                page(v_page[b], cache_v, b, vpage_in[b])
            for b in range(3, DEC):
                sp.wait_ge(kpage_used, b - 2)
                page(k_page[b % 3], ck, b, kpage_in[b % 3])
            for b in range(4, DEC):
                sp.wait_ge(vpage_used, b - 3)
                page(v_page[b % 4], cache_v, b, vpage_in[b % 4])
            for i in range(4, KT):
                load(At(UNIT["w_o"] + i), tiles(attn_w_o[0], 0, KT, slice(i * P, (i + 1) * P)))
            load_ffn(2)
            load_pool(1)
            sp.wait_ge(units_done, UNIT["pool1"])
            sp.dma_start(hist_rows[:], state_pool[1].rearrange("b j d -> (b j) d")).then_inc(hist_in, 16)
            load_ffn(3)
            sp.wait_ge(moved, 48)
            sp.wait_ge(stored, 16 * STORED["end"])

        @block.tensor
        def _(pe):
            def tile_products(m, w_tile, s, k_hi, k_lo, start, stop):
                b = 2 * m.slot(2)
                for t, (w, v) in enumerate(((w_hi[s], k_hi), (w_hi[s], k_lo), (w_lo[s], k_hi))):
                    for h in range(2):
                        last = pe.matmul(acc[:, b + h, 0:HALF], w[:, w_tile * P:(w_tile + 1) * P],
                                         v[:, h * HALF:(h + 1) * HALF],
                                         start=start and t == 0, stop=stop and t == 2)
                return last

            def unit(n, m, hi, lo, k0=0, k1=KT, kn_=KT, before=None):
                pe.wait_ge(split_lo, (n + 1).v)
                if k0 == 0 and (m.i is not None or m.start >= 2):
                    pe.wait_ge(evacuated, (m + -1).v)
                for k in range(k0, k1):
                    if before is not None:
                        before(k)
                    last = tile_products(m, k - k0, n.slot(2), hi[:, k, :], lo[:, k, :], k == 0, k == kn_ - 1)
                last.then_inc(units_done, 1)

            def means(r):
                pe.wait_ge(sq_added, 8 * r + 8)
                if r:
                    pe.wait_ge(rstd_ready, r)
                for h in range(2):
                    last = pe.matmul(pair[:, h, 0:HALF], avg[:], sqacc[:, h * HALF:(h + 1) * HALF], start=True, stop=True)
                last.then_inc(mean_ready, 1)

            def first_unit(n, m, r, xi):
                def before(k):
                    pe.wait_ge(xin_lo_ok, 8 * xi + k + 1)
                    if k == 5:
                        means(r)
                unit(n, m, xin_hi, xin_lo, before=before)

            def batch(b, parts, dst=None):
                if b >= 2:
                    pe.wait_ge(tp_taken, b - 1)
                to = bank[b % 2]
                for cols, src in parts:
                    rows_n, cols_n = src.shape[0], src.shape[-1]
                    last = pe.transpose(to[0:cols_n, cols:cols + rows_n], src, ident[0:rows_n, 0:rows_n])
                last.then_inc(tp_full, 1)

            def pool(q):
                u, m0, tb = UNIT[f"pool{q}"], TILE[f"pool{q}"], TP[f"pool{q}"]
                means(6 * q)
                pe.wait_ge(hist_in, 16 if q == 0 else 64)
                for b in range(2):
                    batch(tb + b, [(120 * k, hist_rows[:, (4 * b + k) * P:(4 * b + k + 1) * P]) for k in range(4)])
                pe.wait_ge(hn_ready, 8 * q + 8)
                for b in range(2):
                    tails(tb + 2 + b, hn, 16 + SEQ - HIST_P, TAIL_P, b)
                for g in range(4):
                    n = At(u + g // 2)
                    pe.wait_ge(split_lo, (n + 1).v)
                    pe.wait_ge(mix_lo_ok, MIX[f"pool{q}"] + g + 1)
                    for mt in range(2):
                        m = At(m0 + 2 * g + mt)
                        if m.start >= 2:
                            pe.wait_ge(evacuated, m.start - 1)
                        for k in range(2):
                            last = tile_products(m, ((g % 2) * 2 + k) * 2 + mt, n.slot(2),
                                                 mix_hi[:, 2 * g + k, :], mix_lo[:, 2 * g + k, :], k == 0, k == 1)
                        last.then_inc(units_done if (g % 2, mt) == (1, 1) else tile_done, 1)

            def tails(b, src, col, n, part):
                if b >= 2:
                    pe.wait_ge(tp_taken, b - 1)
                for k in range(4):
                    last = pe.transpose(bank[b % 2][0:n, k * P:(k + 1) * P], src[:, 4 * part + k, col:col + n], ident)
                last.then_inc(tp_full, 1)

            def ffn(layer):
                u, m0, r = UNIT[f"ffn{layer}"], TILE[f"ffn{layer}"], 2 * layer + 1
                first_unit(At(u), At(m0), r, XIN[r])
                for j in range(1, 4):
                    unit(At(u + j), At(m0 + j), xin_hi, xin_lo)
                with pe.Fori(1, FT // 2) as i:
                    for j in range(4):
                        unit(At(u + j, 4, i), At(m0 + j, 4, i), xin_hi, xin_lo)
                with pe.Fori(0, 2) as i:
                    for c in range(4):
                        m = At(m0 + 2 * FT + c, 4, i)
                        for j, (k0, k1) in enumerate(((0, 8), (8, 16), (16, FT))):
                            def before(k):
                                pe.wait_ge(h_lo_ok, FT * layer + k + 1)
                            unit(At(u + 2 * FT + 3 * c + j, 12, i), m, h_hi, h_lo, k0, k1, FT,
                                 before if c == 0 else None)
                        if layer == 3:
                            if c:
                                y_tile(m0, i, c - 1)
                            if c == 3:
                                y_tile(m0, i, 3)

            def y_tile(m0, i, c):
                pe.wait_ge(evacuated, i * 4 + (m0 + 2 * FT + c + 1))
                tb = TP["end"] + 2 * c
                pe.wait_ge(tp_taken, i * 8 + (tb - 1))
                for b in range(4):
                    last = pe.transpose(bank6[:, b * P:(b + 1) * P], x_out[:, c, b * P:(b + 1) * P], ident)
                last.then_inc(tp_full, 1)
                pe.wait_ge(tp_taken, i * 8 + tb)
                pe.transpose(bank7[0:DEC, 0:P], x_out[:, c, SEQ:T], ident).then_inc(tp_full, 1)

            def conv_mixer():
                u, m0 = UNIT["conv_in"], TILE["conv_in"]
                for i in range(KT):
                    for half in range(2):
                        n = 2 * i + half
                        if n == 0:
                            first_unit(At(u), At(m0), 2, XIN[2])
                        else:
                            unit(At(u + n), At(m0 + n), xin_hi, xin_lo)
                    if i == 1:
                        pe.wait_ge(hist_in, 48)
                        for b in range(4):
                            batch(TP["conv"] + b, [(240 * k + 120 * t, chist_rows[:, t, (2 * b + k) * P:(2 * b + k + 1) * P])
                                                   for k in range(2) for t in range(2)])
                pe.wait_ge(glu_ready, KT)
                for b in range(2):
                    tails(TP["conv"] + 4 + b, glu, SEQ, TAIL_C, b)
                pe.wait_ge(rstd_ready, 3)
                for w in range(TAPS):
                    pe.wait_ge(diag_ready, w + 1)
                    last = pe.matmul(pair[:, 0, :], diag[:, w % 4, :], glu[:, PE_TILE, w:w + SEQ],
                                     start=w == 0, stop=w == TAPS - 1)
                    last.then_inc(diag_used, 1)
                pe.wait_ge(conv_s_ready, 2)
                pe.wait_ge(conv_pe_ready, 1)
                order = [1, 3, 0, 2, 6, 5, 7, 4]
                for j, k in enumerate(order):
                    if k in DVE_TILES:
                        pe.wait_ge(conv_dve_ready, DVE_TILES.index(k) + 1)
                    elif k in POOL_TILES:
                        pe.wait_ge(prod_added, (TAPS - 1) * (POOL_TILES.index(k) + 1))
                    for h in range(2):
                        last = pe.matmul(pair[:, h, 0:HALF], avg[:], conv[:, k, h * HALF:(h + 1) * HALF],
                                         start=j == 0, stop=j == KT - 1)
                last.then_inc(cmean, 1)
                pe.wait_ge(cent, KT)
                for k in range(KT):
                    pe.wait_ge(csq, k + 1)
                    for h in range(2):
                        last = pe.matmul(pair[:, h, 0:HALF], avg[:], glu[:, k, h * HALF:(h + 1) * HALF],
                                         start=k == 0, stop=k == KT - 1)
                last.then_inc(cvar, 1)
                u, m0 = UNIT["conv_out"], TILE["conv_out"]
                for i in range(KT):
                    def before(k):
                        pe.wait_ge(mix_lo_ok, MIX["conv"] + k + 1)
                    unit(At(u + i), At(m0 + i), mix_hi, mix_lo, before=before if i == 0 else None)

            def attention():
                u, m0 = UNIT["qkv"], TILE["qkv"]

                def stats(i):
                    pe.wait_ge(nsq_ready, i + 1)
                    h, j = divmod(i, 2)
                    if h:
                        pe.wait_ge(s_taken, 3 * (h - 1) + j + 1)
                    else:
                        pe.wait_ge(rstd_ready, 5)
                        if j:
                            pe.wait_ge(nrm_ln, 1)
                    for t in range(2):
                        last = pe.matmul(pair[:, t, 0:HALF], blk, sq[:, 0, t * HALF:(t + 1) * HALF], start=True, stop=True)
                    last.then_inc(nrm_ready, 1)

                def turn_head(g):
                    pe.wait_ge(qkn_ready, 2 * g + 2)
                    if g:
                        pe.wait_ge(s_taken, 3 * g)
                    else:
                        pe.wait_ge(nrm_ln, 2)
                    for j, src in enumerate((kn, v_raw)):
                        for b in range(4):
                            last = pe.transpose(pair[:, j, b * P:(b + 1) * P], src[:, b * P:(b + 1) * P], ident)
                    last.then_inc(t_ready, 1)

                def scores(g, piece):
                    if piece == 0:
                        pe.wait_ge(t_taken, 2 * g + 2)
                    elif g + 1 < HEADS:
                        pe.wait_ge(nrm_ln, 2 * (g + 1) + piece)
                    pe.wait_ge(s_taken, 3 * g + piece) if g or piece else None
                    for off, i in PIECES[piece]:
                        for c in range(2):
                            w = (i + 1) * P
                            last = pe.matmul(pair[:, c, off:off + w], qn[c * QK:(c + 1) * QK, i * P:(i + 1) * P],
                                             kn[c * QK:(c + 1) * QK, 0:w], start=True, stop=True)
                    last.then_inc(qk_ready, 1)

                def turn_weights(g, piece):
                    pe.wait_ge(a_ready, 3 * g + piece + 1)
                    if g or piece:
                        pe.wait_ge(at_taken, 3 * g + piece)
                    for off, i in PIECES[piece]:
                        for j in range(i + 1):
                            last = pe.transpose(bank6[:, off + j * P:off + (j + 1) * P], a_buf[:, off + j * P:off + (j + 1) * P], ident)
                    last.then_inc(at_ready, 1)

                def mix_values(g, piece):
                    pe.wait_ge(at_taken, 3 * g + piece + 1)
                    pe.wait_ge(t_taken, 2 * g + 2)
                    if piece == 0 and g:
                        pe.wait_ge(o_taken, g)
                    for off, i in PIECES[piece]:
                        for j in range(i + 1):
                            last = pe.matmul(bank7[:, i * P:(i + 1) * P], aT[:, off + j * P:off + (j + 1) * P],
                                             v_tok[:, g % 2, j, :], start=j == 0, stop=j == i)
                    last.then_inc(pv_done, 1)

                def turn_back(h):
                    pe.wait_ge(o_scaled, h + 1)
                    if h:
                        pe.wait_ge(mix_lo_ok, MIX["attn"] + h)
                    for b in range(4):
                        last = pe.transpose(bank6[:, b * P:(b + 1) * P], o_tok[:, b, h, :], ident)
                    last.then_inc(o_back, 1)

                pe.wait_ge(tp_taken, TP["conv"] + 6)
                def step_of(h, j, mid, end):
                    n, m = At(u + 3 * h + j), At(m0 + 3 * h + j)
                    if h == j == 0:
                        first_unit(n, m, 4, XIN[4])
                    elif h < HEADS:
                        def before(k):
                            if k == KT // 2:
                                mid()
                        unit(n, m, xin_hi, xin_lo, before=before)
                    else:
                        mid()
                    end()

                def if_head(g, do, *piece):
                    if 0 <= g < HEADS:
                        do(g, *piece)

                for h in range(HEADS + 2):
                    def mid():
                        if_head(h - 2, turn_weights, 1)
                        if_head(h - 2, scores, 2)

                    def end():
                        if_head(h - 2, mix_values, 1)
                        if_head(h - 1, turn_head)
                    step_of(h, 0, mid, end)

                    def mid():
                        if_head(h - 2, turn_weights, 2)
                        if_head(h - 1, scores, 0)

                    def end():
                        if h < HEADS:
                            stats(2 * h)
                        if_head(h - 2, mix_values, 2)
                    step_of(h, 1, mid, end)

                    def mid():
                        if_head(h - 1, turn_weights, 0)
                        if_head(h - 1, scores, 1)

                    def end():
                        if h < HEADS:
                            stats(2 * h + 1)
                        if_head(h - 1, mix_values, 0)
                    step_of(h, 2, mid, end)

                pe.wait_ge(saved_s, 3 * HEADS)
                pe.wait_ge(o_taken, HEADS)
                for j, src in enumerate((ks, vs)):
                    last = pe.transpose(bank7[0:R, j * P:(j + 1) * P], src[:].rearrange("p h b -> p (h b)"), ident)
                last.then_inc(rows_s_full, 1)
                pe.wait_ge(evacuated, TILE["w_o"])
                for b in range(DEC):
                    if b >= 2:
                        pe.wait_ge(kpage_used, b - 1)
                    for h in range(HEADS):
                        last = pe.matmul(acc[:, 2 * (b % 2) + h // 4, (h % 4) * P:(h % 4 + 1) * P],
                                         qs[:, h, b:b + 1].to_broadcast([P, P]), ident, start=True, stop=True)
                    last.then_inc(q_all_ready, 1)
                    if b >= 2:
                        turn_back(b - 2)
                turn_back(HEADS - 2)
                turn_back(HEADS - 1)
                pe.wait_ge(s_cols_ok, DEC)
                for c in range(2):
                    for j in range(2):
                        pe.transpose(pair[0:R, 0, (c * 2 + j) * P:(c * 2 + j + 1) * P], s_cols[:, j, :, c], ident)
                pe.wait_ge(new_prod_ok, 1)
                pe.matmul(pair[0:R, 1, 0:2], new_dec[:], blk[:, 0:P:QK], start=True, stop=True).then_inc(s_rows_full, 1)
                pe.wait_ge(a_dec_ok, 1)
                pe.wait_ge(rows_s_taken, 2)
                pe.wait_ge(mix_lo_ok, MIX["attn"] + HEADS)
                for j in range(2):
                    pe.transpose(bank6[:, j * R:(j + 1) * R], a_dec[:, j * PAGE:(j + 1) * PAGE], ident[0:R, 0:R])
                pe.matmul(bank7[:, 0:R], a_dec[:, PAST:PAST + 1].to_broadcast([R, P]), ident[0:R, 0:R],
                          start=True, stop=True).then_inc(a_dec_full, 1)
                for b in range(DEC):
                    pe.wait_ge(v_weighted, b + 1)
                    for j in range(2):
                        for t in range(2):
                            last = pe.matmul(pair[0:DEC, t, :], one_row[:, DEC - 1 - b:2 * DEC - 1 - b],
                                             v_page[b % 4][:, j, t * 512:(t + 1) * 512],
                                             start=b == 0 and j == 0, stop=b == DEC - 1 and j == 1)
                    last.then_inc(vpage_used, 1)
                pe.wait_ge(os_rows_ok, 2)
                for h in range(HEADS):
                    last = pe.transpose(pair[:, 0, h * DEC:(h + 1) * DEC], os_rows[:, h * P:(h + 1) * P], ident[0:DEC, 0:DEC])
                last.then_inc(os_turned, 1)
                pe.wait_ge(os_col_ok, 1)
                pe.transpose(pair[:R, 1, 0:P], os_col[:], ident).then_inc(os_full, 1)
                pe.wait_ge(os_scaled, 1)
                pe.transpose(bank7[:, 0:R], os_tok[:], ident[0:R, 0:R]).then_inc(os_back, 1)
                pe.wait_ge(mix_lo_ok, MIX["attn"] + 1 + HEADS)
                for i in range(KT):
                    unit(At(UNIT["w_o"] + i), At(TILE["w_o"] + i), mix_hi, mix_lo)

            pe.wait_ge(ready0, 3)
            pe.wait_ge(const_in, 16 * N_CONST_LOADS)
            for t, n in enumerate((P, P, 123)):
                batch(t, [(0, vec_rows[0:n, t, :])])
            pe.wait_ge(rows_in, 32)
            batch(3, [(k * DEC, xs_rows[:, k * P:(k + 1) * P]) for k in range(KT)])
            for k in range(KT):
                batch(4 + k, [(b * P, x_rows[:, b, k * P:(k + 1) * P]) for b in range(4)])
            pool(0)
            ffn(0)
            conv_mixer()
            ffn(1)
            attention()
            ffn(2)
            pool(1)
            ffn(3)

        @block.scalar
        def _(act):
            seq = [0]

            def step(ins):
                seq[0] += 1
                ins.then_inc(act_seq, 1)
                act.wait_ge(act_seq, seq[0])

            def split(n, cols=1024):
                act.wait_ge(landed[n.slot(4)], (n.turn(4).v + 1) * 16)
                if n.start >= 2:
                    act.wait_ge(units_done, (n + -1).v)
                act.activation(w_hi[n.slot(2)][:, 0:cols], raw[:, n.slot(4), 0:cols], ACT.Copy).then_inc(split_hi, 1)

            def squares(r, m, c):
                if r or m.start >= 2:
                    act.wait_ge(sq_added, m.v + (8 * r - 1))
                act.activation(sq[:, c % 2, :], tile_of(x, m), ACT.Square).then_inc(sq_ready, 1)

            def updated(r, tile0, m, c, gain):
                act.wait_ge(evacuated, (m + (tile0 + 1)).v)
                squares(r, m, c)
                if gain is not None:
                    g = vec[:, gain + m.start:gain + m.start + 1] if m.i is None else vec[:, bass.ds((m + gain).v, 1)]
                    act.activation(tile_of(xin_hi, m), tile_of(x, m), ACT.Copy, scale=g).then_inc(xin_hi_ok, 1)

            def token_scale(r):
                act.wait_ge(mean_ready, r + 1)
                step(act.activation(halves(lnb[:]), pair[:, :, 0:HALF], ACT.Ln, bias=eps[:]))
                act.activation(rstd[:], lnb[:], ACT.Exp, scale=-0.5).then_inc(rstd_ready, 1)

            def take_batch(b, dst, src):
                act.wait_ge(tp_full, b + 1)
                act.activation(dst, src, ACT.Copy).then_inc(tp_taken, 1)

            def pool(q):
                u, tb, r = UNIT[f"pool{q}"], TP[f"pool{q}"], 6 * q + 1
                token_scale(6 * q)
                for b in range(2):
                    take_batch(tb + b, hist_s[:, 4 * b:4 * b + 4, :, 0:HIST_P],
                               bank[b % 2][:, 0:480].rearrange("p (k b j) -> p k b j", k=4, b=DEC))
                if q:
                    act.wait_ge(stored, 16 * STORED["attn"])
                for b in range(2):
                    take_batch(tb + 2 + b, stage[0:TAIL_P, 512 * b:512 * b + 512], bank[b % 2][0:TAIL_P, :])
                for g in range(5):
                    if g < 4:
                        act.wait_ge(diff_ready, 4 * q + g + 1)
                        act.activation(mix_hi[:, 2 * g:2 * g + 2, :], diff[:, g % 2], ACT.Copy).then_inc(mix_hi_ok, 1)
                    for m in (2 * g - 2, 2 * g - 1) if g else ():
                        if m % 4 == 3:
                            split(At(u + 2 + m // 4))
                        updated(r, TILE[f"pool{q}"], At(m), m, V_FFN + 8 * (3 * q))

            def ffn(layer):
                u, m0, r = UNIT[f"ffn{layer}"], TILE[f"ffn{layer}"], 2 * layer + 1
                token_scale(r)
                if layer == 2:
                    act.wait_ge(stored, 16 * STORED["attn"])
                with act.Fori(0, FT // 2) as i:
                    for c in range(2):
                        n, m, f = At(u + 2 * c, 4, i), At(m0 + 2 * c, 4, i), At(c, 2, i)
                        split(n + 2)
                        act.wait_ge(evacuated, (m + 1).v)
                        act.activation(sg_buf[:, c, :], g_buf[:, c, :], ACT.Silu).then_inc(sg_ready, 1)
                        split(n + 3)
                        act.wait_ge(h_ready, (f + (FT * layer + 1)).v)
                        act.activation(tile_of(h_hi, f), h_buf[:, c, :], ACT.Copy).then_inc(h_hi_ok, 1)
                gain = {0: V_MIX + 8, 1: V_MIX + 16, 2: None, 3: None}[layer]

                def down(i):
                    for c in range(4):
                        n, m = at(u + 2 * FT + 3 * c, 12, i), at(c, 4, i)
                        split(n + 2, 768)
                        for j in (3, 4):
                            if n.i is not None or n.start + j < UNITS:
                                split(n + j)
                        if layer < 3:
                            updated(r + 1, m0 + 2 * FT, m, c, gain)
                        else:
                            for t in (c - 1, c)[c == 0:1 + (c == 3)]:
                                col = m.start - c + t
                                tb = TP["end"] + 2 * col
                                take_batch(tb, y_sb[:, col, 0:SEQ], bank6[:, :])
                                take_batch(tb + 1, y_sb[0:DEC, col, SEQ:SEQ + P], bank7[0:DEC, 0:P])
                if layer < 3:
                    with act.Fori(0, 2) as i:
                        down(i)
                else:
                    for i in range(2):
                        down(i)

            def conv_mixer():
                u, m0 = UNIT["conv_in"], TILE["conv_in"]
                token_scale(2)

                def tap(w, i):
                    return vec[:, V_DW + w * KT + i:V_DW + w * KT + i + 1]

                def products(f0, f1):
                    for f in range(f0, min(f1, TAPS * len(POOL_TILES))):
                        t, w = divmod(f, TAPS)
                        i = POOL_TILES[t]
                        if w == 0:
                            act.wait_ge(glu_ready, i + 1)
                            act.activation(conv[:, i, 0:SEQ], glu[:, i, 0:SEQ], ACT.Identity, scale=tap(0, i),
                                           bias=vec[:, V_DWB + i:V_DWB + i + 1]).then_inc(prod_ready, 1)
                        else:
                            p = (TAPS - 1) * t + w - 1
                            if p >= 3:
                                act.wait_ge(prod_added, p - 2)
                            act.activation(prod_p[:, p % 3, :], glu[:, i, w:w + SEQ], ACT.Copy, scale=tap(w, i)).then_inc(prod_ready, 1)

                for i in range(KT):
                    n = At(u + 2 * i)
                    split(n + 2)
                    if i:
                        products(8 * i - 4, 8 * i)
                    split(n + 3)
                    act.wait_ge(evacuated, m0 + 2 * i + 2)
                    if i >= 2:
                        act.wait_ge(glu_ready, i - 1)
                    act.activation(gate_s[:, i % 2, :], act_in[:, 1, :], ACT.Sigmoid,
                                   bias=vec[:, V_BIN + KT + i:V_BIN + KT + i + 1]).then_inc(gate_ready, 1)
                    if i == 1:
                        for b in range(4):
                            take_batch(TP["conv"] + b, hist_c[:, 2 * b:2 * b + 2, :, 0:HIST_C],
                                       bank[b % 2][:, 0:480].rearrange("p (k b j) -> p k b j", k=2, b=DEC))
                    products(8 * i, 8 * i + 4)
                act.wait_ge(stored, 16 * STORED["pool0"])
                for b in range(2):
                    take_batch(TP["conv"] + 4 + b, stage[0:TAIL_C, 512 * b:512 * b + 512], bank[b % 2][0:TAIL_C, :])
                for w in range(TAPS):
                    if w >= 4:
                        act.wait_ge(diag_used, w - 3)
                    act.activation(diag[:, w % 4, :], ident, ACT.Copy, scale=tap(w, PE_TILE)).then_inc(diag_ready, 1)
                    products(8 * KT - 4 + w, 8 * KT - 3 + w)
                products(8 * KT - 4 + TAPS, TAPS * len(POOL_TILES))
                act.wait_ge(diag_used, TAPS)
                act.activation(conv[:, PE_TILE, 0:SEQ], pair[:, 0, :], ACT.Identity,
                               bias=vec[:, V_DWB + PE_TILE:V_DWB + PE_TILE + 1]).then_inc(conv_pe_ready, 1)
                for k in range(KT):
                    act.wait_ge(cent, k + 1)
                    act.activation(glu[:, k, 0:T], conv[:, k, :], ACT.Square).then_inc(csq, 1)
                act.wait_ge(cvar, 1)
                step(act.activation(halves(lnb[:]), pair[:, :, 0:HALF], ACT.Ln, bias=eps[:]))
                act.activation(sq[:, 0, :], lnb[:], ACT.Exp, scale=-0.5).then_inc(crstd, 1)
                for k in range(KT):
                    act.wait_ge(cnorm, k + 1)
                    act.activation(conv[:, k, :], glu[:, k, 0:T], ACT.Silu, scale=vec[:, V_LNG + k:V_LNG + k + 1],
                                   bias=vec[:, V_LNB + k:V_LNB + k + 1]).then_inc(cact, 1)
                    act.wait_ge(cact, k + 1)
                    act.activation(mix_hi[:, k, :], conv[:, k, :], ACT.Copy).then_inc(mix_hi_ok, 1)
                for i in range(KT):
                    split(At(UNIT["conv_out"] + i + 2))
                    updated(3, TILE["conv_out"], At(i), i, V_FFN + 8)

            def attention():
                u, m0 = UNIT["qkv"], TILE["qkv"]
                token_scale(4)

                def norm(i, dst):
                    act.wait_ge(nrm_ready, i + 1)
                    act.activation(halves(dst[:]), pair[:, :, 0:HALF], ACT.Ln, bias=eps[:]).then_inc(nrm_ln, 1)
                    act.wait_ge(nrm_ln, i + 1)
                    act.activation(dst[:], dst[:], ACT.Exp, scale=-0.5).then_inc(nrm_exp, 1)

                def square(i, src, m):
                    act.wait_ge(evacuated, m + 1)
                    if i:
                        act.wait_ge(nrm_ready, i)
                    act.activation(sq[:, 0, :], src[:], ACT.Square).then_inc(nsq_ready, 1)

                def exps(g, piece):
                    act.wait_ge(max_ready, 3 * g + piece + 1)
                    for off, i in PIECES[piece]:
                        for c in range(2):
                            w, j = (i + 1) * P, i % 2
                            ins = act.activation(s_buf[:, c, off:off + w], s_buf[:, c, off:off + w], ACT.Exp,
                                                 bias=row_max[:, c, j:j + 1], scale=SCALE, accum_out=row_sum[:, c, j:j + 1])
                    ins.then_inc(exp_done, 1)

                def take_weights(g, piece):
                    act.wait_ge(at_ready, 3 * g + piece + 1)
                    if g or piece:
                        act.wait_ge(pv_done, 3 * g + piece)
                    w = (384, 384, 512)[piece]
                    act.activation(aT[:, 0:w], bank6[:, 0:w], ACT.Copy).then_inc(at_taken, 1)

                for h in range(HEADS + 2):
                    n = At(u + 3 * h)
                    g = h - 1
                    if h < HEADS:
                        split(n + 2)
                    if 1 <= h <= HEADS:
                        act.wait_ge(t_ready, g + 1)
                        if g >= 2:
                            act.wait_ge(rows_stored[g % 2], 32 * (g // 2))
                        for j, to in enumerate((k_tok, v_tok)):
                            act.activation(to[:, g % 2], pair[:, j, :].rearrange("p (b c) -> p b c", b=4), ACT.Copy).then_inc(t_taken, 1)
                    if h < HEADS:
                        square(2 * h, q_raw, m0 + 3 * h)
                    if h >= 2:
                        take_weights(h - 2, 2)
                    if 1 <= h <= HEADS:
                        exps(g, 0)
                    if h < HEADS:
                        split(n + 3)
                        norm(2 * h, ln_q)
                        square(2 * h + 1, k_raw, m0 + 3 * h + 1)
                    if h >= 2:
                        act.wait_ge(o_taken, h - 1)
                        if h > 2:
                            act.wait_ge(oss_done, h - 2)
                        act.activation(o_sq[:].rearrange("p (b c) -> p b c", b=4), o_tok[:, :, h - 2, :], ACT.Square).then_inc(osq_done, 1)
                    if 1 <= h <= HEADS:
                        take_weights(g, 0)
                        exps(g, 1)
                    if h < HEADS:
                        split(n + 4)
                        norm(2 * h + 1, ln_k)
                    if 1 <= h <= HEADS:
                        take_weights(g, 1)
                        exps(g, 2)

                act.wait_ge(rows_s_full, 1)
                for j in range(2):
                    act.wait_ge(rows_stored[j], 16 * HEADS)
                act.activation(ks_rows_sb[:], bank7[0:R, 0:P], ACT.Copy).then_inc(rows_s_taken, 1)
                act.activation(vs_rows_sb[:], bank7[0:R, P:2 * P], ACT.Copy).then_inc(rows_s_taken, 1)
                act.wait_ge(roots_in, 1)
                act.activation(o_tmp[:, 0:2, :], o_tmp[:, 0:2, :], ACT.Sqrt).then_inc(roots_ok, 1)
                for h in range(HEADS):
                    act.wait_ge(o_back, h + 1)
                    act.activation(mix_hi[:, h, 0:SEQ], bank6[:, :], ACT.Copy, scale=sub_gain[:]).then_inc(mix_hi_ok, 1)
                act.wait_ge(dec_max_ok, 1)
                for c in range(2):
                    ins = act.activation(s_dec[:, c, :], s_dec[:, c, :], ACT.Exp, bias=m_dec[:, 2 + c:3 + c], scale=SCALE,
                                         accum_out=m_dec[:, 4 + c:5 + c])
                ins.then_inc(dec_exp_ok, 1)
                act.wait_ge(a_dec_full, 1)
                act.activation(aT_dec[:].rearrange("p j r -> p (j r)"), bank6[:, 0:2 * R], ACT.Copy).then_inc(aT_dec_ok, 1)
                act.wait_ge(vpage_used, DEC)
                act.activation(os_rows[:, 0:512], pair[0:DEC, 0, :], ACT.Copy).then_inc(os_rows_ok, 1)
                act.wait_ge(os_in_ok, 1)
                act.activation(os_sq[:], os_tok[:], ACT.Square, accum_out=m_dec[:, 8:9]).then_inc(os_sq_ok, 1)
                act.wait_ge(roots_in, 2)
                act.activation(m_dec[:, 9:11], m_dec[:, 9:11], ACT.Sqrt).then_inc(roots_ok, 1)
                act.wait_ge(os_back, 1)
                act.activation(mix_hi[:, :, SEQ:T], bank7[:, 0:R].rearrange("p (h b) -> p h b", h=HEADS), ACT.Copy,
                               scale=sub_gain[:]).then_inc(mix_hi_ok, 1)
                for i in range(KT):
                    split(At(UNIT["w_o"] + i + 2))
                    updated(5, TILE["w_o"], At(i), i, V_FFN + 16)

            split(At(0))
            split(At(1))
            for t, n in enumerate((P, P, 123)):
                take_batch(t, vec[:, t * P:t * P + n], bank[t % 2][:, 0:n])
            take_batch(3, x[:, :, SEQ:T], bank7[:, 0:KT * DEC].rearrange("p (k b) -> p k b", k=KT))
            for k in range(KT):
                take_batch(4 + k, x[:, k, 0:SEQ], bank[k % 2][:, :])
                act.wait_ge(tp_taken, 5 + k)
                squares(0, At(k), k)
            act.wait_ge(lam_sums, 2)
            act.activation(lam_tmp[:, QK:QK + 2], lam_tmp[:, QK:QK + 2], ACT.Exp).then_inc(lam_exps, 1)
            pool(0)
            ffn(0)
            conv_mixer()
            ffn(1)
            attention()
            ffn(2)
            pool(1)
            ffn(3)

        @block.vector
        def _(dve):
            seq = [0]

            def step(ins):
                seq[0] += 1
                ins.then_inc(dve_seq, 1)
                dve.wait_ge(dve_seq, seq[0])

            def split(n, cols=1024):
                dve.wait_ge(split_hi, (n + 1).v)
                if n.start >= 2:
                    dve.wait_ge(units_done, (n + -1).v)
                dve.tensor_tensor(w_lo[n.slot(2)][:, 0:cols], raw[:, n.slot(4), 0:cols],
                                  w_hi[n.slot(2)][:, 0:cols].bitcast(F32), ALU.subtract).then_inc(split_lo, 1)

            def accumulator(m):
                b = 2 * m.slot(2)
                return acc[:, b:b + 2, 0:HALF]

            def next_low(xi, m, gain):
                dve.wait_ge(xin_hi_ok, m.v + (8 * xi + 1))
                g = vec[:, gain + m.start:gain + m.start + 1] if m.i is None else vec[:, bass.ds((m + gain).v, 1)]
                dve.scalar_tensor_tensor(tile_of(xin_lo, m), tile_of(x, m), g, tile_of(xin_hi, m).bitcast(F32),
                                         ALU.mult, ALU.subtract).then_inc(xin_lo_ok, 1)

            def pool(q):
                u, m0, l = UNIT[f"pool{q}"], TILE[f"pool{q}"], 3 * q
                gain = V_MIX + 8 * l
                dve.wait_ge(rstd_ready, 6 * q + 1)
                dve.memset(hn[:, :, 0:16], 0.0)
                step(dve.memset(wsum[:, :, :, 0:16], 0.0))
                for k in range(KT):
                    dve.scalar_tensor_tensor(hn[:, k, 16:16 + T], x[:, k, :], vec[:, gain + k:gain + k + 1], rstd[:],
                                             ALU.mult, ALU.mult).then_inc(hn_ready, 1)
                dve.wait_ge(hn_ready, 8 * q + KT)

                def difference(g):
                    win = WINDOWS[g]
                    here = slice(2 * g, 2 * g + 2)
                    cur = hn[:, here, :]
                    for lev in range(g + 1):
                        to = wsum[:, lev % 2]
                        step(dve.tensor_tensor(to[:, :, 16:16 + SEQ], cur[:, :, 16:16 + SEQ],
                                               cur[:, :, 16 - (1 << lev):16 + SEQ - (1 << lev)], ALU.add))
                        cur = to
                    out = diff[:, g % 2]
                    if g >= 2:
                        dve.wait_ge(mix_lo_ok, MIX[f"pool{q}"] + g - 1)
                    step(dve.scalar_tensor_tensor(out[:, :, 0:SEQ], cur[:, :, 16:16 + SEQ], 1.0 / win,
                                                  hn[:, here, 16:16 + SEQ], ALU.mult, ALU.subtract))
                    inv = const[:, C_CNT + 16 * g:C_CNT + 16 * g + 16].unsqueeze(1).to_broadcast([P, 2, 16])
                    step(dve.tensor_tensor(edge[:], cur[:, :, 16:32], inv, ALU.mult))
                    dve.tensor_tensor(out[:, :, 0:16], edge[:], hn[:, here, 16:32], ALU.subtract)
                    dve.wait_ge(tp_taken, TP[f"pool{q}"] + 2)
                    step(dve.tensor_copy(hist_s[:, here, :, HIST_P], hn[:, here, 16 + SEQ:16 + T]))
                    step(dve.tensor_reduce(last_s[:], hist_s[:, here, :, 16 - win:16], AX.X, ALU.add))
                    dve.scalar_tensor_tensor(out[:, :, SEQ:T], last_s[:], 1.0 / win, hn[:, here, 16 + SEQ:16 + T],
                                             ALU.mult, ALU.subtract).then_inc(diff_ready, 1)

                def low(g):
                    dve.wait_ge(mix_hi_ok, MIX[f"pool{q}"] + g + 1)
                    dve.wait_ge(diff_ready, 4 * q + g + 1)
                    dve.tensor_tensor(mix_lo[:, 2 * g:2 * g + 2, :], diff[:, g % 2], mix_hi[:, 2 * g:2 * g + 2, :].bitcast(F32),
                                      ALU.subtract).then_inc(mix_lo_ok, 1)

                def update(m):
                    if m % 4 == 3:
                        dve.wait_ge(units_done, u + m // 4 + 1)
                    else:
                        dve.wait_ge(tile_done, 6 * q + 3 * (m // 4) + m % 4 + 1)
                    s = V_PSCALE + 8 * q + m
                    dve.scalar_tensor_tensor(halves(x[:, m, :]), accumulator(At(m0 + m)), vec[:, s:s + 1], halves(x[:, m, :]),
                                             ALU.mult, ALU.add).then_inc(evacuated, 1)
                    if m % 4 == 3:
                        split(At(u + 2 + m // 4))
                    next_low(XIN[6 * q + 1], At(m), V_FFN + 8 * l)

                difference(0)
                low(0)
                for g in range(1, 4):
                    difference(g)
                    low(g)
                    update(2 * g - 2)
                    update(2 * g - 1)
                update(6)
                update(7)

            def ffn(layer):
                u, m0, r = UNIT[f"ffn{layer}"], TILE[f"ffn{layer}"], 2 * layer + 1
                dve.wait_ge(rstd_ready, r + 1)
                if layer == 2:
                    dve.wait_ge(stored, 16 * STORED["attn"])
                with dve.Fori(0, FT // 2) as i:
                    for c in range(2):
                        n, m, f = At(u + 2 * c, 4, i), At(m0 + 2 * c, 4, i), At(c, 2, i)
                        dve.wait_ge(units_done, (n + 1).v)
                        dve.tensor_tensor(halves(g_buf[:, c, :]), accumulator(m), halves(rstd[:]), ALU.mult).then_inc(evacuated, 1)
                        split(n + 2)
                        dve.wait_ge(units_done, (n + 2).v)
                        dve.tensor_tensor(halves(u_buf[:]), accumulator(m + 1), halves(rstd[:]), ALU.mult).then_inc(evacuated, 1)
                        dve.wait_ge(sg_ready, (f + (FT * layer + 1)).v)
                        dve.wait_ge(evacuated, (m + 2).v)
                        dve.tensor_tensor(h_buf[:, c, :], u_buf[:], sg_buf[:, c, :], ALU.mult).then_inc(h_ready, 1)
                        split(n + 3)
                        dve.wait_ge(h_hi_ok, (f + (FT * layer + 1)).v)
                        dve.tensor_tensor(tile_of(h_lo, f), h_buf[:, c, :], tile_of(h_hi, f).bitcast(F32), ALU.subtract)\
                           .then_inc(h_lo_ok, 1)
                gain = {0: V_MIX + 8, 1: V_MIX + 16, 2: None, 3: None}[layer]

                def down(i):
                    for c in range(4):
                        n, m = at(u + 2 * FT + 3 * c, 12, i), at(c, 4, i)
                        split(n + 2, 768)
                        if n.i is not None or n.start + 3 < UNITS:
                            split(n + 3)
                        dve.wait_ge(units_done, (n + 3).v)
                        out = tile_of(x, m) if layer < 3 else x_out[:, c, :]
                        dve.tensor_tensor(halves(out), accumulator(At(c)), halves(tile_of(x, m)), ALU.add)\
                           .then_inc(evacuated, 1)
                        if n.i is not None or n.start + 4 < UNITS:
                            split(n + 4)
                        if gain is not None:
                            next_low(XIN[r + 1], m, gain)
                if layer < 3:
                    with dve.Fori(0, 2) as i:
                        down(i)
                else:
                    for i in range(2):
                        down(i)

            def conv_mixer():
                u, m0 = UNIT["conv_in"], TILE["conv_in"]
                dve.wait_ge(rstd_ready, 3)
                step(dve.memset(glu[:, :, 0:HIST_C], 0.0))

                def taps(f0, f1):
                    for f in range(f0, f1):
                        t, w = divmod(f, TAPS)
                        i = DVE_TILES[t]
                        tap = vec[:, V_DW + w * KT + i:V_DW + w * KT + i + 1]
                        out = conv[:, i, 0:SEQ]
                        if w == 0:
                            ins = dve.tensor_scalar(out, glu[:, i, 0:SEQ], tap, vec[:, V_DWB + i:V_DWB + i + 1], ALU.mult, ALU.add)
                        else:
                            ins = dve.scalar_tensor_tensor(out, glu[:, i, w:w + SEQ], tap, out, ALU.mult, ALU.add)
                        if w < TAPS - 1:
                            step(ins)
                        else:
                            ins.then_inc(conv_dve_ready, 1)

                def samples(half):
                    k = slice(4 * half, 4 * half + 4)
                    step(dve.tensor_copy(hist_c[:, k, :, HIST_C], glu[:, k, HIST_C + SEQ:HIST_C + T]))
                    w = vec[:, V_DW:V_DW + TAPS * KT].rearrange("p (w k) -> p k w", k=KT)[:, k].unsqueeze(2)\
                        .to_broadcast([P, KT // 2, DEC, TAPS])
                    step(dve.tensor_tensor(prod_s[:], hist_c[:, k], w, ALU.mult))
                    step(dve.tensor_reduce(conv[:, k, SEQ:T], prod_s[:], AX.X, ALU.add))
                    b = vec[:, V_DWB + 4 * half:V_DWB + 4 * half + 4].unsqueeze(2).to_broadcast([P, KT // 2, DEC])
                    dve.tensor_tensor(conv[:, k, SEQ:T], conv[:, k, SEQ:T], b, ALU.add).then_inc(conv_s_ready, 1)

                for i in range(KT):
                    n = At(u + 2 * i)
                    dve.wait_ge(units_done, (n + 1).v)
                    if i:
                        dve.wait_ge(glu_ready, i)
                    dve.tensor_tensor(halves(act_in[:, 0, :]), accumulator(At(0)), halves(rstd[:]), ALU.mult).then_inc(evacuated, 1)
                    split(n + 2)
                    if i >= 2:
                        taps(10 * i - 15, 10 * i - 10)
                    dve.wait_ge(units_done, (n + 2).v)
                    dve.tensor_tensor(halves(act_in[:, 1, :]), accumulator(At(1)), halves(rstd[:]), ALU.mult).then_inc(evacuated, 1)
                    split(n + 3)
                    dve.wait_ge(gate_ready, i + 1)
                    dve.wait_ge(evacuated, m0 + 2 * i + 1)
                    dve.scalar_tensor_tensor(glu[:, i, HIST_C:HIST_C + T], act_in[:, 0, :], vec[:, V_BIN + i:V_BIN + i + 1],
                                             gate_s[:, i % 2, :], ALU.add, ALU.mult).then_inc(glu_ready, 1)
                    if i >= 1:
                        if i == 1 or 10 * i - 10 == TAPS:
                            dve.wait_ge(glu_ready, i + 1)
                        taps(10 * i - 10, 10 * i - 5)
                    if i == 3:
                        dve.wait_ge(tp_taken, TP["conv"] + 4)
                        dve.wait_ge(glu_ready, 4)
                        samples(0)
                dve.wait_ge(glu_ready, KT)
                samples(1)
                taps(10 * KT - 15, TAPS * len(DVE_TILES))
                dve.wait_ge(cmean, 1)
                for k in range(KT):
                    dve.tensor_tensor(halves(conv[:, k, :]), halves(conv[:, k, :]), pair[:, :, 0:HALF], ALU.subtract).then_inc(cent, 1)
                dve.wait_ge(crstd, 1)
                for j in range(KT + 2):
                    if j < KT:
                        dve.tensor_tensor(glu[:, j, 0:T], conv[:, j, :], sq[:, 0, :], ALU.mult).then_inc(cnorm, 1)
                    if j >= 2:
                        k = j - 2
                        dve.wait_ge(mix_hi_ok, MIX["conv"] + k + 1)
                        dve.tensor_tensor(mix_lo[:, k, :], conv[:, k, :], mix_hi[:, k, :].bitcast(F32), ALU.subtract).then_inc(mix_lo_ok, 1)
                u = UNIT["conv_out"]
                for i in range(KT):
                    dve.wait_ge(units_done, u + i + 1)
                    dve.scalar_tensor_tensor(halves(x[:, i, :]), accumulator(At(i)), vec[:, V_BOUT + i:V_BOUT + i + 1],
                                             halves(x[:, i, :]), ALU.add, ALU.add).then_inc(evacuated, 1)
                    split(At(u + i + 2))
                    next_low(XIN[3], At(i), V_FFN + 8)

            def attention():
                u, m0 = UNIT["qkv"], TILE["qkv"]
                dve.wait_ge(rstd_ready, 5)

                def project(h, j, dst):
                    n = At(u + 3 * h + j)
                    dve.wait_ge(units_done, (n + 1).v)
                    if h:
                        if j < 2:
                            dve.wait_ge(qkn_ready, 2 * h)
                        else:
                            dve.wait_ge(t_ready, h)
                            dve.wait_ge(saved_s, 3 * h)
                    dve.tensor_tensor(halves(dst[:]), accumulator(At(m0 + 3 * h + j)), halves(rstd[:]), ALU.mult).then_inc(evacuated, 1)
                    split(n + 2)

                def maxima(g, piece):
                    dve.wait_ge(qk_ready, 3 * g + piece + 1)
                    dve.wait_ge(bias_ready, g + 1)
                    if g or piece:
                        dve.wait_ge(a_ready, 3 * g + piece)
                    for off, i in PIECES[piece]:
                        for c in range(2):
                            w, j = (i + 1) * P, i % 2
                            last = dve.tensor_tensor_reduce(
                                out=s_buf[:, c, off:off + w], in0=pair[:, c, off:off + w], in1=bias_h[:, g % 2, SEQ - w:SEQ],
                                scale=1.0, scalar=-3e38, op0=ALU.add, op1=ALU.max, accum_out=row_scl[:, c, j:j + 1])
                    last.then_inc(s_taken, 1)
                    dve.wait_ge(s_taken, 3 * g + piece + 1)
                    dve.tensor_scalar(row_max[:], row_scl[:], -SCALE, None, ALU.mult).then_inc(max_ready, 1)

                def weights(g, piece):
                    dve.wait_ge(exp_done, 3 * g + piece + 1)
                    step(dve.reciprocal(row_inv[:], row_sum[:]))
                    step(dve.tensor_scalar(row_inv[:, 1, :], row_inv[:, 1, :], neg_lam[:], None, ALU.mult))
                    if g or piece:
                        dve.wait_ge(at_ready, 3 * g + piece)
                    for off, i in PIECES[piece]:
                        w, j = (i + 1) * P, i % 2
                        dve.tensor_scalar(t_buf[:, off:off + w], s_buf[:, 1, off:off + w], row_inv[:, 1, j:j + 1], None, ALU.mult)\
                           .then_inc(dve_seq, 1)
                        seq[0] += 1
                    for off, i in PIECES[piece]:
                        w, j = (i + 1) * P, i % 2
                        dve.wait_ge(dve_seq, seq[0])
                        last = dve.scalar_tensor_tensor(a_buf[:, off:off + w], s_buf[:, 0, off:off + w], row_inv[:, 0, j:j + 1],
                                                        t_buf[:, off:off + w], ALU.mult, ALU.add)
                    last.then_inc(a_ready, 1)

                def take_output(g):
                    dve.wait_ge(pv_done, 3 * g + 3)
                    rows = bank7[:, :].rearrange("p (b c) -> p b c", b=4)
                    step(dve.tensor_reduce(o_max[:, :, g], rows, AX.X, ALU.max, apply_absolute_value=True))
                    step(dve.tensor_scalar(o_max[:, :, g], o_max[:, :, g], 1e-15, 1e37, ALU.max, ALU.min))
                    step(dve.reciprocal(o_inv[:, :, g], o_max[:, :, g]))
                    dve.tensor_tensor(o_tok[:, :, g, :], rows, o_inv[:, :, g:g + 1].to_broadcast([P, 4, P]), ALU.mult)\
                       .then_inc(o_taken, 1)
                    dve.wait_ge(osq_done, g + 1)
                    dve.tensor_reduce(o_ss[:, :, g], o_sq[:].rearrange("p (b c) -> p b c", b=4), AX.X, ALU.add)\
                       .then_inc(oss_done, 1)

                for h in range(HEADS + 2):
                    if h < HEADS:
                        project(h, 0, q_raw)
                    if 1 <= h <= HEADS:
                        maxima(h - 1, 0)
                        weights(h - 1, 0)
                    if h < HEADS:
                        project(h, 1, k_raw)
                    if h >= 2:
                        take_output(h - 2)
                    if 1 <= h <= HEADS:
                        maxima(h - 1, 1)
                        weights(h - 1, 1)
                    if h < HEADS:
                        project(h, 2, v_raw)
                    if 1 <= h <= HEADS:
                        maxima(h - 1, 2)
                    if h < HEADS:
                        for j, (src, ln, gain, dst) in enumerate(((q_raw, ln_q, V_QN, qn), (k_raw, ln_k, V_KN, kn))):
                            dve.wait_ge(nrm_exp, 2 * h + j + 1)
                            if h:
                                dve.wait_ge(saved_s, 3 * h)
                            dve.scalar_tensor_tensor(dst[:], src[:], vec[:, gain:gain + 1], ln[:], ALU.mult, ALU.mult)\
                               .then_inc(qkn_ready, 1)
                    if 1 <= h <= HEADS:
                        weights(h - 1, 2)

                def radicands(mean_out, sum_out, ss, inv):
                    step(dve.tensor_tensor(mean_out, inv, inv, ALU.mult))
                    step(dve.tensor_scalar(mean_out, mean_out, EPS, None, ALU.mult))
                    step(dve.scalar_tensor_tensor(mean_out, ss, 1.0 / P, mean_out, ALU.mult, ALU.add))
                    step(dve.tensor_copy(sum_out, ss))

                def factors(out, mean_root, sum_root, largest):
                    step(dve.scalar_tensor_tensor(sum_root, largest, 2.0 ** -64, sum_root, ALU.mult, ALU.mult))
                    step(dve.tensor_scalar(sum_root, sum_root, 1.0, None, ALU.is_lt))
                    step(dve.reciprocal(out, mean_root))
                    step(dve.tensor_tensor(out, out, sum_root, ALU.mult))

                flat = "p b h -> p (b h)"
                dve.wait_ge(oss_done, HEADS)
                radicands(o_tmp[:, 0, :], o_tmp[:, 1, :], o_ss[:].rearrange(flat), o_inv[:].rearrange(flat))
                dve.memset(row_inv[:, 0, 0:1], 0.0).then_inc(roots_in, 1)
                dve.wait_ge(saved_s, 3 * HEADS)
                dve.tensor_tensor(new_dec[:], qs[:].rearrange("p h b -> p (h b)"), ks[:].rearrange("p h b -> p (h b)"), ALU.mult)\
                   .then_inc(new_prod_ok, 1)

                def head_low(h):
                    dve.wait_ge(mix_hi_ok, MIX["attn"] + 1 + h)
                    dve.scalar_tensor_tensor(mix_lo[:, h, 0:SEQ], bank6[:, :], sub_gain[:], mix_hi[:, h, 0:SEQ].bitcast(F32),
                                             ALU.mult, ALU.subtract).then_inc(mix_lo_ok, 1)

                for b in range(DEC):
                    dve.wait_ge(q_all_ready, b + 1)
                    dve.wait_ge(kpage_in[b % 3], 32 * (b // 3 + 1))
                    if b:
                        dve.wait_ge(s_cols_ok, b)
                    q_all = acc[:, 2 * (b % 2):2 * (b % 2) + 2, :].unsqueeze(1).to_broadcast([P, 2, 2, D // 2])
                    dve.tensor_tensor(k_prod[:], k_page[b % 3][:].rearrange("p j (t c) -> p j t c", t=2), q_all, ALU.mult)\
                       .then_inc(kpage_used, 1)
                    if b == 0:
                        dve.wait_ge(roots_ok, 1)
                        factors(o_tmp[:, 2, :], o_tmp[:, 0, :], o_tmp[:, 1, :], o_max[:].rearrange(flat))
                        dve.memset(row_inv[:, 0, 0:1], 0.0).then_inc(factors_ok, 1)
                    dve.wait_ge(kpage_used, b + 1)
                    dve.tensor_reduce(s_cols[:].rearrange("p j (h b) c -> p (j h) b c", b=DEC)[:, :, b, :],
                                      k_prod[:].rearrange("p j t (g c d) -> p (j t g) c d", c=2, d=QK), AX.X, ALU.add)\
                       .then_inc(s_cols_ok, 1)
                    if b >= 2:
                        head_low(b - 2)
                head_low(HEADS - 2)
                head_low(HEADS - 1)
                dve.wait_ge(s_rows_full, 1)
                dve.tensor_tensor(s_dec[:, :, 0:PAST], pair[0:R, 0, :].rearrange("p (c k) -> p c k", c=2),
                                  const[0:R, C_POS:C_POS + PAST].unsqueeze(1).to_broadcast([R, 2, PAST]), ALU.add)
                step(dve.tensor_scalar(s_dec[:, :, PAST], pair[0:R, 1, 0:2], float(QK), None, ALU.mult))
                step(dve.tensor_reduce(m_dec[:, 0:2], s_dec[:], AX.X, ALU.max))
                dve.tensor_scalar(m_dec[:, 2:4], m_dec[:, 0:2], -SCALE, None, ALU.mult).then_inc(dec_max_ok, 1)
                dve.wait_ge(dec_exp_ok, 1)
                step(dve.reciprocal(m_dec[:, 6:8], m_dec[:, 4:6]))
                step(dve.tensor_scalar(m_dec[:, 7:8], m_dec[:, 7:8], neg_lam[0:R, :], None, ALU.mult))
                step(dve.tensor_scalar(t_dec[:], s_dec[:, 1, :], m_dec[:, 7:8], None, ALU.mult))
                dve.scalar_tensor_tensor(a_dec[:], s_dec[:, 0, :], m_dec[:, 6:7], t_dec[:], ALU.mult, ALU.add).then_inc(a_dec_ok, 1)
                dve.wait_ge(a_dec_full, 1)
                step(dve.tensor_tensor(new_dec[:], bank7[:, 0:R], vs[:].rearrange("p h b -> p (h b)"), ALU.mult))
                dve.wait_ge(aT_dec_ok, 1)
                for b in range(DEC):
                    dve.wait_ge(vpage_in[b % 4], 32 * (b // 4 + 1))
                    a = aT_dec[:].rearrange("p j (h b) -> p (j h) b", b=DEC)[:, :, b:b + 1].to_broadcast([P, 2 * HEADS, P])
                    v = v_page[b % 4][:].rearrange("p j (h d) -> p (j h) d", d=P)
                    dve.tensor_tensor(v, v, a, ALU.mult).then_inc(v_weighted, 1)
                dve.wait_ge(vpage_used, DEC)
                dve.tensor_copy(os_rows[:, 512:D], pair[0:DEC, 1, :]).then_inc(os_rows_ok, 1)
                dve.wait_ge(os_turned, 1)
                dve.tensor_tensor(os_col[:], pair[:, 0, 0:R], new_dec[:], ALU.add).then_inc(os_col_ok, 1)
                dve.wait_ge(os_full, 1)
                step(dve.tensor_reduce(m_dec[:, 11:12], pair[0:R, 1, 0:P], AX.X, ALU.max, apply_absolute_value=True))
                step(dve.tensor_scalar(m_dec[:, 11:12], m_dec[:, 11:12], 1e-15, 1e37, ALU.max, ALU.min))
                step(dve.reciprocal(m_dec[:, 12:13], m_dec[:, 11:12]))
                dve.tensor_scalar(os_tok[:], pair[0:R, 1, 0:P], m_dec[:, 12:13], None, ALU.mult).then_inc(os_in_ok, 1)

                dve.wait_ge(os_sq_ok, 1)
                radicands(m_dec[:, 9:10], m_dec[:, 10:11], m_dec[:, 8:9], m_dec[:, 12:13])
                dve.memset(row_inv[:, 0, 0:1], 0.0).then_inc(roots_in, 1)
                dve.wait_ge(roots_ok, 2)
                factors(m_dec[:, 13:14], m_dec[:, 9:10], m_dec[:, 10:11], m_dec[:, 11:12])
                dve.tensor_scalar(os_tok[:], os_tok[:], m_dec[:, 13:14], None, ALU.mult).then_inc(os_scaled, 1)
                dve.wait_ge(mix_hi_ok, MIX["attn"] + HEADS + 1)
                dve.scalar_tensor_tensor(mix_lo[:, :, SEQ:T], bank7[:, 0:R].rearrange("p (h b) -> p h b", h=HEADS), sub_gain[:],
                                         mix_hi[:, :, SEQ:T].bitcast(F32), ALU.mult, ALU.subtract).then_inc(mix_lo_ok, 1)
                u = UNIT["w_o"]
                for i in range(KT):
                    dve.wait_ge(units_done, u + i + 1)
                    dve.tensor_tensor(halves(x[:, i, :]), accumulator(At(i)), halves(x[:, i, :]), ALU.add).then_inc(evacuated, 1)
                    split(At(u + i + 2))
                    next_low(XIN[5], At(i), V_FFN + 16)

            split(At(0))
            split(At(1))
            dve.wait_ge(lam_in, 64)
            for j in range(2):
                dve.tensor_tensor_reduce(out=lam_tmp[:, 0:QK], in0=lam_rows[:, 2 * j, :], in1=lam_rows[:, 2 * j + 1, :],
                                         scale=1.0, scalar=0.0, op0=ALU.mult, op1=ALU.add,
                                         accum_out=lam_tmp[:, QK + j:QK + j + 1]).then_inc(lam_sums, 1)
                dve.wait_ge(lam_sums, j + 1)
            dve.wait_ge(lam_exps, 1)
            step(dve.tensor_tensor(neg_lam[:], lam_tmp[:, QK + 1:QK + 2], lam_tmp[:, QK:QK + 1], ALU.subtract))
            step(dve.tensor_scalar(neg_lam[:], neg_lam[:], -LAMBDA_INIT, None, ALU.add))
            dve.wait_ge(tp_taken, 3)
            step(dve.tensor_scalar(sub_gain[:], vec[:, V_SUB:V_SUB + 1], 1.0 - LAMBDA_INIT, None, ALU.mult))
            pool(0)
            ffn(0)
            conv_mixer()
            ffn(1)
            attention()
            ffn(2)
            pool(1)
            ffn(3)

        @block.gpsimd
        def _(pool_e):
            def add_squares(r):
                for m in range(KT):
                    pool_e.wait_ge(sq_ready, 8 * r + m + 1)
                    if m == 0:
                        if r:
                            pool_e.wait_ge(mean_ready, r)
                        pool_e.tensor_copy(sqacc[:], sq[:, 0, :]).then_inc(sq_added, 1)
                    else:
                        pool_e.wait_ge(sq_added, 8 * r + m)
                        pool_e.tensor_tensor(sqacc[:], sqacc[:], sq[:, m % 2, :], ALU.add).then_inc(sq_added, 1)

            def store_stage(b, hist, states_p, states_s):
                pool_e.wait_ge(tp_taken, b)
                pool_e.dma_start(states_p, stage[0:hist, :]).then_inc(stored, 16)
                pool_e.dma_start(states_s, stage[hist:hist + DEC, :]).then_inc(stored, 16)

            pool_e.memset(avg[:], 1.0 / D).then_inc(ready0, 1)
            pool_e.memset(eps[:], EPS).then_inc(ready0, 1)
            pool_e.memset(one_row[:], 0.0).then_inc(pool_seq, 1)
            pool_e.wait_ge(pool_seq, 1)
            pool_e.memset(one_row[:, DEC - 1:DEC], 1.0).then_inc(ready0, 1)
            add_squares(0)
            for q in range(2):
                store_stage(TP[f"pool{q}"] + 4, HIST_P, pool_state_p[q, 0], pool_state_s[q, :, HIST_P - 1, :])
                add_squares(6 * q + 1)
                if q:
                    break
                add_squares(2)
                for t, i in enumerate(POOL_TILES):
                    out = conv[:, i, 0:SEQ]
                    for w in range(1, TAPS):
                        p = (TAPS - 1) * t + w - 1
                        pool_e.wait_ge(prod_ready, TAPS * t + w + 1)
                        if w > 1:
                            pool_e.wait_ge(prod_added, p)
                        pool_e.tensor_tensor(out, out, prod_p[:, p % 3, :], ALU.add).then_inc(prod_added, 1)
                store_stage(TP["conv"] + 6, HIST_C, conv_state_p[0, 0], conv_state_s[0, :, HIST_C - 1, :])
                add_squares(3)
                add_squares(4)
                k_out = k_rows_p[0, 0].rearrange("(b p) h c d -> p b h (c d)", p=P)
                v_out = v_rows_p[0, 0].rearrange("(b p) h d -> p b h d", p=P)
                pool_e.wait_ge(units_done, UNIT["qkv"])
                for h in range(HEADS + 1):
                    if h < HEADS:
                        if h >= 2:
                            pool_e.wait_ge(s_taken, 3 * (h - 1))
                        pool_e.tensor_scalar(bias_h[:, h % 2, :], const[:, C_DIST:C_DIST + SEQ], 2.0 ** -(h + 1) / SCALE, 0.0,
                                             ALU.mult, ALU.add).then_inc(bias_ready, 1)
                        pool_e.wait_ge(evacuated, TILE["qkv"] + 3 * h + 3)
                        pool_e.tensor_copy(vs[:, h, :], v_raw[:, SEQ:T]).then_inc(saved_s, 1)
                        pool_e.wait_ge(qkn_ready, 2 * h + 2)
                        pool_e.tensor_copy(qs[:, h, :], qn[:, SEQ:T]).then_inc(saved_s, 1)
                        pool_e.tensor_copy(ks[:, h, :], kn[:, SEQ:T]).then_inc(saved_s, 1)
                    if h:
                        g = h - 1
                        pool_e.wait_ge(t_taken, 2 * g + 2)
                        pool_e.dma_start(k_out[:, :, g, :], k_tok[:, g % 2]).then_inc(rows_stored[g % 2], 16)
                        pool_e.dma_start(v_out[:, :, g, :], v_tok[:, g % 2]).then_inc(rows_stored[g % 2], 16)
                pool_e.wait_ge(factors_ok, 1)
                scale = o_tmp[:, 2, :].rearrange("p (b h) -> p b h", b=4)
                for h in range(HEADS):
                    pool_e.tensor_tensor(o_tok[:, :, h, :], o_tok[:, :, h, :], scale[:, :, h:h + 1].to_broadcast([P, 4, P]), ALU.mult)\
                          .then_inc(o_scaled, 1)
                pool_e.wait_ge(rows_s_taken, 2)
                for h in range(HEADS):
                    pool_e.dma_start(k_rows_s[0, :, 0, h].rearrange("b c d -> b (c d)"), ks_rows_sb[h * DEC:(h + 1) * DEC, :])\
                          .then_inc(stored, 16)
                    pool_e.dma_start(v_rows_s[0, :, 0, h, :], vs_rows_sb[h * DEC:(h + 1) * DEC, :]).then_inc(stored, 16)
                add_squares(5)
                add_squares(6)
            for m in range(KT):
                tb = TP["end"] + 2 * m
                pool_e.wait_ge(tp_taken, tb + 1)
                pool_e.dma_start(y_prompt[0].rearrange("(b p) c -> p b c", p=P)[:, :, m * P:(m + 1) * P],
                                 y_sb[:, m, 0:SEQ].rearrange("p (b c) -> p b c", b=4)).then_inc(stored, 16)
                pool_e.wait_ge(tp_taken, tb + 2)
                pool_e.dma_start(y_sample[:, 0, m * P:(m + 1) * P], y_sb[0:DEC, m, SEQ:SEQ + P]).then_inc(stored, 16)


OUTPUTS = (("y_prompt", (1, SEQ, D)), ("y_sample", (DEC, 1, D)),
           ("pool_state_p", (2, 1, HIST_P, D)), ("pool_state_s", (2, DEC, HIST_P, D)),
           ("conv_state_p", (1, 1, HIST_C, D)), ("conv_state_s", (1, DEC, HIST_C, D)),
           ("k_rows_p", (1, 1, SEQ, HEADS, 2, QK)), ("v_rows_p", (1, 1, SEQ, HEADS, P)),
           ("k_rows_s", (1, DEC, 1, HEADS, 2, QK)), ("v_rows_s", (1, DEC, 1, HEADS, P)))
INPUTS = ("x_prompt", "x_sample", "state_pool", "state_conv", "cache_k", "cache_v", "page_table",
          "norm_mix", "norm_ffn", "pool_w", "pool_scale", "conv_w_in", "conv_b_in", "conv_dw", "conv_dw_b",
          "conv_ln_g", "conv_ln_b", "conv_w_out", "conv_b_out", "attn_w_qkv", "attn_q_norm", "attn_k_norm",
          "attn_lq1", "attn_lk1", "attn_lq2", "attn_lk2", "attn_subln", "attn_w_o",
          "ffn_w_gate", "ffn_w_up", "ffn_w_down")


def kernel(**inputs):
    from concourse import bacc
    from concourse.bass_utils import run_bass_kernel_spmd

    nc = bacc.Bacc("TRN2", target_bir_lowering=False, num_devices=1)
    arrays, args = {}, []
    for name in INPUTS:
        a = np.ascontiguousarray(inputs[name])
        arrays[f"in_{name}"] = a
        args.append(nc.dram_tensor(f"in_{name}", a.shape, mybir.dt.from_np(a.dtype), kind="ExternalInput").ap())
    arrays["in_shape_constants"] = constants()
    args.append(nc.dram_tensor("in_shape_constants", (P, N_CONST), F32, kind="ExternalInput").ap())
    for name, shape in OUTPUTS:
        args.append(nc.dram_tensor(f"out_{name}", shape, F32, kind="ExternalOutput").ap())
    trunk_step(nc, *args)
    r = run_bass_kernel_spmd(nc, [arrays], core_ids=[0])
    return tuple(r.results[0][f"out_{name}"] for name, _ in OUTPUTS)
```

```python
import math
from contextlib import ExitStack

import numpy as np

import concourse.bass as bass
from concourse import mybir

F32 = mybir.dt.float32
F32R = mybir.dt.float32r
I32 = mybir.dt.int32
ALU = mybir.AluOpType
ACT = mybir.ActivationFunctionType
AX = mybir.AxisListType

P = 128
D = 1024
KT = D // P
SEQ, DEC = 512, 8
T = SEQ + DEC
HALF = T // 2
FF = 2816
FT = FF // P
HEADS, QK = 8, 64
PAST, PAGE = 256, 128
WINDOWS = (2, 4, 8, 16)
HIST_P, HIST_C, TAPS = 15, 30, 31
EPS = 1e-6
LAMBDA_INIT = 0.8 - 0.6 * math.exp(-0.3 * 2)
SCALE = QK ** -0.5
TAIL_P = HIST_P + DEC
TAIL_C = HIST_C + DEC

ORDER = [("pool0", 2, 8), ("ffn0", 2 * FT + 24, 2 * FT + 8), ("conv_in", 16, 16), ("conv_out", 8, 8),
         ("ffn1", 2 * FT + 24, 2 * FT + 8), ("qkv", 24, 24), ("w_o", 8, 8),
         ("ffn2", 2 * FT + 24, 2 * FT + 8), ("pool1", 2, 8), ("ffn3", 2 * FT + 24, 2 * FT + 8)]
UNIT, TILE = {}, {}
_u = _m = 0
for _name, _units, _tiles in ORDER:
    UNIT[_name], TILE[_name] = _u, _m
    _u, _m = _u + _units, _m + _tiles
UNITS = _u

V_MIX, V_FFN, V_PSCALE, V_BIN, V_DWB, V_LNG, V_LNB, V_BOUT, V_DW, V_QN, V_KN, V_SUB = (
    0, 32, 64, 80, 96, 104, 112, 120, 128, 376, 377, 378)
C_ID, C_BLK, C_DIST, C_POS, C_CNT = 0, 128, 256, 768, 1024
N_CONST = C_CNT + 64


class At:

    def __init__(self, start, step=0, i=None):
        self.start, self.step, self.i = start, step, i

    def __add__(self, k):
        return At(self.start + k, self.step, self.i)

    @property
    def v(self):
        return self.start if self.i is None else self.i * self.step + self.start

    def slot(self, depth):
        assert self.step % depth == 0
        return self.start % depth

    def turn(self, depth):
        assert self.step % depth == 0
        return At(self.start // depth, self.step // depth, self.i)


def at(start, step, i):
    return At(start + step * i) if isinstance(i, int) else At(start, step, i)


def tile_of(t, m):
    if m.i is None:
        return t[:, m.start, :]
    return t[:, bass.ds(m.v, 1), :].rearrange("p o c -> p (o c)")


XIN = {1: 0, 2: 1, 3: 2, 4: 3, 5: 4, 7: 5}
PIECES = (((0, 0), (P, 1)), ((0, 2),), ((0, 3),))
MIX = {"pool0": 0, "conv": 4, "attn": 12, "pool1": 21}
N_VEC_LOADS = 10 + 5
DVE_TILES, POOL_TILES, PE_TILE, SHARED_TAPS = (1, 3, 5, 7), (0, 2, 4), 6, 12
PE_TAPS = [(DVE_TILES[-1], w, SHARED_TAPS - 1) for w in range(SHARED_TAPS)] + [(PE_TILE, w, TAPS - 1) for w in range(TAPS)]
TILES_IN_ORDER = (1, 3, 0, 2, 6, 5, 4, 7)
STORED = {"pool0": 2, "conv": 4, "attn": 4 + 2 * HEADS, "pool1": 6 + 2 * HEADS, "end": 6 + 2 * HEADS + 2 * KT}


def constants():
    c = np.zeros((P, N_CONST), np.float32)
    c[:, C_ID:C_ID + P] = np.eye(P)
    c[0:QK, C_BLK:C_BLK + QK] = 1.0 / QK
    c[QK:P, C_BLK + QK:C_BLK + P] = 1.0 / QK
    dist = np.arange(SEQ)[None, :] - (SEQ - P) - np.arange(P)[:, None]
    c[:, C_DIST:C_DIST + SEQ] = np.where(dist <= 0, dist, -1e33)
    slope = 2.0 ** -(np.arange(HEADS * DEC) // DEC + 1.0)
    c[0:HEADS * DEC, C_POS:C_POS + PAST] = slope[:, None] * (np.arange(PAST) - PAST)[None, :] / SCALE
    for g, win in enumerate(WINDOWS):
        c[:, C_CNT + 16 * g:C_CNT + 16 * g + 16] = 1.0 / np.minimum(np.arange(16) + 1, win)
    return c


def trunk_step(nc, x_prompt, x_sample, state_pool, state_conv, cache_k, cache_v, page_table,
               norm_mix, norm_ffn, pool_w, pool_scale, conv_w_in, conv_b_in, conv_dw, conv_dw_b,
               conv_ln_g, conv_ln_b, conv_w_out, conv_b_out, attn_w_qkv, attn_q_norm, attn_k_norm,
               attn_lq1, attn_lk1, attn_lq2, attn_lk2, attn_subln, attn_w_o,
               ffn_w_gate, ffn_w_up, ffn_w_down, shape_constants,
               y_prompt, y_sample, pool_state_p, pool_state_s, conv_state_p, conv_state_s,
               k_rows_p, v_rows_p, k_rows_s, v_rows_s):
    ctx = ExitStack()
    with ctx:
        place = [16512]

        def fixed(name, shape, dt=F32):
            t = nc.alloc_sbuf_tensor_at(name, shape, dt, offset=place[0])
            place[0] += (4 * int(np.prod(shape[1:])) + 31) // 32 * 32
            return t

        def overlay(start):
            at = [start]

            def take(name, shape, dt=F32):
                t = nc.alloc_sbuf_tensor_at(name, shape, dt, offset=at[0])
                at[0] += (4 * int(np.prod(shape[1:])) + 31) // 32 * 32
                take.end = at[0]
                return t
            return take

        x = fixed("x", [P, KT, T])
        xin_at = place[0]
        xin_hi = fixed("xin_hi", [P, KT, T], F32R)
        xin_lo = fixed("xin_lo", [P, KT, T], F32R)
        rstd_at = place[0]
        rstd = fixed("rstd", [P, T])
        lnb = fixed("lnb", [P, T])
        sqacc = fixed("sqacc", [P, T])
        sq = fixed("sq", [P, 2, T])
        raw = fixed("raw", [P, 4, 1024])
        w_hi = [fixed(f"w_hi{s}", [P, 1024], F32R) for s in range(2)]
        w_lo = [fixed(f"w_lo{s}", [P, 1024], F32R) for s in range(2)]
        const = fixed("const", [P, N_CONST])
        vec = fixed("vec", [P, 379])
        avg = fixed("avg", [P, P])
        eps = fixed("eps", [P, 1])
        one_row = fixed("one_row", [P, 2 * DEC - 1])
        neg_lam = fixed("neg_lam", [P, 1])
        sub_gain = fixed("sub_gain", [P, 1])
        stage = fixed("stage", [TAIL_C, D])
        qs, ks, vs = (fixed(n, [P, HEADS, DEC]) for n in ("qs", "ks", "vs"))
        temps_at = place[0]
        take = overlay(temps_at)
        g_buf = take("g_buf", [P, 2, T])
        sg_buf = take("sg_buf", [P, 2, T])
        u_buf = take("u_buf", [P, T])
        h_buf = take("h_buf", [P, 2, T])
        arena_at = take.end
        take = overlay(arena_at)
        h_hi = take("h_hi", [P, FT, T], F32R)
        h_lo = take("h_lo", [P, FT, T], F32R)
        arena_end = take.end
        assert arena_end <= nc.sbuf_usable_end
        ident = const[:, C_ID:C_ID + P]
        blk = const[:, C_BLK:C_BLK + P]

        take = overlay(arena_at)
        x_rows = take("x_rows", [P, 4, D])
        xs_rows = take("xs_rows", [DEC, D])
        vec_rows = take("vec_rows", [P, 3, P])
        lam_rows = take("lam_rows", [P, 4, QK])
        lam_tmp = take("lam_tmp", [P, QK + 4])
        take = overlay(arena_at)
        mix_hi = take("mix_hi", [P, KT, T], F32R)
        mix_lo = take("mix_lo", [P, KT, T], F32R)
        mixer_at = take.end
        take = overlay(mixer_at)
        hn = take("hn", [P, KT, 16 + T])
        hist_rows = take("hist_rows", [DEC * HIST_P, D])
        hist_s = take("hist_s", [P, KT, DEC, 16])
        wsum = take("wsum", [P, 2, 2, 16 + SEQ])
        diff = take("diff", [P, 4, 2, T])
        edge = take("edge", [P, 4, 2, 16])
        last_s = take("last_s", [P, KT, DEC])
        assert take.end <= arena_end
        take = overlay(temps_at)
        wsum_p = take("wsum_p", [P, 3, 2, 16 + SEQ])
        assert take.end <= arena_at
        take = overlay(mixer_at)
        glu = take("glu", [P, KT, HIST_C + T])
        conv = take("conv", [P, KT, T])
        hist_c = take("hist_c", [P, KT, DEC, TAPS])
        chist_rows = take("chist_rows", [4 * HIST_C, 2, D])
        prod_p = take("prod_p", [P, 3, SEQ])
        assert take.end <= arena_end
        x_out = nc.alloc_sbuf_tensor_at("x_out", [P, 4, T], F32, offset=temps_at)
        prod_s = nc.alloc_sbuf_tensor_at("prod_s", [P, KT // 2, DEC, TAPS], F32, offset=temps_at + 5 * 4 * T)
        assert KT // 2 * DEC * TAPS <= 2 * T
        diag = nc.alloc_sbuf_tensor_at("diag", [P, 4, P], F32, offset=temps_at + 4 * 4 * T)
        act_in = g_buf
        gate_s = sg_buf
        take = overlay(temps_at)
        q_raw, k_raw, v_raw, qn, kn, ln_q, ln_k = (
            take(n, [P, T]) for n in ("q_raw", "k_raw", "v_raw", "qn", "kn", "ln_q", "ln_k"))
        assert take.end <= arena_at
        take = overlay(mixer_at)
        o_tok = take("o_tok", [P, 4, HEADS, P])
        v_page = [take(f"v_page{n}", [P, 2, D]) for n in range(2)]
        head_at = take.end
        s_buf = take("s_buf", [P, 2, SEQ])
        a_buf = take("a_buf", [P, SEQ])
        t_buf = take("t_buf", [P, SEQ])
        aT = take("aT", [P, SEQ])
        v_tok = take("v_tok", [P, 2, 4, P])
        k_tok = take("k_tok", [P, 2, 4, P])
        bias_h = take("bias_h", [P, 2, SEQ])
        o_sq = take("o_sq", [P, SEQ])
        small_at = take.end
        row_max = take("row_max", [P, 2, 2])
        row_sum = take("row_sum", [P, 2, 2])
        row_scl = take("row_scl", [P, 2, 2])
        row_inv = take("row_inv", [P, 2, 2])
        o_max = take("o_max", [P, 4, HEADS])
        o_inv = take("o_inv", [P, 4, HEADS])
        o_ss = take("o_ss", [P, 4, HEADS])
        o_tmp = take("o_tmp", [P, 3, 4 * HEADS])
        assert take.end <= arena_end, take.end - arena_end
        take = overlay(head_at)
        v_page += [take(f"v_page{n}", [P, 2, D]) for n in range(2, 4)]
        ks_rows_sb = take("ks_rows_sb", [HEADS * DEC, P])
        vs_rows_sb = take("vs_rows_sb", [HEADS * DEC, P])
        os_tok = take("os_tok", [HEADS * DEC, P])
        os_sq = take("os_sq", [HEADS * DEC, P])
        assert take.end <= small_at, take.end - small_at
        R = HEADS * DEC
        take = overlay(temps_at)
        k_prod = take("k_prod", [P, 2, D])
        s_cols = take("s_cols", [P, 2, R, 2])
        s_dec = take("s_dec", [R, 2, PAST + 1])
        assert take.end <= temps_at + 7 * 4 * T
        a_dec = nc.alloc_sbuf_tensor_at("a_dec", [R, PAST + 1], F32, offset=xin_at)
        t_dec = nc.alloc_sbuf_tensor_at("t_dec", [R, PAST + 1], F32, offset=xin_at + 1056)
        aT_dec = nc.alloc_sbuf_tensor_at("aT_dec", [P, 2, R], F32, offset=xin_at + 2112)
        os_col = nc.alloc_sbuf_tensor_at("os_col", [P, R], F32, offset=xin_at + 2624)
        m_dec = nc.alloc_sbuf_tensor_at("m_dec", [R, 16], F32, offset=xin_at + 2880)
        new_dec = nc.alloc_sbuf_tensor_at("new_dec", [P, R], F32, offset=xin_at + 2944)
        os_rows = nc.alloc_sbuf_tensor_at("os_rows", [DEC, D], F32, offset=temps_at)
        take = overlay(xin_at + 3520)
        k_page = [take(f"k_page{n}", [P, 2, D]) for n in range(3)]
        assert take.end <= rstd_at
        v_place = v_page + [k_page[2], k_page[0], k_page[1]] + v_page[:DEC - 7]
        y_sb = nc.alloc_sbuf_tensor_at("y_sb", [P, KT, SEQ + P], F32, offset=xin_at)

        acc = nc.alloc_psum_tensor("acc", [P, 4, 512], F32)
        pair = nc.alloc_psum_tensor("pair", [P, 2, 512], F32)
        bank6 = nc.alloc_psum_tensor("bank6", [P, 512], F32)
        bank7 = nc.alloc_psum_tensor("bank7", [P, 512], F32)
        bank = [bank6, bank7]

        def sem(name):
            return ctx.enter_context(nc.semaphore(name))

        landed = [sem(f"landed{s}") for s in range(4)]
        split_hi, split_lo = sem("split_hi"), sem("split_lo")
        units_done = sem("units_done")
        tile_done = sem("tile_done")
        evacuated = sem("evacuated")
        sq_ready, sq_added = sem("sq_ready"), sem("sq_added")
        mean_ready, rstd_ready = sem("mean_ready"), sem("rstd_ready")
        xin_hi_ok, xin_lo_ok = sem("xin_hi_ok"), sem("xin_lo_ok")
        tp_full, tp_taken = sem("tp_full"), sem("tp_taken")
        sg_ready, h_ready, h_hi_ok, h_lo_ok = sem("sg_ready"), sem("h_ready"), sem("h_hi_ok"), sem("h_lo_ok")
        ident_in, vecs_in, lam_in, hist_in = sem("ident_in"), sem("vecs_in"), sem("lam_in"), sem("hist_in")
        rows_in = [sem(f"rows_in{s}") for s in range(2)]
        ready0 = sem("ready0")
        stored, moved = sem("stored"), sem("moved")
        act_seq, dve_seq, pool_seq = sem("act_seq"), sem("dve_seq"), sem("pool_seq")
        pads_ready, pool_sums = sem("pads_ready"), sem("pool_sums")
        hn_ready, diff_ready, mix_hi_ok, mix_lo_ok = sem("hn_ready"), sem("diff_ready"), sem("mix_hi_ok"), sem("mix_lo_ok")
        glu_ready, gate_ready = sem("glu_ready"), sem("gate_ready")
        conv_dve_ready, conv_pe_ready, conv_s_ready = sem("conv_dve_ready"), sem("conv_pe_ready"), sem("conv_s_ready")
        prod_ready, prod_added = sem("prod_ready"), sem("prod_added")
        diag_ready, diag_used = sem("diag_ready"), sem("diag_used")
        cmean, cent, csq, cvar, crstd, cnorm, cact = (
            sem(n) for n in ("cmean", "cent", "csq", "cvar", "crstd", "cnorm", "cact"))
        nsq_ready, nrm_ready, nrm_ln, nrm_exp = sem("nsq_ready"), sem("nrm_ready"), sem("nrm_ln"), sem("nrm_exp")
        qkn_ready, t_ready, t_taken = sem("qkn_ready"), sem("t_ready"), sem("t_taken")
        qk_ready, s_taken, max_ready, exp_done, a_ready, at_ready, at_taken, pv_done = (
            sem(n) for n in ("qk_ready", "s_taken", "max_ready", "exp_done", "a_ready", "at_ready", "at_taken", "pv_done"))
        bias_ready, o_taken, osq_done, oss_done, saved_s = (
            sem(n) for n in ("bias_ready", "o_taken", "osq_done", "oss_done", "saved_s"))
        rows_stored = [sem(f"rows_stored{s}") for s in range(2)]
        kpage_in = [sem(f"kpage_in{s}") for s in range(3)]
        vpage_in = [sem(f"vpage_in{s}") for s in range(DEC)]
        q_all_ready, k_prod_ok, k_folded, vpage_used, factors_ok, v_weighted, v_summed, os_rows_ok, os_turned = (
            sem(n) for n in ("q_all_ready", "k_prod_ok", "k_folded", "vpage_used", "factors_ok", "v_weighted", "v_summed",
                             "os_rows_ok", "os_turned"))
        s_cols_ok, new_prod_ok, s_rows_full, dec_max_ok, dec_exp_ok, a_dec_ok, a_dec_full, aT_dec_ok = (
            sem(n) for n in ("s_cols_ok", "new_prod_ok", "s_rows_full", "dec_max_ok", "dec_exp_ok", "a_dec_ok",
                             "a_dec_full", "aT_dec_ok"))
        rows_s_full, rows_s_taken, os_col_ok, os_full, os_in_ok, os_sq_ok, os_scaled, os_back = (
            sem(n) for n in ("rows_s_full", "rows_s_taken", "os_col_ok", "os_full", "os_in_ok", "os_sq_ok",
                             "os_scaled", "os_back"))
        roots_in, roots_ok, o_scaled, o_back, lam_sums, lam_exps = (
            sem(n) for n in ("roots_in", "roots_ok", "o_scaled", "o_back", "lam_sums", "lam_exps"))

        block = ctx.enter_context(nc.Block())

        def halves(t):
            return t.rearrange("p (h c) -> p h c", h=2)

        TP = {"start": 0, "pool0": 12, "conv": 16, "pool1": 22, "end": 26}

        @block.sync
        def _(sp):
            def load(n, src, cols=1024):
                if n.i is not None or n.start >= 4:
                    sp.wait_ge(split_lo, (n + -3).v)
                sp.dma_start(raw[:, n.slot(4), 0:cols].rearrange("p (k c) -> p k c", c=src.shape[-1]), src)\
                  .then_inc(landed[n.slot(4)], 16)

            def tiles(w, k0, k1, col):
                return w[k0 * P:k1 * P, col].rearrange("(k p) c -> p k c", p=P)

            def load_pool(q):
                for u in range(2):
                    load(At(UNIT[f"pool{q}"] + u), pool_w[q, 2 * u:2 * u + 2].rearrange("g (k p) c -> p (g k) c", p=P))

            def load_ffn(layer):
                base = UNIT[f"ffn{layer}"]

                def two_tiles(i):
                    for j in range(4):
                        w = (ffn_w_gate, ffn_w_up)[j % 2][layer]
                        load(at(base + j, 4, i), tiles(w, 0, KT, bass.ds(i * (2 * P) + (j // 2) * P, P)))
                two_tiles(0)
                with sp.Fori(1, FT // 2) as i:
                    two_tiles(i)
                with sp.Fori(0, 2) as i:
                    for c in range(4):
                        for j, (k0, k1) in enumerate(((0, 8), (8, 16), (16, FT))):
                            load(At(base + 2 * FT + 3 * c + j, 12, i),
                                 tiles(ffn_w_down[layer], k0, k1, bass.ds(i * (4 * P) + c * P, P)), (k1 - k0) * P)

            sp.dma_start(const[:], shape_constants).then_inc(ident_in, 16)
            sp.dma_start(xs_rows[:], x_sample[:, 0, :]).then_inc(rows_in[0], 16)
            for half in range(2):
                cols = slice(half * 512, half * 512 + 512)
                sp.dma_start(x_rows[:, :, cols], x_prompt[0].rearrange("(b p) d -> p b d", p=P)[:, :, cols]).then_inc(rows_in[half], 16)
            load_pool(0)
            sp.dma_start(hist_rows[:], state_pool[0].rearrange("b j d -> (b j) d")).then_inc(hist_in, 16)
            for q in range(2):
                sp.dma_start(pool_state_s[q, :, 0:HIST_P - 1, :], state_pool[q, :, 1:HIST_P, :]).then_inc(moved, 16)
            sp.dma_start(conv_state_s[0, :, 0:HIST_C - 1, :], state_conv[0, :, 1:HIST_C, :]).then_inc(moved, 16)

            load_ffn(0)
            for i in range(KT):
                for half in range(2):
                    load(At(UNIT["conv_in"] + 2 * i + half), tiles(conv_w_in[0], 0, KT, slice(half * D + i * P, half * D + (i + 1) * P)))
                if i == 0:
                    sp.wait_ge(units_done, UNIT["conv_in"])
                    for t in range(2):
                        sp.dma_start(chist_rows[:, t, :], state_conv[0, 4 * t:4 * t + 4].rearrange("b j d -> (b j) d")).then_inc(hist_in, 16)
            for i in range(KT):
                load(At(UNIT["conv_out"] + i), tiles(conv_w_out[0], 0, KT, slice(i * P, (i + 1) * P)))
            load_ffn(1)
            def page(dst, cache, b, landed_sem):
                for j in range(2):
                    r = sp.value_load(page_table[b:b + 1, j:j + 1], min_val=0, max_val=cache.shape[1] - 1)
                    sp.dma_start(dst[:, j, :], cache[0, bass.ds(r, 1)].rearrange("o p h d -> p (o h d)")).then_inc(landed_sem, 16)
            for h in range(HEADS):
                for j in range(3):
                    load(At(UNIT["qkv"] + 3 * h + j), tiles(attn_w_qkv[0], 0, KT, slice(j * D + h * P, j * D + (h + 1) * P)))
                if h == 0:
                    sp.wait_ge(units_done, UNIT["qkv"])
                    for b in range(2):
                        page(v_page[b], cache_v, b, vpage_in[b])
            for i in range(4):
                load(At(UNIT["w_o"] + i), tiles(attn_w_o[0], 0, KT, slice(i * P, (i + 1) * P)))
            ck = cache_k.rearrange("l n p h c d -> l n p h (c d)")
            sp.wait_ge(units_done, UNIT["w_o"])
            for b in range(3):
                page(k_page[b], ck, b, kpage_in[b])
            sp.wait_ge(pv_done, 3 * HEADS)
            sp.wait_ge(oss_done, HEADS)
            for s in range(2):
                sp.wait_ge(rows_stored[s], 16 * HEADS)
            for b in range(2, 4):
                page(v_place[b], cache_v, b, vpage_in[b])
            for b in range(3, DEC):
                sp.wait_ge(k_prod_ok, 2 * (b - 2))
                page(k_page[b % 3], ck, b, kpage_in[b % 3])
            for b in range(4, DEC):
                if b < 7:
                    sp.wait_ge(k_prod_ok, 2 * (b + 2))
                else:
                    sp.wait_ge(vpage_used, b - 6)
                page(v_place[b], cache_v, b, vpage_in[b])
            for i in range(4, KT):
                load(At(UNIT["w_o"] + i), tiles(attn_w_o[0], 0, KT, slice(i * P, (i + 1) * P)))
            load_ffn(2)
            load_pool(1)
            sp.wait_ge(units_done, UNIT["pool1"])
            sp.dma_start(hist_rows[:], state_pool[1].rearrange("b j d -> (b j) d")).then_inc(hist_in, 16)
            load_ffn(3)
            sp.wait_ge(moved, 48)
            sp.wait_ge(stored, 16 * STORED["end"])

        @block.tensor
        def _(pe):
            def tile_products(m, w_tile, s, k_hi, k_lo, start, stop):
                b = 2 * m.slot(2)
                for t, (w, v) in enumerate(((w_hi[s], k_hi), (w_hi[s], k_lo), (w_lo[s], k_hi))):
                    for h in range(2):
                        last = pe.matmul(acc[:, b + h, 0:HALF], w[:, w_tile * P:(w_tile + 1) * P],
                                         v[:, h * HALF:(h + 1) * HALF],
                                         start=start and t == 0, stop=stop and t == 2)
                return last

            def unit(n, m, hi, lo, k0=0, k1=KT, kn_=KT, before=None):
                pe.wait_ge(split_lo, (n + 1).v)
                if k0 == 0 and (m.i is not None or m.start >= 2):
                    pe.wait_ge(evacuated, (m + -1).v)
                for k in range(k0, k1):
                    if before is not None:
                        before(k)
                    last = tile_products(m, k - k0, n.slot(2), hi[:, k, :], lo[:, k, :], k == 0, k == kn_ - 1)
                last.then_inc(units_done, 1)

            def means(r):
                pe.wait_ge(sq_added, 8 * r + 8)
                if r:
                    pe.wait_ge(rstd_ready, r)
                for h in range(2):
                    last = pe.matmul(pair[:, h, 0:HALF], avg[:], sqacc[:, h * HALF:(h + 1) * HALF], start=True, stop=True)
                last.then_inc(mean_ready, 1)

            def first_unit(n, m, r, xi):
                def before(k):
                    pe.wait_ge(xin_lo_ok, 8 * xi + k + 1)
                    if k == 5:
                        means(r)
                unit(n, m, xin_hi, xin_lo, before=before)

            def batch(b, parts, dst=None):
                if b >= 2:
                    pe.wait_ge(tp_taken, b - 1)
                to = bank[b % 2]
                for cols, src in parts:
                    rows_n, cols_n = src.shape[0], src.shape[-1]
                    last = pe.transpose(to[0:cols_n, cols:cols + rows_n], src, ident[0:rows_n, 0:rows_n])
                last.then_inc(tp_full, 1)

            def pool(q):
                u, m0, tb = UNIT[f"pool{q}"], TILE[f"pool{q}"], TP[f"pool{q}"]
                if q:
                    means(6)
                pe.wait_ge(hist_in, 16 if q == 0 else 64)
                for b in range(2):
                    batch(tb + b, [(120 * k, hist_rows[:, (4 * b + k) * P:(4 * b + k + 1) * P]) for k in range(4)])
                pe.wait_ge(hn_ready, 8 * q + 8)
                for b in range(2):
                    tails(tb + 2 + b, hn, 16 + SEQ - HIST_P, TAIL_P, b)
                for g in range(4):
                    n = At(u + g // 2)
                    pe.wait_ge(split_lo, (n + 1).v)
                    pe.wait_ge(mix_lo_ok, MIX[f"pool{q}"] + g + 1)
                    for mt in range(2):
                        m = At(m0 + 2 * g + mt)
                        if m.start >= 2:
                            pe.wait_ge(evacuated, m.start - 1)
                        for k in range(2):
                            last = tile_products(m, ((g % 2) * 2 + k) * 2 + mt, n.slot(2),
                                                 mix_hi[:, 2 * g + k, :], mix_lo[:, 2 * g + k, :], k == 0, k == 1)
                        last.then_inc(units_done if (g % 2, mt) == (1, 1) else tile_done, 1)

            def tails(b, src, col, n, part):
                if b >= 2:
                    pe.wait_ge(tp_taken, b - 1)
                for k in range(4):
                    last = pe.transpose(bank[b % 2][0:n, k * P:(k + 1) * P], src[:, 4 * part + k, col:col + n], ident)
                last.then_inc(tp_full, 1)

            def ffn(layer):
                u, m0, r = UNIT[f"ffn{layer}"], TILE[f"ffn{layer}"], 2 * layer + 1
                first_unit(At(u), At(m0), r, XIN[r])
                for j in range(1, 4):
                    unit(At(u + j), At(m0 + j), xin_hi, xin_lo)
                with pe.Fori(1, FT // 2) as i:
                    for j in range(4):
                        unit(At(u + j, 4, i), At(m0 + j, 4, i), xin_hi, xin_lo)
                with pe.Fori(0, 2) as i:
                    for c in range(4):
                        m = At(m0 + 2 * FT + c, 4, i)
                        for j, (k0, k1) in enumerate(((0, 8), (8, 16), (16, FT))):
                            def before(k):
                                pe.wait_ge(h_lo_ok, FT * layer + k + 1)
                            unit(At(u + 2 * FT + 3 * c + j, 12, i), m, h_hi, h_lo, k0, k1, FT,
                                 before if c == 0 else None)
                        if layer == 3:
                            if c:
                                y_tile(m0, i, c - 1)
                            if c == 3:
                                y_tile(m0, i, 3)

            def y_tile(m0, i, c):
                pe.wait_ge(evacuated, i * 4 + (m0 + 2 * FT + c + 1))
                tb = TP["end"] + 2 * c
                pe.wait_ge(tp_taken, i * 8 + (tb - 1))
                for b in range(4):
                    last = pe.transpose(bank6[:, b * P:(b + 1) * P], x_out[:, c, b * P:(b + 1) * P], ident)
                last.then_inc(tp_full, 1)
                pe.wait_ge(tp_taken, i * 8 + tb)
                pe.transpose(bank7[0:DEC, 0:P], x_out[:, c, SEQ:T], ident).then_inc(tp_full, 1)

            def conv_mixer():
                u, m0 = UNIT["conv_in"], TILE["conv_in"]
                for i in range(KT):
                    for half in range(2):
                        n = 2 * i + half
                        if n == 0:
                            first_unit(At(u), At(m0), 2, XIN[2])
                        else:
                            unit(At(u + n), At(m0 + n), xin_hi, xin_lo)
                    if i == 1:
                        pe.wait_ge(hist_in, 48)
                        for b in range(4):
                            batch(TP["conv"] + b, [(240 * k + 120 * t, chist_rows[:, t, (2 * b + k) * P:(2 * b + k + 1) * P])
                                                   for k in range(2) for t in range(2)])
                pe.wait_ge(glu_ready, KT)
                for b in range(2):
                    tails(TP["conv"] + 4 + b, glu, SEQ, TAIL_C, b)
                pe.wait_ge(evacuated, m0 + 2 * KT)
                for f, (i, w, last_tap) in enumerate(PE_TAPS):
                    pe.wait_ge(diag_ready, f + 1)
                    pe.matmul(acc[:, 2 + (i == PE_TILE), :], diag[:, f % 4, :], glu[:, i, w:w + SEQ],
                              start=w == 0, stop=w == last_tap).then_inc(diag_used, 1)
                pe.wait_ge(rstd_ready, 3)
                pe.wait_ge(conv_s_ready, 2)
                pe.wait_ge(conv_pe_ready, 2)
                for j, k in enumerate(TILES_IN_ORDER):
                    if k in DVE_TILES:
                        pe.wait_ge(conv_dve_ready, DVE_TILES.index(k) + 1)
                    elif k in POOL_TILES:
                        pe.wait_ge(prod_added, (TAPS - 1) * (POOL_TILES.index(k) + 1))
                    for h in range(2):
                        last = pe.matmul(pair[:, h, 0:HALF], avg[:], conv[:, k, h * HALF:(h + 1) * HALF],
                                         start=j == 0, stop=j == KT - 1)
                last.then_inc(cmean, 1)
                for k in range(KT):
                    pe.wait_ge(csq, k + 1)
                    for h in range(2):
                        last = pe.matmul(acc[:, h, 0:HALF], avg[:], glu[:, k, h * HALF:(h + 1) * HALF],
                                         start=k == 0, stop=k == KT - 1)
                last.then_inc(cvar, 1)
                u, m0 = UNIT["conv_out"], TILE["conv_out"]
                for i in range(KT):
                    def before(k):
                        pe.wait_ge(mix_lo_ok, MIX["conv"] + k + 1)
                    unit(At(u + i), At(m0 + i), mix_hi, mix_lo, before=before if i == 0 else None)

            def attention():
                u, m0 = UNIT["qkv"], TILE["qkv"]

                def stats(i):
                    pe.wait_ge(nsq_ready, i + 1)
                    h, j = divmod(i, 2)
                    if h:
                        pe.wait_ge(s_taken, 3 * (h - 1) + j + 1)
                    else:
                        pe.wait_ge(rstd_ready, 5)
                        if j:
                            pe.wait_ge(nrm_ln, 1)
                    for t in range(2):
                        last = pe.matmul(pair[:, t, 0:HALF], blk, sq[:, 0, t * HALF:(t + 1) * HALF], start=True, stop=True)
                    last.then_inc(nrm_ready, 1)

                def turn_head(g):
                    pe.wait_ge(qkn_ready, 2 * g + 2)
                    if g:
                        pe.wait_ge(s_taken, 3 * g)
                    else:
                        pe.wait_ge(nrm_ln, 2)
                    for j, src in enumerate((kn, v_raw)):
                        for b in range(4):
                            last = pe.transpose(pair[:, j, b * P:(b + 1) * P], src[:, b * P:(b + 1) * P], ident)
                    last.then_inc(t_ready, 1)

                def scores(g, piece):
                    if piece == 0:
                        pe.wait_ge(t_taken, 2 * g + 2)
                    elif g + 1 < HEADS:
                        pe.wait_ge(nrm_ln, 2 * (g + 1) + piece)
                    pe.wait_ge(s_taken, 3 * g + piece) if g or piece else None
                    for off, i in PIECES[piece]:
                        for c in range(2):
                            w = (i + 1) * P
                            last = pe.matmul(pair[:, c, off:off + w], qn[c * QK:(c + 1) * QK, i * P:(i + 1) * P],
                                             kn[c * QK:(c + 1) * QK, 0:w], start=True, stop=True)
                    last.then_inc(qk_ready, 1)

                def turn_weights(g, piece):
                    pe.wait_ge(a_ready, 3 * g + piece + 1)
                    if g or piece:
                        pe.wait_ge(at_taken, 3 * g + piece)
                    for off, i in PIECES[piece]:
                        for j in range(i + 1):
                            last = pe.transpose(bank6[:, off + j * P:off + (j + 1) * P], a_buf[:, off + j * P:off + (j + 1) * P], ident)
                    last.then_inc(at_ready, 1)

                def mix_values(g, piece):
                    pe.wait_ge(at_taken, 3 * g + piece + 1)
                    pe.wait_ge(t_taken, 2 * g + 2)
                    if piece == 0 and g:
                        pe.wait_ge(o_taken, g)
                    for off, i in PIECES[piece]:
                        for j in range(i + 1):
                            last = pe.matmul(bank7[:, i * P:(i + 1) * P], aT[:, off + j * P:off + (j + 1) * P],
                                             v_tok[:, g % 2, j, :], start=j == 0, stop=j == i)
                    last.then_inc(pv_done, 1)

                def turn_back(h):
                    pe.wait_ge(o_scaled, h + 1)
                    if h:
                        pe.wait_ge(mix_lo_ok, MIX["attn"] + h)
                    for b in range(4):
                        last = pe.transpose(bank6[:, b * P:(b + 1) * P], o_tok[:, b, h, :], ident)
                    last.then_inc(o_back, 1)

                pe.wait_ge(tp_taken, TP["conv"] + 6)
                def step_of(h, j, mid, end):
                    n, m = At(u + 3 * h + j), At(m0 + 3 * h + j)
                    if h == j == 0:
                        first_unit(n, m, 4, XIN[4])
                    elif h < HEADS:
                        def before(k):
                            if k == KT // 2:
                                mid()
                        unit(n, m, xin_hi, xin_lo, before=before)
                    else:
                        mid()
                    end()

                def if_head(g, do, *piece):
                    if 0 <= g < HEADS:
                        do(g, *piece)

                for h in range(HEADS + 2):
                    def mid():
                        if_head(h - 2, turn_weights, 1)
                        if_head(h - 2, scores, 2)

                    def end():
                        if_head(h - 2, mix_values, 1)
                        if_head(h - 1, turn_head)
                    step_of(h, 0, mid, end)

                    def mid():
                        if_head(h - 2, turn_weights, 2)
                        if_head(h - 1, scores, 0)

                    def end():
                        if h < HEADS:
                            stats(2 * h)
                        if_head(h - 2, mix_values, 2)
                    step_of(h, 1, mid, end)

                    def mid():
                        if_head(h - 1, turn_weights, 0)
                        if_head(h - 1, scores, 1)

                    def end():
                        if h < HEADS:
                            stats(2 * h + 1)
                        if_head(h - 1, mix_values, 0)
                    step_of(h, 2, mid, end)

                pe.wait_ge(saved_s, 3 * HEADS)
                pe.wait_ge(o_taken, HEADS)
                for j, src in enumerate((ks, vs)):
                    last = pe.transpose(bank7[0:R, j * P:(j + 1) * P], src[:].rearrange("p h b -> p (h b)"), ident)
                last.then_inc(rows_s_full, 1)
                pe.wait_ge(evacuated, TILE["w_o"])
                for b in range(DEC):
                    if b >= 2:
                        pe.wait_ge(k_prod_ok, 2 * (b - 1))
                    for h in range(HEADS):
                        last = pe.matmul(acc[:, 2 * (b % 2) + h // 4, (h % 4) * P:(h % 4 + 1) * P],
                                         qs[:, h, b:b + 1].to_broadcast([P, P]), ident, start=True, stop=True)
                    last.then_inc(q_all_ready, 1)
                    if b >= 2:
                        turn_back(b - 2)
                turn_back(HEADS - 2)
                turn_back(HEADS - 1)
                pe.wait_ge(s_cols_ok, 2 * DEC)
                for c in range(2):
                    for j in range(2):
                        pe.transpose(pair[0:R, 0, (c * 2 + j) * P:(c * 2 + j + 1) * P], s_cols[:, j, :, c], ident)
                pe.wait_ge(new_prod_ok, 1)
                pe.matmul(pair[0:R, 1, 0:2], new_dec[:], blk[:, 0:P:QK], start=True, stop=True).then_inc(s_rows_full, 1)
                pe.wait_ge(a_dec_ok, 1)
                pe.wait_ge(rows_s_taken, 2)
                pe.wait_ge(mix_lo_ok, MIX["attn"] + HEADS)
                for j in range(2):
                    pe.transpose(bank6[:, j * R:(j + 1) * R], a_dec[:, j * PAGE:(j + 1) * PAGE], ident[0:R, 0:R])
                pe.matmul(bank7[:, 0:R], a_dec[:, PAST:PAST + 1].to_broadcast([R, P]), ident[0:R, 0:R],
                          start=True, stop=True).then_inc(a_dec_full, 1)
                for b in range(DEC):
                    pe.wait_ge(v_summed, b + 1)
                    for t in range(2):
                        last = pe.matmul(pair[0:DEC, t, :], one_row[:, DEC - 1 - b:2 * DEC - 1 - b],
                                         v_place[b][:, 0, t * 512:(t + 1) * 512],
                                         start=b == 0, stop=b == DEC - 1)
                    last.then_inc(vpage_used, 1)
                pe.wait_ge(os_rows_ok, 2)
                for h in range(HEADS):
                    last = pe.transpose(pair[:, 0, h * DEC:(h + 1) * DEC], os_rows[:, h * P:(h + 1) * P], ident[0:DEC, 0:DEC])
                last.then_inc(os_turned, 1)
                pe.wait_ge(os_col_ok, 1)
                pe.transpose(pair[:R, 1, 0:P], os_col[:], ident).then_inc(os_full, 1)
                pe.wait_ge(os_scaled, 1)
                pe.transpose(bank7[:, 0:R], os_tok[:], ident[0:R, 0:R]).then_inc(os_back, 1)
                pe.wait_ge(mix_lo_ok, MIX["attn"] + 1 + HEADS)
                for i in range(KT):
                    unit(At(UNIT["w_o"] + i), At(TILE["w_o"] + i), mix_hi, mix_lo)

            pe.wait_ge(ready0, 3)
            pe.wait_ge(ident_in, 16)
            pe.wait_ge(rows_in[0], 32)
            batch(0, [(k * DEC, xs_rows[:, k * P:(k + 1) * P]) for k in range(KT)])
            for k in range(KT):
                if k == KT // 2:
                    pe.wait_ge(rows_in[1], 16)
                batch(1 + k, [(b * P, x_rows[:, b, k * P:(k + 1) * P]) for b in range(4)])
            means(0)
            pe.wait_ge(vecs_in, 16 * N_VEC_LOADS)
            for t, n in enumerate((P, P, 123)):
                batch(9 + t, [(0, vec_rows[0:n, t, :])])
            pool(0)
            ffn(0)
            conv_mixer()
            ffn(1)
            attention()
            ffn(2)
            pool(1)
            ffn(3)

        @block.scalar
        def _(act):
            seq = [0]

            def step(ins):
                seq[0] += 1
                ins.then_inc(act_seq, 1)
                act.wait_ge(act_seq, seq[0])

            def split(n, cols=1024):
                act.wait_ge(landed[n.slot(4)], (n.turn(4).v + 1) * 16)
                if n.start >= 2:
                    act.wait_ge(units_done, (n + -1).v)
                act.activation(w_hi[n.slot(2)][:, 0:cols], raw[:, n.slot(4), 0:cols], ACT.Copy).then_inc(split_hi, 1)

            def squares(r, m, c):
                if r or m.start >= 2:
                    act.wait_ge(sq_added, m.v + (8 * r - 1))
                act.activation(sq[:, c % 2, :], tile_of(x, m), ACT.Square).then_inc(sq_ready, 1)

            def updated(r, tile0, m, c, gain):
                act.wait_ge(evacuated, (m + (tile0 + 1)).v)
                squares(r, m, c)
                if gain is not None:
                    g = vec[:, gain + m.start:gain + m.start + 1] if m.i is None else vec[:, bass.ds((m + gain).v, 1)]
                    act.activation(tile_of(xin_hi, m), tile_of(x, m), ACT.Copy, scale=g).then_inc(xin_hi_ok, 1)

            def token_scale(r):
                act.wait_ge(mean_ready, r + 1)
                step(act.activation(halves(lnb[:]), pair[:, :, 0:HALF], ACT.Ln, bias=eps[:]))
                act.activation(rstd[:], lnb[:], ACT.Exp, scale=-0.5).then_inc(rstd_ready, 1)

            def take_batch(b, dst, src):
                act.wait_ge(tp_full, b + 1)
                act.activation(dst, src, ACT.Copy).then_inc(tp_taken, 1)

            def pool(q):
                u, tb, r = UNIT[f"pool{q}"], TP[f"pool{q}"], 6 * q + 1
                if q:
                    token_scale(6)
                for b in range(2):
                    take_batch(tb + b, hist_s[:, 4 * b:4 * b + 4, :, 0:HIST_P],
                               bank[b % 2][:, 0:480].rearrange("p (k b j) -> p k b j", k=4, b=DEC))
                if q:
                    act.wait_ge(stored, 16 * STORED["attn"])
                for b in range(2):
                    take_batch(tb + 2 + b, stage[0:TAIL_P, 512 * b:512 * b + 512], bank[b % 2][0:TAIL_P, :])
                for g in range(5):
                    for m in {2: (0, 1), 3: (2, 3), 4: (4, 5, 6, 7)}.get(g, ()):
                        if m % 4 == 3:
                            split(At(u + 2 + m // 4))
                        updated(r, TILE[f"pool{q}"], At(m), m, V_FFN + 8 * (3 * q))
                    if g < 4:
                        act.wait_ge(diff_ready, 4 * q + g + 1)
                        act.activation(mix_hi[:, 2 * g:2 * g + 2, :], diff[:, g], ACT.Copy).then_inc(mix_hi_ok, 1)

            def ffn(layer):
                u, m0, r = UNIT[f"ffn{layer}"], TILE[f"ffn{layer}"], 2 * layer + 1
                token_scale(r)
                if layer == 2:
                    act.wait_ge(stored, 16 * STORED["attn"])
                with act.Fori(0, FT // 2) as i:
                    for c in range(2):
                        n, m, f = At(u + 2 * c, 4, i), At(m0 + 2 * c, 4, i), At(c, 2, i)
                        split(n + 2)
                        act.wait_ge(evacuated, (m + 1).v)
                        act.activation(sg_buf[:, c, :], g_buf[:, c, :], ACT.Silu).then_inc(sg_ready, 1)
                        split(n + 3)
                        act.wait_ge(h_ready, (f + (FT * layer + 1)).v)
                        act.activation(tile_of(h_hi, f), h_buf[:, c, :], ACT.Copy).then_inc(h_hi_ok, 1)
                gain = {0: V_MIX + 8, 1: V_MIX + 16, 2: None, 3: None}[layer]

                def down(i):
                    for c in range(4):
                        n, m = at(u + 2 * FT + 3 * c, 12, i), at(c, 4, i)
                        split(n + 2, 768)
                        for j in (3, 4):
                            if n.i is not None or n.start + j < UNITS:
                                split(n + j)
                        if layer < 3:
                            updated(r + 1, m0 + 2 * FT, m, c, gain)
                        else:
                            for t in (c - 1, c)[c == 0:1 + (c == 3)]:
                                col = m.start - c + t
                                tb = TP["end"] + 2 * col
                                take_batch(tb, y_sb[:, col, 0:SEQ], bank6[:, :])
                                take_batch(tb + 1, y_sb[0:DEC, col, SEQ:SEQ + P], bank7[0:DEC, 0:P])
                if layer < 3:
                    with act.Fori(0, 2) as i:
                        down(i)
                else:
                    for i in range(2):
                        down(i)

            def conv_mixer():
                u, m0 = UNIT["conv_in"], TILE["conv_in"]
                token_scale(2)

                def tap(w, i):
                    return vec[:, V_DW + w * KT + i:V_DW + w * KT + i + 1]

                def products(f0, f1):
                    for f in range(f0, min(f1, TAPS * len(POOL_TILES))):
                        t, w = divmod(f, TAPS)
                        i = POOL_TILES[t]
                        if w == 0:
                            act.wait_ge(glu_ready, i + 1)
                            act.activation(conv[:, i, 0:SEQ], glu[:, i, 0:SEQ], ACT.Identity, scale=tap(0, i),
                                           bias=vec[:, V_DWB + i:V_DWB + i + 1]).then_inc(prod_ready, 1)
                        else:
                            p = (TAPS - 1) * t + w - 1
                            if p >= 3:
                                act.wait_ge(prod_added, p - 2)
                            act.activation(prod_p[:, p % 3, :], glu[:, i, w:w + SEQ], ACT.Copy, scale=tap(w, i)).then_inc(prod_ready, 1)

                for i in range(KT):
                    n = At(u + 2 * i)
                    split(n + 2)
                    if i:
                        products(8 * i - 4, 8 * i)
                    split(n + 3)
                    act.wait_ge(evacuated, m0 + 2 * i + 2)
                    if i >= 2:
                        act.wait_ge(glu_ready, i - 1)
                    act.activation(gate_s[:, i % 2, :], act_in[:, 1, :], ACT.Sigmoid,
                                   bias=vec[:, V_BIN + KT + i:V_BIN + KT + i + 1]).then_inc(gate_ready, 1)
                    if i == 1:
                        for b in range(4):
                            take_batch(TP["conv"] + b, hist_c[:, 2 * b:2 * b + 2, :, 0:HIST_C],
                                       bank[b % 2][:, 0:480].rearrange("p (k b j) -> p k b j", k=2, b=DEC))
                    products(8 * i, 8 * i + 4)
                act.wait_ge(stored, 16 * STORED["pool0"])
                for b in range(2):
                    take_batch(TP["conv"] + 4 + b, stage[0:TAIL_C, 512 * b:512 * b + 512], bank[b % 2][0:TAIL_C, :])
                def take_sum(k, used):
                    act.wait_ge(diag_used, used)
                    act.activation(conv[:, k, 0:SEQ], acc[:, 2 + (k == PE_TILE), :], ACT.Identity,
                                   bias=vec[:, V_DWB + k:V_DWB + k + 1]).then_inc(conv_pe_ready, 1)

                done = 8 * KT - 4
                for f, (i, w, last_tap) in enumerate(PE_TAPS):
                    if f >= 4:
                        act.wait_ge(diag_used, f - 3)
                    act.activation(diag[:, f % 4, :], ident, ACT.Copy, scale=tap(w, i)).then_inc(diag_ready, 1)
                    if f == SHARED_TAPS + 3:
                        take_sum(DVE_TILES[-1], SHARED_TAPS)
                    if f % 3 != 2:
                        products(done, done + 1)
                        done += 1
                last = TAPS * len(POOL_TILES)
                products(done, last - 2)
                take_sum(PE_TILE, len(PE_TAPS))
                products(last - 2, last)
                for k in range(KT):
                    act.wait_ge(cent, k + 1)
                    act.activation(glu[:, k, 0:T], conv[:, k, :], ACT.Square).then_inc(csq, 1)
                act.wait_ge(cvar, 1)
                step(act.activation(halves(lnb[:]), acc[:, 0:2, 0:HALF], ACT.Ln, bias=eps[:]))
                act.activation(sq[:, 0, :], lnb[:], ACT.Exp, scale=-0.5).then_inc(crstd, 1)
                for k in range(KT):
                    act.wait_ge(cnorm, k + 1)
                    act.activation(conv[:, k, :], glu[:, k, 0:T], ACT.Silu, scale=vec[:, V_LNG + k:V_LNG + k + 1],
                                   bias=vec[:, V_LNB + k:V_LNB + k + 1]).then_inc(cact, 1)
                    act.wait_ge(cact, k + 1)
                    act.activation(mix_hi[:, k, :], conv[:, k, :], ACT.Copy).then_inc(mix_hi_ok, 1)
                for i in range(KT):
                    split(At(UNIT["conv_out"] + i + 2))
                    updated(3, TILE["conv_out"], At(i), i, V_FFN + 8)

            def attention():
                u, m0 = UNIT["qkv"], TILE["qkv"]
                token_scale(4)

                def norm(i, dst):
                    act.wait_ge(nrm_ready, i + 1)
                    act.activation(halves(dst[:]), pair[:, :, 0:HALF], ACT.Ln, bias=eps[:]).then_inc(nrm_ln, 1)
                    act.wait_ge(nrm_ln, i + 1)
                    act.activation(dst[:], dst[:], ACT.Exp, scale=-0.5).then_inc(nrm_exp, 1)

                def square(i, src, m):
                    act.wait_ge(evacuated, m + 1)
                    if i:
                        act.wait_ge(nrm_ready, i)
                    act.activation(sq[:, 0, :], src[:], ACT.Square).then_inc(nsq_ready, 1)

                def exps(g, piece):
                    act.wait_ge(max_ready, 3 * g + piece + 1)
                    for off, i in PIECES[piece]:
                        for c in range(2):
                            w, j = (i + 1) * P, i % 2
                            ins = act.activation(s_buf[:, c, off:off + w], s_buf[:, c, off:off + w], ACT.Exp,
                                                 bias=row_max[:, c, j:j + 1], scale=SCALE, accum_out=row_sum[:, c, j:j + 1])
                    ins.then_inc(exp_done, 1)

                def take_weights(g, piece):
                    act.wait_ge(at_ready, 3 * g + piece + 1)
                    if g or piece:
                        act.wait_ge(pv_done, 3 * g + piece)
                    w = (384, 384, 512)[piece]
                    act.activation(aT[:, 0:w], bank6[:, 0:w], ACT.Copy).then_inc(at_taken, 1)

                for h in range(HEADS + 2):
                    n = At(u + 3 * h)
                    g = h - 1
                    if h < HEADS:
                        split(n + 2)
                    if 1 <= h <= HEADS:
                        act.wait_ge(t_ready, g + 1)
                        if g >= 2:
                            act.wait_ge(rows_stored[g % 2], 32 * (g // 2))
                        for j, to in enumerate((k_tok, v_tok)):
                            act.activation(to[:, g % 2], pair[:, j, :].rearrange("p (b c) -> p b c", b=4), ACT.Copy).then_inc(t_taken, 1)
                    if h < HEADS:
                        square(2 * h, q_raw, m0 + 3 * h)
                    if h >= 2:
                        take_weights(h - 2, 2)
                    if 1 <= h <= HEADS:
                        exps(g, 0)
                    if h < HEADS:
                        split(n + 3)
                        norm(2 * h, ln_q)
                        square(2 * h + 1, k_raw, m0 + 3 * h + 1)
                    if h >= 2:
                        act.wait_ge(o_taken, h - 1)
                        if h > 2:
                            act.wait_ge(oss_done, h - 2)
                        act.activation(o_sq[:].rearrange("p (b c) -> p b c", b=4), o_tok[:, :, h - 2, :], ACT.Square).then_inc(osq_done, 1)
                    if 1 <= h <= HEADS:
                        take_weights(g, 0)
                        exps(g, 1)
                    if h < HEADS:
                        split(n + 4)
                        norm(2 * h + 1, ln_k)
                    if 1 <= h <= HEADS:
                        take_weights(g, 1)
                        exps(g, 2)

                act.wait_ge(rows_s_full, 1)
                for j in range(2):
                    act.wait_ge(rows_stored[j], 16 * HEADS)
                act.activation(ks_rows_sb[:], bank7[0:R, 0:P], ACT.Copy).then_inc(rows_s_taken, 1)
                act.activation(vs_rows_sb[:], bank7[0:R, P:2 * P], ACT.Copy).then_inc(rows_s_taken, 1)
                act.wait_ge(roots_in, 1)
                act.activation(o_tmp[:, 0:2, :], o_tmp[:, 0:2, :], ACT.Sqrt).then_inc(roots_ok, 1)
                for h in range(HEADS):
                    act.wait_ge(o_back, h + 1)
                    act.activation(mix_hi[:, h, 0:SEQ], bank6[:, :], ACT.Copy, scale=sub_gain[:]).then_inc(mix_hi_ok, 1)
                act.wait_ge(dec_max_ok, 1)
                for c in range(2):
                    ins = act.activation(s_dec[:, c, :], s_dec[:, c, :], ACT.Exp, bias=m_dec[:, 2 + c:3 + c], scale=SCALE,
                                         accum_out=m_dec[:, 4 + c:5 + c])
                ins.then_inc(dec_exp_ok, 1)
                act.wait_ge(a_dec_full, 1)
                act.activation(aT_dec[:].rearrange("p j r -> p (j r)"), bank6[:, 0:2 * R], ACT.Copy).then_inc(aT_dec_ok, 1)
                act.wait_ge(vpage_used, DEC)
                act.activation(os_rows[:, 0:512], pair[0:DEC, 0, :], ACT.Copy).then_inc(os_rows_ok, 1)
                act.wait_ge(os_in_ok, 1)
                act.activation(os_sq[:], os_tok[:], ACT.Square, accum_out=m_dec[:, 8:9]).then_inc(os_sq_ok, 1)
                act.wait_ge(roots_in, 2)
                act.activation(m_dec[:, 9:11], m_dec[:, 9:11], ACT.Sqrt).then_inc(roots_ok, 1)
                act.wait_ge(os_back, 1)
                act.activation(mix_hi[:, :, SEQ:T], bank7[:, 0:R].rearrange("p (h b) -> p h b", h=HEADS), ACT.Copy,
                               scale=sub_gain[:]).then_inc(mix_hi_ok, 1)
                for i in range(KT):
                    split(At(UNIT["w_o"] + i + 2))
                    updated(5, TILE["w_o"], At(i), i, V_FFN + 16)

            take_batch(0, x[:, :, SEQ:T], bank6[:, 0:KT * DEC].rearrange("p (k b) -> p k b", k=KT))
            act.wait_ge(tp_taken, 1)
            for k in range(KT):
                take_batch(1 + k, x[:, k, 0:SEQ], bank[(1 + k) % 2][:, :])
                act.wait_ge(tp_taken, 2 + k)
                squares(0, At(k), k)
            token_scale(0)
            for t, n in enumerate((P, P, 123)):
                take_batch(9 + t, vec[:, t * P:t * P + n], bank[(9 + t) % 2][:, 0:n])
            act.wait_ge(lam_sums, 2)
            act.activation(lam_tmp[:, QK:QK + 2], lam_tmp[:, QK:QK + 2], ACT.Exp).then_inc(lam_exps, 1)
            split(At(0))
            split(At(1))
            pool(0)
            ffn(0)
            conv_mixer()
            ffn(1)
            attention()
            ffn(2)
            pool(1)
            ffn(3)

        @block.vector
        def _(dve):
            seq = [0]

            def step(ins):
                seq[0] += 1
                ins.then_inc(dve_seq, 1)
                dve.wait_ge(dve_seq, seq[0])

            def split(n, cols=1024):
                dve.wait_ge(split_hi, (n + 1).v)
                if n.start >= 2:
                    dve.wait_ge(units_done, (n + -1).v)
                dve.tensor_tensor(w_lo[n.slot(2)][:, 0:cols], raw[:, n.slot(4), 0:cols],
                                  w_hi[n.slot(2)][:, 0:cols].bitcast(F32), ALU.subtract).then_inc(split_lo, 1)

            def accumulator(m):
                b = 2 * m.slot(2)
                return acc[:, b:b + 2, 0:HALF]

            def next_low(xi, m, gain):
                dve.wait_ge(xin_hi_ok, m.v + (8 * xi + 1))
                g = vec[:, gain + m.start:gain + m.start + 1] if m.i is None else vec[:, bass.ds((m + gain).v, 1)]
                dve.scalar_tensor_tensor(tile_of(xin_lo, m), tile_of(x, m), g, tile_of(xin_hi, m).bitcast(F32),
                                         ALU.mult, ALU.subtract).then_inc(xin_lo_ok, 1)

            def pool(q):
                u, m0, l = UNIT[f"pool{q}"], TILE[f"pool{q}"], 3 * q
                gain = V_MIX + 8 * l
                dve.wait_ge(rstd_ready, 6 * q + 1)
                dve.memset(hn[:, :, 0:16], 0.0).then_inc(pads_ready, 1)
                dve.memset(wsum[:, :, :, 0:16], 0.0).then_inc(pads_ready, 1)
                for k in (4, 5, 6, 7, 0, 1, 2, 3):
                    dve.scalar_tensor_tensor(hn[:, k, 16:16 + T], x[:, k, :], vec[:, gain + k:gain + k + 1], rstd[:],
                                             ALU.mult, ALU.mult).then_inc(hn_ready, 1)
                dve.wait_ge(pads_ready, 3 * q + 2)
                dve.wait_ge(hn_ready, 8 * q + KT)
                dve.wait_ge(tp_taken, TP[f"pool{q}"] + 2)
                step(dve.tensor_copy(hist_s[:, :, :, HIST_P], hn[:, :, 16 + SEQ:16 + T]))
                for g, win in enumerate(WINDOWS):
                    here = slice(2 * g, 2 * g + 2)
                    last = dve.tensor_reduce(last_s[:, here, :], hist_s[:, here, :, 16 - win:16], AX.X, ALU.add)
                step(last)
                for g, win in enumerate(WINDOWS):
                    here = slice(2 * g, 2 * g + 2)
                    dve.scalar_tensor_tensor(diff[:, g, :, SEQ:T], last_s[:, here, :], 1.0 / win, hn[:, here, 16 + SEQ:16 + T],
                                             ALU.mult, ALU.subtract)

                def difference(g):
                    win = WINDOWS[g]
                    here = slice(2 * g, 2 * g + 2)
                    if g < 2:
                        cur = hn[:, here, :]
                        for lev in range(g + 1):
                            to = wsum[:, (g + lev) % 2]
                            if lev:
                                dve.wait_ge(diff_ready, 4 * q + 1)
                            step(dve.tensor_tensor(to[:, :, 16:16 + SEQ], cur[:, :, 16:16 + SEQ],
                                                   cur[:, :, 16 - (1 << lev):16 + SEQ - (1 << lev)], ALU.add))
                            cur = to
                    else:
                        dve.wait_ge(pool_sums, 2 * q + g - 1)
                        cur = wsum_p[:, 2 * g - 4]
                    inv = const[:, C_CNT + 16 * g:C_CNT + 16 * g + 16].unsqueeze(1).to_broadcast([P, 2, 16])
                    step(dve.tensor_tensor(edge[:, g], cur[:, :, 16:32], inv, ALU.mult))
                    dve.tensor_tensor(diff[:, g, :, 0:16], edge[:, g], hn[:, here, 16:32], ALU.subtract)
                    dve.scalar_tensor_tensor(diff[:, g, :, 16:SEQ], cur[:, :, 32:16 + SEQ], 1.0 / win,
                                             hn[:, here, 32:16 + SEQ], ALU.mult, ALU.subtract).then_inc(diff_ready, 1)

                def low(g):
                    dve.wait_ge(mix_hi_ok, MIX[f"pool{q}"] + g + 1)
                    dve.wait_ge(diff_ready, 4 * q + g + 1)
                    dve.tensor_tensor(mix_lo[:, 2 * g:2 * g + 2, :], diff[:, g], mix_hi[:, 2 * g:2 * g + 2, :].bitcast(F32),
                                      ALU.subtract).then_inc(mix_lo_ok, 1)

                def update(m):
                    if m % 4 == 3:
                        dve.wait_ge(units_done, u + m // 4 + 1)
                    else:
                        dve.wait_ge(tile_done, 6 * q + 3 * (m // 4) + m % 4 + 1)
                    s = V_PSCALE + 8 * q + m
                    dve.scalar_tensor_tensor(halves(x[:, m, :]), accumulator(At(m0 + m)), vec[:, s:s + 1], halves(x[:, m, :]),
                                             ALU.mult, ALU.add).then_inc(evacuated, 1)
                    if m % 4 == 3:
                        split(At(u + 2 + m // 4))

                def update_two(g):
                    for m in (2 * g, 2 * g + 1):
                        update(m)

                def low_two(g):
                    for m in (2 * g, 2 * g + 1):
                        next_low(XIN[6 * q + 1], At(m), V_FFN + 8 * l)

                difference(0)
                difference(1)
                if q == 0:
                    split(At(0))
                    split(At(1))
                low(0)
                low(1)
                update_two(0)
                difference(2)
                low_two(0)
                low(2)
                update_two(1)
                difference(3)
                low_two(1)
                low(3)
                for g in (2, 3):
                    update_two(g)
                    low_two(g)

            def ffn(layer):
                u, m0, r = UNIT[f"ffn{layer}"], TILE[f"ffn{layer}"], 2 * layer + 1
                dve.wait_ge(rstd_ready, r + 1)
                if layer == 2:
                    dve.wait_ge(stored, 16 * STORED["attn"])
                with dve.Fori(0, FT // 2) as i:
                    for c in range(2):
                        n, m, f = At(u + 2 * c, 4, i), At(m0 + 2 * c, 4, i), At(c, 2, i)
                        dve.wait_ge(units_done, (n + 1).v)
                        dve.tensor_tensor(halves(g_buf[:, c, :]), accumulator(m), halves(rstd[:]), ALU.mult).then_inc(evacuated, 1)
                        split(n + 2)
                        dve.wait_ge(units_done, (n + 2).v)
                        dve.tensor_tensor(halves(u_buf[:]), accumulator(m + 1), halves(rstd[:]), ALU.mult).then_inc(evacuated, 1)
                        dve.wait_ge(sg_ready, (f + (FT * layer + 1)).v)
                        dve.wait_ge(evacuated, (m + 2).v)
                        dve.tensor_tensor(h_buf[:, c, :], u_buf[:], sg_buf[:, c, :], ALU.mult).then_inc(h_ready, 1)
                        split(n + 3)
                        dve.wait_ge(h_hi_ok, (f + (FT * layer + 1)).v)
                        dve.tensor_tensor(tile_of(h_lo, f), h_buf[:, c, :], tile_of(h_hi, f).bitcast(F32), ALU.subtract)\
                           .then_inc(h_lo_ok, 1)
                gain = {0: V_MIX + 8, 1: V_MIX + 16, 2: None, 3: None}[layer]

                def down(i):
                    for c in range(4):
                        n, m = at(u + 2 * FT + 3 * c, 12, i), at(c, 4, i)
                        split(n + 2, 768)
                        if n.i is not None or n.start + 3 < UNITS:
                            split(n + 3)
                        dve.wait_ge(units_done, (n + 3).v)
                        out = tile_of(x, m) if layer < 3 else x_out[:, c, :]
                        dve.tensor_tensor(halves(out), accumulator(At(c)), halves(tile_of(x, m)), ALU.add)\
                           .then_inc(evacuated, 1)
                        if n.i is not None or n.start + 4 < UNITS:
                            split(n + 4)
                        if gain is not None:
                            next_low(XIN[r + 1], m, gain)
                if layer < 3:
                    with dve.Fori(0, 2) as i:
                        down(i)
                else:
                    for i in range(2):
                        down(i)

            def conv_mixer():
                u, m0 = UNIT["conv_in"], TILE["conv_in"]
                dve.wait_ge(rstd_ready, 3)
                step(dve.memset(glu[:, :, 0:HIST_C], 0.0))

                def taps(f0, f1):
                    for f in range(f0, f1):
                        t, w = divmod(f, TAPS)
                        i = DVE_TILES[t]
                        tap = vec[:, V_DW + w * KT + i:V_DW + w * KT + i + 1]
                        out = conv[:, i, 0:SEQ]
                        if i == DVE_TILES[-1] and w < SHARED_TAPS:
                            continue
                        if i == DVE_TILES[-1] and w == SHARED_TAPS:
                            dve.wait_ge(conv_pe_ready, 1)
                        if w == 0:
                            ins = dve.tensor_scalar(out, glu[:, i, 0:SEQ], tap, vec[:, V_DWB + i:V_DWB + i + 1], ALU.mult, ALU.add)
                        else:
                            ins = dve.scalar_tensor_tensor(out, glu[:, i, w:w + SEQ], tap, out, ALU.mult, ALU.add)
                        if w < TAPS - 1:
                            step(ins)
                        else:
                            ins.then_inc(conv_dve_ready, 1)

                def samples(half):
                    k = slice(4 * half, 4 * half + 4)
                    step(dve.tensor_copy(hist_c[:, k, :, HIST_C], glu[:, k, HIST_C + SEQ:HIST_C + T]))
                    w = vec[:, V_DW:V_DW + TAPS * KT].rearrange("p (w k) -> p k w", k=KT)[:, k].unsqueeze(2)\
                        .to_broadcast([P, KT // 2, DEC, TAPS])
                    step(dve.tensor_tensor(prod_s[:], hist_c[:, k], w, ALU.mult))
                    step(dve.tensor_reduce(conv[:, k, SEQ:T], prod_s[:], AX.X, ALU.add))
                    b = vec[:, V_DWB + 4 * half:V_DWB + 4 * half + 4].unsqueeze(2).to_broadcast([P, KT // 2, DEC])
                    dve.tensor_tensor(conv[:, k, SEQ:T], conv[:, k, SEQ:T], b, ALU.add).then_inc(conv_s_ready, 1)

                for i in range(KT):
                    n = At(u + 2 * i)
                    dve.wait_ge(units_done, (n + 1).v)
                    if i:
                        dve.wait_ge(glu_ready, i)
                    dve.tensor_tensor(halves(act_in[:, 0, :]), accumulator(At(0)), halves(rstd[:]), ALU.mult).then_inc(evacuated, 1)
                    split(n + 2)
                    if i >= 2:
                        taps(10 * i - 15, 10 * i - 10)
                    dve.wait_ge(units_done, (n + 2).v)
                    dve.tensor_tensor(halves(act_in[:, 1, :]), accumulator(At(1)), halves(rstd[:]), ALU.mult).then_inc(evacuated, 1)
                    split(n + 3)
                    dve.wait_ge(gate_ready, i + 1)
                    dve.wait_ge(evacuated, m0 + 2 * i + 1)
                    dve.scalar_tensor_tensor(glu[:, i, HIST_C:HIST_C + T], act_in[:, 0, :], vec[:, V_BIN + i:V_BIN + i + 1],
                                             gate_s[:, i % 2, :], ALU.add, ALU.mult).then_inc(glu_ready, 1)
                    if i >= 1:
                        if i == 1 or 10 * i - 10 == TAPS:
                            dve.wait_ge(glu_ready, i + 1)
                        taps(10 * i - 10, 10 * i - 5)
                    if i == 3:
                        dve.wait_ge(tp_taken, TP["conv"] + 4)
                        dve.wait_ge(glu_ready, 4)
                        samples(0)
                dve.wait_ge(glu_ready, KT)
                samples(1)
                taps(10 * KT - 15, TAPS * len(DVE_TILES))
                dve.wait_ge(cmean, 1)
                for k in range(KT):
                    dve.tensor_tensor(halves(conv[:, k, :]), halves(conv[:, k, :]), pair[:, :, 0:HALF], ALU.subtract).then_inc(cent, 1)
                dve.wait_ge(crstd, 1)
                for j in range(KT + 2):
                    if j < KT:
                        dve.tensor_tensor(glu[:, j, 0:T], conv[:, j, :], sq[:, 0, :], ALU.mult).then_inc(cnorm, 1)
                    if j >= 2:
                        k = j - 2
                        dve.wait_ge(mix_hi_ok, MIX["conv"] + k + 1)
                        dve.tensor_tensor(mix_lo[:, k, :], conv[:, k, :], mix_hi[:, k, :].bitcast(F32), ALU.subtract).then_inc(mix_lo_ok, 1)
                u = UNIT["conv_out"]
                for i in range(KT):
                    dve.wait_ge(units_done, u + i + 1)
                    dve.scalar_tensor_tensor(halves(x[:, i, :]), accumulator(At(i)), vec[:, V_BOUT + i:V_BOUT + i + 1],
                                             halves(x[:, i, :]), ALU.add, ALU.add).then_inc(evacuated, 1)
                    split(At(u + i + 2))
                    next_low(XIN[3], At(i), V_FFN + 8)

            def attention():
                u, m0 = UNIT["qkv"], TILE["qkv"]
                dve.wait_ge(rstd_ready, 5)

                def project(h, j, dst):
                    n = At(u + 3 * h + j)
                    dve.wait_ge(units_done, (n + 1).v)
                    if h:
                        if j < 2:
                            dve.wait_ge(qkn_ready, 2 * h)
                        else:
                            dve.wait_ge(t_ready, h)
                            dve.wait_ge(saved_s, 3 * h)
                    dve.tensor_tensor(halves(dst[:]), accumulator(At(m0 + 3 * h + j)), halves(rstd[:]), ALU.mult).then_inc(evacuated, 1)
                    split(n + 2)

                def maxima(g, piece):
                    dve.wait_ge(qk_ready, 3 * g + piece + 1)
                    dve.wait_ge(bias_ready, g + 1)
                    if g or piece:
                        dve.wait_ge(a_ready, 3 * g + piece)
                    for off, i in PIECES[piece]:
                        for c in range(2):
                            w, j = (i + 1) * P, i % 2
                            last = dve.tensor_tensor_reduce(
                                out=s_buf[:, c, off:off + w], in0=pair[:, c, off:off + w], in1=bias_h[:, g % 2, SEQ - w:SEQ],
                                scale=1.0, scalar=-3e38, op0=ALU.add, op1=ALU.max, accum_out=row_scl[:, c, j:j + 1])
                    last.then_inc(s_taken, 1)
                    dve.wait_ge(s_taken, 3 * g + piece + 1)
                    dve.tensor_scalar(row_max[:], row_scl[:], -SCALE, None, ALU.mult).then_inc(max_ready, 1)

                def weights(g, piece):
                    dve.wait_ge(exp_done, 3 * g + piece + 1)
                    step(dve.reciprocal(row_inv[:], row_sum[:]))
                    step(dve.tensor_scalar(row_inv[:, 1, :], row_inv[:, 1, :], neg_lam[:], None, ALU.mult))
                    if g or piece:
                        dve.wait_ge(at_ready, 3 * g + piece)
                    for off, i in PIECES[piece]:
                        w, j = (i + 1) * P, i % 2
                        dve.tensor_scalar(t_buf[:, off:off + w], s_buf[:, 1, off:off + w], row_inv[:, 1, j:j + 1], None, ALU.mult)\
                           .then_inc(dve_seq, 1)
                        seq[0] += 1
                    for off, i in PIECES[piece]:
                        w, j = (i + 1) * P, i % 2
                        dve.wait_ge(dve_seq, seq[0])
                        last = dve.scalar_tensor_tensor(a_buf[:, off:off + w], s_buf[:, 0, off:off + w], row_inv[:, 0, j:j + 1],
                                                        t_buf[:, off:off + w], ALU.mult, ALU.add)
                    last.then_inc(a_ready, 1)

                def take_output(g):
                    dve.wait_ge(pv_done, 3 * g + 3)
                    rows = bank7[:, :].rearrange("p (b c) -> p b c", b=4)
                    step(dve.tensor_reduce(o_max[:, :, g], rows, AX.X, ALU.max, apply_absolute_value=True))
                    step(dve.tensor_scalar(o_max[:, :, g], o_max[:, :, g], 1e-15, 1e37, ALU.max, ALU.min))
                    step(dve.reciprocal(o_inv[:, :, g], o_max[:, :, g]))
                    dve.tensor_tensor(o_tok[:, :, g, :], rows, o_inv[:, :, g:g + 1].to_broadcast([P, 4, P]), ALU.mult)\
                       .then_inc(o_taken, 1)
                    dve.wait_ge(osq_done, g + 1)
                    dve.tensor_reduce(o_ss[:, :, g], o_sq[:].rearrange("p (b c) -> p b c", b=4), AX.X, ALU.add)\
                       .then_inc(oss_done, 1)

                for h in range(HEADS + 2):
                    if h < HEADS:
                        project(h, 0, q_raw)
                    if 1 <= h <= HEADS:
                        maxima(h - 1, 0)
                        weights(h - 1, 0)
                    if h < HEADS:
                        project(h, 1, k_raw)
                    if h >= 2:
                        take_output(h - 2)
                    if 1 <= h <= HEADS:
                        maxima(h - 1, 1)
                        weights(h - 1, 1)
                    if h < HEADS:
                        project(h, 2, v_raw)
                    if 1 <= h <= HEADS:
                        maxima(h - 1, 2)
                    if h < HEADS:
                        for j, (src, ln, gain, dst) in enumerate(((q_raw, ln_q, V_QN, qn), (k_raw, ln_k, V_KN, kn))):
                            dve.wait_ge(nrm_exp, 2 * h + j + 1)
                            if h:
                                dve.wait_ge(saved_s, 3 * h)
                            dve.scalar_tensor_tensor(dst[:], src[:], vec[:, gain:gain + 1], ln[:], ALU.mult, ALU.mult)\
                               .then_inc(qkn_ready, 1)
                    if 1 <= h <= HEADS:
                        weights(h - 1, 2)

                def radicands(mean_out, sum_out, ss, inv):
                    step(dve.tensor_tensor(mean_out, inv, inv, ALU.mult))
                    step(dve.tensor_scalar(mean_out, mean_out, EPS, None, ALU.mult))
                    step(dve.scalar_tensor_tensor(mean_out, ss, 1.0 / P, mean_out, ALU.mult, ALU.add))
                    step(dve.tensor_copy(sum_out, ss))

                def factors(out, mean_root, sum_root, largest):
                    step(dve.scalar_tensor_tensor(sum_root, largest, 2.0 ** -64, sum_root, ALU.mult, ALU.mult))
                    step(dve.tensor_scalar(sum_root, sum_root, 1.0, None, ALU.is_lt))
                    step(dve.reciprocal(out, mean_root))
                    step(dve.tensor_tensor(out, out, sum_root, ALU.mult))

                flat = "p b h -> p (b h)"
                dve.wait_ge(oss_done, HEADS)
                radicands(o_tmp[:, 0, :], o_tmp[:, 1, :], o_ss[:].rearrange(flat), o_inv[:].rearrange(flat))
                dve.memset(row_inv[:, 0, 0:1], 0.0).then_inc(roots_in, 1)
                dve.wait_ge(saved_s, 3 * HEADS)
                dve.tensor_tensor(new_dec[:], qs[:].rearrange("p h b -> p (h b)"), ks[:].rearrange("p h b -> p (h b)"), ALU.mult)\
                   .then_inc(new_prod_ok, 1)

                def head_low(h):
                    dve.wait_ge(mix_hi_ok, MIX["attn"] + 1 + h)
                    dve.scalar_tensor_tensor(mix_lo[:, h, 0:SEQ], bank6[:, :], sub_gain[:], mix_hi[:, h, 0:SEQ].bitcast(F32),
                                             ALU.mult, ALU.subtract).then_inc(mix_lo_ok, 1)

                def key_scores(f):
                    b, j = divmod(f, 2)
                    dve.wait_ge(k_folded, f + 1)
                    dve.tensor_reduce(s_cols[:].rearrange("p j (h b) c -> p j h b c", b=DEC)[:, j, :, b, :],
                                      k_prod[:, j, :].rearrange("p (h c d) -> p h c d", c=2, d=QK)[:, :, :, 0:QK // 2],
                                      AX.X, ALU.add).then_inc(s_cols_ok, 1)

                for b in range(DEC):
                    dve.wait_ge(q_all_ready, b + 1)
                    dve.wait_ge(kpage_in[b % 3], 32 * (b // 3 + 1))
                    for j in range(2):
                        f = 2 * b + j
                        if f >= 2:
                            dve.wait_ge(s_cols_ok, f - 1)
                        dve.tensor_tensor(k_prod[:, j, :].rearrange("p (t c) -> p t c", t=2),
                                          k_page[b % 3][:, j, :].rearrange("p (t c) -> p t c", t=2),
                                          acc[:, 2 * (b % 2):2 * (b % 2) + 2, :], ALU.mult).then_inc(k_prod_ok, 1)
                        if f == 0:
                            dve.wait_ge(roots_ok, 1)
                            factors(o_tmp[:, 2, :], o_tmp[:, 0, :], o_tmp[:, 1, :], o_max[:].rearrange(flat))
                            dve.memset(row_inv[:, 0, 0:1], 0.0).then_inc(factors_ok, 1)
                        else:
                            key_scores(f - 1)
                    if b >= 2:
                        head_low(b - 2)
                key_scores(2 * DEC - 1)
                head_low(HEADS - 2)
                head_low(HEADS - 1)
                dve.wait_ge(s_rows_full, 1)
                dve.tensor_tensor(s_dec[:, :, 0:PAST], pair[0:R, 0, :].rearrange("p (c k) -> p c k", c=2),
                                  const[0:R, C_POS:C_POS + PAST].unsqueeze(1).to_broadcast([R, 2, PAST]), ALU.add)
                step(dve.tensor_scalar(s_dec[:, :, PAST], pair[0:R, 1, 0:2], float(QK), None, ALU.mult))
                step(dve.tensor_reduce(m_dec[:, 0:2], s_dec[:], AX.X, ALU.max))
                dve.tensor_scalar(m_dec[:, 2:4], m_dec[:, 0:2], -SCALE, None, ALU.mult).then_inc(dec_max_ok, 1)
                dve.wait_ge(dec_exp_ok, 1)
                step(dve.reciprocal(m_dec[:, 6:8], m_dec[:, 4:6]))
                step(dve.tensor_scalar(m_dec[:, 7:8], m_dec[:, 7:8], neg_lam[0:R, :], None, ALU.mult))
                step(dve.tensor_scalar(t_dec[:], s_dec[:, 1, :], m_dec[:, 7:8], None, ALU.mult))
                dve.scalar_tensor_tensor(a_dec[:], s_dec[:, 0, :], m_dec[:, 6:7], t_dec[:], ALU.mult, ALU.add).then_inc(a_dec_ok, 1)
                dve.wait_ge(a_dec_full, 1)
                step(dve.tensor_tensor(new_dec[:], bank7[:, 0:R], vs[:].rearrange("p h b -> p (h b)"), ALU.mult))
                dve.wait_ge(aT_dec_ok, 1)
                for b in range(DEC):
                    dve.wait_ge(vpage_in[b], 32)
                    a = aT_dec[:].rearrange("p j (h b) -> p (j h) b", b=DEC)[:, :, b:b + 1].to_broadcast([P, 2 * HEADS, P])
                    v = v_place[b][:].rearrange("p j (h d) -> p (j h) d", d=P)
                    dve.tensor_tensor(v, v, a, ALU.mult).then_inc(v_weighted, 1)
                dve.wait_ge(vpage_used, DEC)
                dve.tensor_copy(os_rows[:, 512:D], pair[0:DEC, 1, :]).then_inc(os_rows_ok, 1)
                dve.wait_ge(os_turned, 1)
                dve.tensor_tensor(os_col[:], pair[:, 0, 0:R], new_dec[:], ALU.add).then_inc(os_col_ok, 1)
                dve.wait_ge(os_full, 1)
                step(dve.tensor_reduce(m_dec[:, 11:12], pair[0:R, 1, 0:P], AX.X, ALU.max, apply_absolute_value=True))
                step(dve.tensor_scalar(m_dec[:, 11:12], m_dec[:, 11:12], 1e-15, 1e37, ALU.max, ALU.min))
                step(dve.reciprocal(m_dec[:, 12:13], m_dec[:, 11:12]))
                dve.tensor_scalar(os_tok[:], pair[0:R, 1, 0:P], m_dec[:, 12:13], None, ALU.mult).then_inc(os_in_ok, 1)

                dve.wait_ge(os_sq_ok, 1)
                radicands(m_dec[:, 9:10], m_dec[:, 10:11], m_dec[:, 8:9], m_dec[:, 12:13])
                dve.memset(row_inv[:, 0, 0:1], 0.0).then_inc(roots_in, 1)
                dve.wait_ge(roots_ok, 2)
                factors(m_dec[:, 13:14], m_dec[:, 9:10], m_dec[:, 10:11], m_dec[:, 11:12])
                dve.tensor_scalar(os_tok[:], os_tok[:], m_dec[:, 13:14], None, ALU.mult).then_inc(os_scaled, 1)
                dve.wait_ge(mix_hi_ok, MIX["attn"] + HEADS + 1)
                dve.scalar_tensor_tensor(mix_lo[:, :, SEQ:T], bank7[:, 0:R].rearrange("p (h b) -> p h b", h=HEADS), sub_gain[:],
                                         mix_hi[:, :, SEQ:T].bitcast(F32), ALU.mult, ALU.subtract).then_inc(mix_lo_ok, 1)
                u = UNIT["w_o"]
                for i in range(KT):
                    dve.wait_ge(units_done, u + i + 1)
                    dve.tensor_tensor(halves(x[:, i, :]), accumulator(At(i)), halves(x[:, i, :]), ALU.add).then_inc(evacuated, 1)
                    split(At(u + i + 2))
                    next_low(XIN[5], At(i), V_FFN + 16)

            dve.wait_ge(sq_ready, 1)
            dve.tensor_copy(sqacc[:], sq[:, 0, :]).then_inc(sq_added, 1)
            for m in range(1, KT):
                dve.wait_ge(sq_ready, m + 1)
                dve.wait_ge(sq_added, m)
                dve.tensor_tensor(sqacc[:], sqacc[:], sq[:, m % 2, :], ALU.add).then_inc(sq_added, 1)
            dve.wait_ge(lam_in, 64)
            for j in range(2):
                dve.tensor_tensor_reduce(out=lam_tmp[:, 0:QK], in0=lam_rows[:, 2 * j, :], in1=lam_rows[:, 2 * j + 1, :],
                                         scale=1.0, scalar=0.0, op0=ALU.mult, op1=ALU.add,
                                         accum_out=lam_tmp[:, QK + j:QK + j + 1]).then_inc(lam_sums, 1)
                dve.wait_ge(lam_sums, j + 1)
            dve.wait_ge(lam_exps, 1)
            step(dve.tensor_tensor(neg_lam[:], lam_tmp[:, QK + 1:QK + 2], lam_tmp[:, QK:QK + 1], ALU.subtract))
            step(dve.tensor_scalar(neg_lam[:], neg_lam[:], -LAMBDA_INIT, None, ALU.add))
            dve.wait_ge(tp_taken, TP["pool0"])
            step(dve.tensor_scalar(sub_gain[:], vec[:, V_SUB:V_SUB + 1], 1.0 - LAMBDA_INIT, None, ALU.mult))
            pool(0)
            ffn(0)
            conv_mixer()
            ffn(1)
            attention()
            ffn(2)
            pool(1)
            ffn(3)

        @block.gpsimd
        def _(pool_e):
            def add_squares(r):
                for m in range(KT):
                    pool_e.wait_ge(sq_ready, 8 * r + m + 1)
                    if m == 0:
                        if r:
                            pool_e.wait_ge(mean_ready, r)
                        pool_e.tensor_copy(sqacc[:], sq[:, 0, :]).then_inc(sq_added, 1)
                    else:
                        pool_e.wait_ge(sq_added, 8 * r + m)
                        pool_e.tensor_tensor(sqacc[:], sqacc[:], sq[:, m % 2, :], ALU.add).then_inc(sq_added, 1)

            seq = [0]

            def step(ins):
                seq[0] += 1
                ins.then_inc(pool_seq, 1)
                pool_e.wait_ge(pool_seq, seq[0])

            def window_sums(q):
                pool_e.memset(wsum_p[:, :, :, 0:16], 0.0).then_inc(pads_ready, 1)
                pool_e.wait_ge(pads_ready, 3 * q + 3)
                for g, places in ((2, (0, 1, 0)), (3, (1, 2, 1, 2))):
                    pool_e.wait_ge(hn_ready, 8 * q + 2 * g - 2)
                    if g == 3:
                        pool_e.wait_ge(pool_sums, 2 * q + 1)
                    cur = hn[:, 2 * g:2 * g + 2, :]
                    for lev, place in enumerate(places):
                        to = wsum_p[:, place]
                        ins = pool_e.tensor_tensor(to[:, :, 16:16 + SEQ], cur[:, :, 16:16 + SEQ],
                                                   cur[:, :, 16 - (1 << lev):16 + SEQ - (1 << lev)], ALU.add)
                        if lev < g:
                            step(ins)
                        else:
                            ins.then_inc(pool_sums, 1)
                        cur = to

            def store_stage(b, hist, states_p, states_s):
                pool_e.wait_ge(tp_taken, b)
                pool_e.dma_start(states_p, stage[0:hist, :]).then_inc(stored, 16)
                pool_e.dma_start(states_s, stage[hist:hist + DEC, :]).then_inc(stored, 16)

            pool_e.memset(avg[:], 1.0 / D).then_inc(ready0, 1)
            pool_e.memset(eps[:], EPS).then_inc(ready0, 1)
            step(pool_e.memset(one_row[:], 0.0))
            pool_e.memset(one_row[:, DEC - 1:DEC], 1.0).then_inc(ready0, 1)
            row = [0]

            def rows(src):
                n = src.shape[0]
                r = row[0]
                while n:
                    t, p0 = divmod(r, P)
                    k = min(n, P - p0)
                    pool_e.dma_start(vec_rows[p0:p0 + k, t, :], src[src.shape[0] - n:src.shape[0] - n + k, :]).then_inc(vecs_in, 16)
                    r, n = r + k, n - k
                row[0] = r
            for src in (norm_mix, norm_ffn, pool_scale, conv_b_in, conv_dw_b, conv_ln_g, conv_ln_b, conv_b_out,
                        conv_dw[0]):
                rows(src.rearrange("l (k p) -> (l k) p", p=P))
            for j, src in enumerate((attn_q_norm, attn_k_norm)):
                for c in range(2):
                    pool_e.dma_start(vec_rows[120 + j:121 + j, 2, c * QK:(c + 1) * QK], src).then_inc(vecs_in, 16)
            pool_e.dma_start(vec_rows[122:123, 2, :], attn_subln).then_inc(vecs_in, 16)
            for j, src in enumerate((attn_lq1, attn_lk1, attn_lq2, attn_lk2)):
                pool_e.dma_start(lam_rows[:, j, :], src[0].partition_broadcast(P)).then_inc(lam_in, 16)
            for q in range(2):
                window_sums(q)
                store_stage(TP[f"pool{q}"] + 4, HIST_P, pool_state_p[q, 0], pool_state_s[q, :, HIST_P - 1, :])
                add_squares(6 * q + 1)
                if q:
                    break
                add_squares(2)
                for t, i in enumerate(POOL_TILES):
                    out = conv[:, i, 0:SEQ]
                    for w in range(1, TAPS):
                        p = (TAPS - 1) * t + w - 1
                        pool_e.wait_ge(prod_ready, TAPS * t + w + 1)
                        if w > 1:
                            pool_e.wait_ge(prod_added, p)
                        pool_e.tensor_tensor(out, out, prod_p[:, p % 3, :], ALU.add).then_inc(prod_added, 1)
                store_stage(TP["conv"] + 6, HIST_C, conv_state_p[0, 0], conv_state_s[0, :, HIST_C - 1, :])
                add_squares(3)
                add_squares(4)
                k_out = k_rows_p[0, 0].rearrange("(b p) h c d -> p b h (c d)", p=P)
                v_out = v_rows_p[0, 0].rearrange("(b p) h d -> p b h d", p=P)
                pool_e.wait_ge(units_done, UNIT["qkv"])
                for h in range(HEADS + 1):
                    if h < HEADS:
                        if h >= 2:
                            pool_e.wait_ge(s_taken, 3 * (h - 1))
                        pool_e.tensor_scalar(bias_h[:, h % 2, :], const[:, C_DIST:C_DIST + SEQ], 2.0 ** -(h + 1) / SCALE, 0.0,
                                             ALU.mult, ALU.add).then_inc(bias_ready, 1)
                        pool_e.wait_ge(evacuated, TILE["qkv"] + 3 * h + 3)
                        pool_e.tensor_copy(vs[:, h, :], v_raw[:, SEQ:T]).then_inc(saved_s, 1)
                        pool_e.wait_ge(qkn_ready, 2 * h + 2)
                        pool_e.tensor_copy(qs[:, h, :], qn[:, SEQ:T]).then_inc(saved_s, 1)
                        pool_e.tensor_copy(ks[:, h, :], kn[:, SEQ:T]).then_inc(saved_s, 1)
                    if h:
                        g = h - 1
                        pool_e.wait_ge(t_taken, 2 * g + 2)
                        pool_e.dma_start(k_out[:, :, g, :], k_tok[:, g % 2]).then_inc(rows_stored[g % 2], 16)
                        pool_e.dma_start(v_out[:, :, g, :], v_tok[:, g % 2]).then_inc(rows_stored[g % 2], 16)
                pool_e.wait_ge(factors_ok, 1)
                scale = o_tmp[:, 2, :].rearrange("p (b h) -> p b h", b=4)
                for h in range(HEADS):
                    pool_e.tensor_tensor(o_tok[:, :, h, :], o_tok[:, :, h, :], scale[:, :, h:h + 1].to_broadcast([P, 4, P]), ALU.mult)\
                          .then_inc(o_scaled, 1)
                    for j in range(2):
                        pool_e.wait_ge(k_prod_ok, 2 * h + j + 1)
                        prod = k_prod[:, j, :].rearrange("p (g d) -> p g d", d=QK)
                        pool_e.tensor_tensor(prod[:, :, 0:QK // 2], prod[:, :, 0:QK // 2], prod[:, :, QK // 2:QK], ALU.add)\
                              .then_inc(k_folded, 1)
                for b in range(DEC):
                    pool_e.wait_ge(v_weighted, b + 1)
                    v = v_place[b]
                    pool_e.tensor_tensor(v[:, 0, :], v[:, 0, :], v[:, 1, :], ALU.add).then_inc(v_summed, 1)
                pool_e.wait_ge(rows_s_taken, 2)
                for h in range(HEADS):
                    pool_e.dma_start(k_rows_s[0, :, 0, h].rearrange("b c d -> b (c d)"), ks_rows_sb[h * DEC:(h + 1) * DEC, :])\
                          .then_inc(stored, 16)
                    pool_e.dma_start(v_rows_s[0, :, 0, h, :], vs_rows_sb[h * DEC:(h + 1) * DEC, :]).then_inc(stored, 16)
                add_squares(5)
                add_squares(6)
            for m in range(KT):
                tb = TP["end"] + 2 * m
                pool_e.wait_ge(tp_taken, tb + 1)
                pool_e.dma_start(y_prompt[0].rearrange("(b p) c -> p b c", p=P)[:, :, m * P:(m + 1) * P],
                                 y_sb[:, m, 0:SEQ].rearrange("p (b c) -> p b c", b=4)).then_inc(stored, 16)
                pool_e.wait_ge(tp_taken, tb + 2)
                pool_e.dma_start(y_sample[:, 0, m * P:(m + 1) * P], y_sb[0:DEC, m, SEQ:SEQ + P]).then_inc(stored, 16)


OUTPUTS = (("y_prompt", (1, SEQ, D)), ("y_sample", (DEC, 1, D)),
           ("pool_state_p", (2, 1, HIST_P, D)), ("pool_state_s", (2, DEC, HIST_P, D)),
           ("conv_state_p", (1, 1, HIST_C, D)), ("conv_state_s", (1, DEC, HIST_C, D)),
           ("k_rows_p", (1, 1, SEQ, HEADS, 2, QK)), ("v_rows_p", (1, 1, SEQ, HEADS, P)),
           ("k_rows_s", (1, DEC, 1, HEADS, 2, QK)), ("v_rows_s", (1, DEC, 1, HEADS, P)))
INPUTS = ("x_prompt", "x_sample", "state_pool", "state_conv", "cache_k", "cache_v", "page_table",
          "norm_mix", "norm_ffn", "pool_w", "pool_scale", "conv_w_in", "conv_b_in", "conv_dw", "conv_dw_b",
          "conv_ln_g", "conv_ln_b", "conv_w_out", "conv_b_out", "attn_w_qkv", "attn_q_norm", "attn_k_norm",
          "attn_lq1", "attn_lk1", "attn_lq2", "attn_lk2", "attn_subln", "attn_w_o",
          "ffn_w_gate", "ffn_w_up", "ffn_w_down")


def kernel(**inputs):
    from concourse import bacc
    from concourse.bass_utils import run_bass_kernel_spmd

    nc = bacc.Bacc("TRN2", target_bir_lowering=False, num_devices=1)
    arrays, args = {}, []
    for name in INPUTS:
        a = np.ascontiguousarray(inputs[name])
        arrays[f"in_{name}"] = a
        args.append(nc.dram_tensor(f"in_{name}", a.shape, mybir.dt.from_np(a.dtype), kind="ExternalInput").ap())
    arrays["in_shape_constants"] = constants()
    args.append(nc.dram_tensor("in_shape_constants", (P, N_CONST), F32, kind="ExternalInput").ap())
    for name, shape in OUTPUTS:
        args.append(nc.dram_tensor(f"out_{name}", shape, F32, kind="ExternalOutput").ap())
    trunk_step(nc, *args)
    r = run_bass_kernel_spmd(nc, [arrays], core_ids=[0])
    return tuple(r.results[0][f"out_{name}"] for name, _ in OUTPUTS)
```
